# Optimizing a Trainium2 kernel written in Bass

```python
import math
import jax, jax.numpy as jnp
from jax import lax
import numpy as np

D_MODEL = 1024
BATCH = 1
SEQ = 512
DEPTH = 2

N_MIXERS = 2
CHUNK = 64
A_HEADS = 8
A_DK = 128
A_DV = 128
A_CONV = 5
A_W = A_HEADS * A_DK
A_VW = A_HEADS * A_DV
A_CONV_CH = 2 * A_W + A_VW
A_IN = 2 * A_W + 2 * A_VW + 4 * A_HEADS
B_HEADS = 4
B_DK = 128
B_DV = 256
B_RANK = 16
B_TAU = 16.0
B_KW = B_HEADS * B_DK
B_VW = B_HEADS * B_DV
B_IN = 2 * B_KW + 2 * B_VW + 2 * B_RANK
D_FF = 4 * D_MODEL
DEEPNORM_ALPHA = (2 * DEPTH) ** 0.25
DEEPNORM_BETA = (8 * DEPTH) ** -0.25
LN_EPS = 1e-5
RMS_EPS = 1e-6
N_A_LAYERS = (DEPTH + 1) // 2
N_B_LAYERS = DEPTH // 2


F32 = jnp.float32

def _layernorm(x, g, b):
    xf = x.astype(F32)
    mu = jnp.mean(xf, axis=-1, keepdims=True)
    xc = xf - mu
    var = jnp.mean(xc * xc, axis=-1, keepdims=True)
    return (xc * lax.rsqrt(var + LN_EPS) * g.astype(F32) + b.astype(F32)).astype(x.dtype)

def _rmsnorm(x, g):
    return x * lax.rsqrt(jnp.mean(x * x, axis=-1, keepdims=True) + RMS_EPS) * g.astype(F32)

def _l2norm(x):
    return x * lax.rsqrt(jnp.sum(x * x, axis=-1, keepdims=True) + 1e-6)

def _flip(t):
    return jnp.flip(t, axis=2)

def _depthwise_conv(u, w):
    k = w.shape[0]
    return lax.conv_general_dilated(
        u, w[:, None, :], window_strides=(1,), padding=[(k // 2, k // 2)],
        dimension_numbers=("NWC", "WIO", "NWC"), feature_group_count=u.shape[-1])

def _gated_delta_chunked(q, k, v, beta, g):
    bn, h, s, dk = q.shape
    dv = v.shape[-1]
    n = s // CHUNK
    q = q.reshape(bn, h, n, CHUNK, dk)
    k = k.reshape(bn, h, n, CHUNK, dk)
    v = v.reshape(bn, h, n, CHUNK, dv)
    beta = beta.reshape(bn, h, n, CHUNK)
    gc = jnp.cumsum(g.reshape(bn, h, n, CHUNK), axis=-1)
    causal = jnp.tril(jnp.ones((CHUNK, CHUNK), bool))
    strict = jnp.tril(jnp.ones((CHUNK, CHUNK), bool), -1)
    decay_mat = jnp.exp(jnp.where(causal, gc[..., :, None] - gc[..., None, :], -jnp.inf))
    kb = k * beta[..., None]
    a_mat = jnp.where(strict, jnp.einsum('bhncd,bhnsd->bhncs', kb, k) * decay_mat, 0.0)
    lhs = a_mat + jnp.eye(CHUNK, dtype=F32)
    rhs = jnp.concatenate([v * beta[..., None], kb * jnp.exp(gc)[..., None]], axis=-1)
    sol = lax.linalg.triangular_solve(lhs, rhs, left_side=True, lower=True, unit_diagonal=True)
    u, w = sol[..., :dv], sol[..., dv:]
    qk = jnp.einsum('bhncd,bhnsd->bhncs', q, k) * decay_mat
    q_dec = q * jnp.exp(gc)[..., None]
    k_dec = k * jnp.exp(gc[..., -1:] - gc)[..., None]
    g_last = jnp.exp(gc[..., -1])
    xs = tuple(jnp.moveaxis(t, 2, 0) for t in (qk, q_dec, k_dec, u, w, g_last))

    def step(state, inp):
        qk_c, qd_c, kd_c, u_c, w_c, gl_c = inp
        v_new = u_c - jnp.einsum('bhcd,bhde->bhce', w_c, state)
        o = jnp.einsum('bhcd,bhde->bhce', qd_c, state) + jnp.einsum('bhcs,bhse->bhce', qk_c, v_new)
        state = state * gl_c[..., None, None] + jnp.einsum('bhcd,bhce->bhde', kd_c, v_new)
        return state, o

    s0 = jnp.zeros((bn, h, dk, dv), F32)
    _, o = lax.scan(step, s0, xs)
    return jnp.moveaxis(o, 0, 2).reshape(bn, h, s, dv)

def _gla_chunked(q, k, v, log_a):
    bn, h, s, dk = q.shape
    dv = v.shape[-1]
    n = s // CHUNK

    def to_chunks(t):
        return jnp.moveaxis(t.reshape(bn, h, n, CHUNK, t.shape[-1]), 2, 0)

    qc, kc, vc = to_chunks(q), to_chunks(k), to_chunks(v)
    bc = jnp.cumsum(to_chunks(log_a), axis=3)
    causal = jnp.tril(jnp.ones((CHUNK, CHUNK), bool))[:, :, None]

    def step(state, inp):
        q_c, k_c, v_c, b_c = inp
        dec = jnp.exp(jnp.where(causal, b_c[:, :, :, None, :] - b_c[:, :, None, :, :], -jnp.inf))
        scores = jnp.einsum('bhid,bhjd,bhijd->bhij', q_c, k_c, dec)
        o = jnp.einsum('bhid,bhde->bhie', q_c * jnp.exp(b_c), state) + jnp.einsum('bhij,bhje->bhie', scores, v_c)
        b_last = b_c[:, :, -1:, :]
        state = jnp.exp(b_last[:, :, 0, :])[..., None] * state + jnp.einsum(
            'bhjd,bhje->bhde', k_c * jnp.exp(b_last - b_c), v_c)
        return state, o

    s0 = jnp.zeros((bn, h, dk, dv), F32)
    _, o = lax.scan(step, s0, (qc, kc, vc, bc))
    return jnp.moveaxis(o, 0, 2).reshape(bn, h, s, dv)

def _mixer_gdn(h, w_in, conv_w, a_log, dt_bias, norm_g, w_out):
    bn, s, _ = h.shape
    proj = jnp.matmul(h, w_in).astype(F32)
    qkv = jax.nn.silu(_depthwise_conv(proj[..., :A_CONV_CH], conv_w.astype(F32)))
    z = proj[..., A_CONV_CH:A_CONV_CH + A_VW]
    ba = proj[..., A_CONV_CH + A_VW:].reshape(bn, s, 2, 2, A_HEADS)

    def heads(t, d):
        return t.reshape(bn, s, A_HEADS, d).transpose(0, 2, 1, 3)

    q = _l2norm(heads(qkv[..., :A_W], A_DK)) * (A_DK ** -0.5)
    k = _l2norm(heads(qkv[..., A_W:2 * A_W], A_DK))
    v = heads(qkv[..., 2 * A_W:], A_DV)
    beta = jax.nn.sigmoid(ba[:, :, 0]).transpose(2, 0, 3, 1)
    g = (-jnp.exp(a_log.astype(F32)) * jax.nn.softplus(ba[:, :, 1] + dt_bias.astype(F32))).transpose(2, 0, 3, 1)
    o_f = _gated_delta_chunked(q, k, v, beta[0], g[0])
    o_b = _flip(_gated_delta_chunked(_flip(q), _flip(k), _flip(v), _flip(beta[1]), _flip(g[1])))
    o = (o_f + o_b).transpose(0, 2, 1, 3)
    o = _rmsnorm(o, norm_g) * jax.nn.silu(z.reshape(bn, s, A_HEADS, A_DV))
    return jnp.matmul(o.reshape(bn, s, A_VW).astype(w_out.dtype), w_out)

def _mixer_gla(h, w_in, gate_w2, gate_b, norm_g, w_out):
    bn, s, _ = h.shape
    proj = jnp.matmul(h, w_in).astype(F32)

    def heads(t, d):
        return t.reshape(bn, s, B_HEADS, d).transpose(0, 2, 1, 3)

    q = heads(proj[..., :B_KW], B_DK) * (B_DK ** -0.5)
    k = heads(proj[..., B_KW:2 * B_KW], B_DK)
    v = heads(proj[..., 2 * B_KW:2 * B_KW + B_VW], B_DV)
    r = proj[..., 2 * B_KW + B_VW:2 * B_KW + 2 * B_VW]
    gl = proj[..., 2 * B_KW + 2 * B_VW:].reshape(bn, s, 2, B_RANK)
    gate_logit = jnp.einsum('bsnr,nrk->nbsk', gl, gate_w2.astype(F32)) + gate_b.astype(F32)[:, None, None, :]
    log_a = (jax.nn.log_sigmoid(gate_logit) / B_TAU).reshape(2, bn, s, B_HEADS, B_DK).transpose(0, 1, 3, 2, 4)
    o_f = _gla_chunked(q, k, v, log_a[0])
    o_b = _flip(_gla_chunked(_flip(q), _flip(k), _flip(v), _flip(log_a[1])))
    o = (o_f + o_b).transpose(0, 2, 1, 3)
    o = _rmsnorm(o, norm_g) * jax.nn.silu(r.reshape(bn, s, B_HEADS, B_DV))
    return jnp.matmul(o.reshape(bn, s, B_VW).astype(w_out.dtype), w_out)

def _sq_relu_mlp(h, w1, w2):
    a = jax.nn.relu(jnp.matmul(h, w1))
    return jnp.matmul(a * a, w2)

def first_inputs(seed: int = 0) -> dict:
    key = jax.random.key(seed)
    ks = jax.random.split(key, 20)
    nrm = jax.random.normal
    x = nrm(ks[0], (BATCH, SEQ, D_MODEL), F32)
    a_w_in = nrm(ks[1], (N_A_LAYERS, D_MODEL, A_IN), F32) * D_MODEL ** -0.5
    a_conv = nrm(ks[2], (N_A_LAYERS, A_CONV, A_CONV_CH), F32) * A_CONV ** -0.5
    a_alog = jnp.log(jax.random.uniform(ks[3], (N_A_LAYERS, 2, A_HEADS), F32, 1.0, 16.0))
    dt = jnp.exp(jax.random.uniform(ks[4], (N_A_LAYERS, 2, A_HEADS), F32, math.log(1e-3), math.log(1e-1)))
    a_dt_bias = dt + jnp.log(-jnp.expm1(-dt))
    a_norm_g = 1.0 + 0.02 * nrm(ks[5], (N_A_LAYERS, A_DV), F32)
    a_w_out = nrm(ks[6], (N_A_LAYERS, A_VW, D_MODEL), F32) * (A_VW ** -0.5 * DEEPNORM_BETA)
    b_w_in = nrm(ks[7], (N_B_LAYERS, D_MODEL, B_IN), F32) * D_MODEL ** -0.5
    b_gate_w2 = nrm(ks[8], (N_B_LAYERS, 2, B_RANK, B_KW), F32) * B_RANK ** -0.5
    b_gate_b = 0.1 * nrm(ks[9], (N_B_LAYERS, 2, B_KW), F32)
    b_norm_g = 1.0 + 0.02 * nrm(ks[10], (N_B_LAYERS, B_DV), F32)
    b_w_out = nrm(ks[11], (N_B_LAYERS, B_VW, D_MODEL), F32) * (B_VW ** -0.5 * DEEPNORM_BETA)
    ln1_g = 1.0 + 0.02 * nrm(ks[12], (DEPTH, D_MODEL), F32)
    ln1_b = 0.02 * nrm(ks[13], (DEPTH, D_MODEL), F32)
    mlp_w1 = nrm(ks[14], (DEPTH, D_MODEL, D_FF), F32) * D_MODEL ** -0.5
    mlp_w2 = nrm(ks[15], (DEPTH, D_FF, D_MODEL), F32) * (D_FF ** -0.5 * DEEPNORM_BETA)
    ln2_g = 1.0 + 0.02 * nrm(ks[16], (DEPTH, D_MODEL), F32)
    ln2_b = 0.02 * nrm(ks[17], (DEPTH, D_MODEL), F32)
    return {"x": x, "a_w_in": a_w_in, "a_conv": a_conv, "a_alog": a_alog, "a_dt_bias": a_dt_bias,
            "a_norm_g": a_norm_g, "a_w_out": a_w_out, "b_w_in": b_w_in, "b_gate_w2": b_gate_w2,
            "b_gate_b": b_gate_b, "b_norm_g": b_norm_g, "b_w_out": b_w_out, "ln1_g": ln1_g,
            "ln1_b": ln1_b, "mlp_w1": mlp_w1, "mlp_w2": mlp_w2, "ln2_g": ln2_g, "ln2_b": ln2_b}

def first_block(x, a_w_in, a_conv, a_alog, a_dt_bias, a_norm_g, a_w_out, b_w_in, b_gate_w2,
              b_gate_b, b_norm_g, b_w_out, ln1_g, ln1_b, mlp_w1, mlp_w2, ln2_g, ln2_b):
    for i in range(DEPTH):
        j = i // N_MIXERS
        if i % N_MIXERS == 0:
            m = _mixer_gdn(x, a_w_in[j], a_conv[j], a_alog[j], a_dt_bias[j], a_norm_g[j], a_w_out[j])
        else:
            m = _mixer_gla(x, b_w_in[j], b_gate_w2[j], b_gate_b[j], b_norm_g[j], b_w_out[j])
        x = _layernorm(DEEPNORM_ALPHA * x + m.astype(x.dtype), ln1_g[i], ln1_b[i])
        x = _layernorm(DEEPNORM_ALPHA * x + _sq_relu_mlp(x, mlp_w1[i], mlp_w2[i]).astype(x.dtype), ln2_g[i], ln2_b[i])
    return x


DEPTH_2 = 1

GRID_W = 64
CTX_LEN = 256
D_MIX = D_MODEL
D_ATTN = D_MIX // 2
D_POOL = D_MIX - D_ATTN
MLA_HEADS = 4
QK_NOPE_DIM = 128
QK_ROPE_DIM = 64
QK_HEAD_DIM = QK_NOPE_DIM + QK_ROPE_DIM
V_HEAD_DIM = D_ATTN // MLA_HEADS
Q_LORA_RANK = 256
KV_LORA_RANK = 128
ROPE_AXIS_DIM = QK_ROPE_DIM // 2
ROPE_BASE = 10000.0
POOL_WINDOWS = (2, 4, 8, 16)
POOL_GROUPS = len(POOL_WINDOWS)
POOL_GROUP_DIM = D_POOL // POOL_GROUPS
Q_BLOCK = 128
NORM_EPS = 1e-6

OFF_CQ = 0
OFF_CKV = OFF_CQ + Q_LORA_RANK
OFF_KR = OFF_CKV + KV_LORA_RANK
OFF_GA = OFF_KR + QK_ROPE_DIM
OFF_PIN = OFF_GA + D_ATTN
OFF_GP = OFF_PIN + D_POOL
D_IN_PROJ = OFF_GP + D_POOL


def _rms(x, g):
    xf = x.astype(jnp.float32)
    y = xf * lax.rsqrt(jnp.mean(xf * xf, axis=-1, keepdims=True) + NORM_EPS)
    return (y * g.astype(jnp.float32)).astype(x.dtype)

def _rotate_half(x):
    x1, x2 = jnp.split(x, 2, axis=-1)
    return jnp.concatenate([-x2, x1], axis=-1)

def _axial_rope_tables(L):
    rows = L // GRID_W
    row = jnp.repeat(jnp.arange(rows, dtype=jnp.float32), GRID_W)
    col = jnp.tile(jnp.arange(GRID_W, dtype=jnp.float32), rows)
    n_freq = ROPE_AXIS_DIM // 2
    inv = ROPE_BASE ** (-jnp.arange(n_freq, dtype=jnp.float32) / n_freq)
    ang_r = row[:, None] * inv
    ang_c = col[:, None] * inv
    ang = jnp.concatenate([ang_r, ang_r, ang_c, ang_c], axis=-1)
    return jnp.cos(ang), jnp.sin(ang)

def _apply_axial_rope(x, cos, sin):
    xr, xc = jnp.split(x, 2, axis=-1)
    rot = jnp.concatenate([_rotate_half(xr), _rotate_half(xc)], axis=-1)
    c = cos[:, None, :]
    s = sin[:, None, :]
    return (x.astype(jnp.float32) * c + rot.astype(jnp.float32) * s).astype(x.dtype)

def _mla_qkv(u, q_lora_g, w_uq, kv_lora_g, w_ukv, q_norm_g, k_norm_g, rope):
    B, L = u.shape[0], u.shape[1]
    cq = u[..., OFF_CQ:OFF_CKV]
    ckv = u[..., OFF_CKV:OFF_KR]
    k_rope = u[..., OFF_KR:OFF_GA]
    q = (_rms(cq, q_lora_g) @ w_uq).reshape(B, L, MLA_HEADS, QK_HEAD_DIM)
    kv = (_rms(ckv, kv_lora_g) @ w_ukv).reshape(B, L, MLA_HEADS, QK_NOPE_DIM + V_HEAD_DIM)
    k_nope, v = kv[..., :QK_NOPE_DIM], kv[..., QK_NOPE_DIM:]
    k = jnp.concatenate(
        [k_nope, jnp.broadcast_to(k_rope[:, :, None, :], (B, L, MLA_HEADS, QK_ROPE_DIM))], axis=-1)
    q = _rms(q, q_norm_g)
    k = _rms(k, k_norm_g)
    if rope is not None:
        cos, sin = rope
        q = jnp.concatenate([q[..., :QK_NOPE_DIM], _apply_axial_rope(q[..., QK_NOPE_DIM:], cos, sin)], axis=-1)
        k = jnp.concatenate([k[..., :QK_NOPE_DIM], _apply_axial_rope(k[..., QK_NOPE_DIM:], cos, sin)], axis=-1)
    tr = lambda t: jnp.transpose(t, (0, 2, 1, 3))
    return tr(q), tr(k), tr(v)

def _attend(q, k, v):
    B, H, Lq, dk = q.shape
    nb = Lq // Q_BLOCK
    scale = QK_HEAD_DIM ** -0.5
    qb = jnp.transpose(q.reshape(B, H, nb, Q_BLOCK, dk), (2, 0, 1, 3, 4))

    def one(qblk):
        s = jnp.einsum('bhqd,bhkd->bhqk', qblk, k).astype(jnp.float32) * scale
        p = jax.nn.softmax(s, axis=-1)
        return jnp.einsum('bhqk,bhkd->bhqd', p.astype(v.dtype), v)

    o = lax.map(one, qb)
    o = jnp.transpose(o, (1, 3, 0, 2, 4)).reshape(B, Lq, H * v.shape[-1])
    return o

def _multiscale_pool(u, w_pool, pool_scale):
    B, L, _ = u.shape
    ug = u.reshape(B, L, POOL_GROUPS, POOL_GROUP_DIM)
    cs = jnp.concatenate(
        [jnp.zeros((B, 1, POOL_GROUPS, POOL_GROUP_DIM), jnp.float32),
         jnp.cumsum(ug.astype(jnp.float32), axis=1)], axis=1)
    t = jnp.arange(L, dtype=jnp.int32)[:, None]
    w = jnp.array(POOL_WINDOWS, dtype=jnp.int32)[None, :]
    lo = jnp.clip(t - w // 2, 0, L)
    hi = jnp.clip(t - w // 2 + w, 0, L)
    g = jnp.arange(POOL_GROUPS, dtype=jnp.int32)[None, :]
    win_sum = cs[:, hi, g, :] - cs[:, lo, g, :]
    cnt = (hi - lo).astype(jnp.float32)[None, :, :, None]
    pooled = (win_sum / cnt - ug.astype(jnp.float32)).astype(u.dtype)
    y = jnp.einsum('blgc,gcd->blgd', pooled, w_pool).reshape(B, L, D_POOL)
    return y * pool_scale

def _branches(u, mla_out, w_pool, pool_scale):
    gate_a = u[..., OFF_GA:OFF_PIN]
    pool_in = u[..., OFF_PIN:OFF_GP]
    gate_p = u[..., OFF_GP:D_IN_PROJ]
    br_a = jax.nn.silu(gate_a) * mla_out
    br_p = jax.nn.silu(gate_p) * _multiscale_pool(pool_in, w_pool, pool_scale)
    return jnp.concatenate([br_a, br_p], axis=-1)

def second_inputs(seed: int = 0) -> dict:
    key = jax.random.key(seed)
    ks = jax.random.split(key, 20)
    f32 = jnp.float32
    nrm = lambda k, shape, s: jax.random.normal(k, shape, f32) * s
    return {
        "x": nrm(ks[0], (BATCH, SEQ, D_MODEL), 1.0),
        "c": nrm(ks[1], (BATCH, D_MODEL), 1.0),
        "ctx": nrm(ks[2], (BATCH, CTX_LEN, D_MODEL), 1.0),
        "c_ctx": nrm(ks[3], (D_MODEL,), 1.0),
        "w_mod": nrm(ks[4], (DEPTH_2, D_MODEL, 3 * D_MODEL), 0.5 * D_MODEL ** -0.5),
        "b_mod": nrm(ks[5], (DEPTH_2, 3 * D_MODEL), 0.02),
        "norm_g": 1.0 + nrm(ks[6], (DEPTH_2, D_MODEL), 0.1),
        "w_in": nrm(ks[7], (DEPTH_2, D_MODEL, D_IN_PROJ), D_MODEL ** -0.5),
        "q_lora_g": 1.0 + nrm(ks[8], (DEPTH_2, Q_LORA_RANK), 0.1),
        "w_uq": nrm(ks[9], (DEPTH_2, Q_LORA_RANK, MLA_HEADS * QK_HEAD_DIM), Q_LORA_RANK ** -0.5),
        "kv_lora_g": 1.0 + nrm(ks[10], (DEPTH_2, KV_LORA_RANK), 0.1),
        "w_ukv": nrm(ks[11], (DEPTH_2, KV_LORA_RANK, MLA_HEADS * (QK_NOPE_DIM + V_HEAD_DIM)), KV_LORA_RANK ** -0.5),
        "q_norm_g": 1.0 + nrm(ks[12], (DEPTH_2, QK_HEAD_DIM), 0.1),
        "k_norm_g": 1.0 + nrm(ks[13], (DEPTH_2, QK_HEAD_DIM), 0.1),
        "w_pool": nrm(ks[14], (DEPTH_2, POOL_GROUPS, POOL_GROUP_DIM, POOL_GROUP_DIM), POOL_GROUP_DIM ** -0.5),
        "pool_scale": 1.0 + nrm(ks[15], (DEPTH_2, D_POOL), 0.1),
        "w_out": nrm(ks[16], (DEPTH_2, D_MIX, D_MODEL), D_MIX ** -0.5),
    }

def second_block(x, c, ctx, c_ctx, w_mod, b_mod, norm_g, w_in, q_lora_g, w_uq, kv_lora_g, w_ukv,
              q_norm_g, k_norm_g, w_pool, pool_scale, w_out):
    L = x.shape[1]
    rope = _axial_rope_tables(L)
    for l in range(DEPTH_2):
        mod = jax.nn.silu(c) @ w_mod[l] + b_mod[l]
        shift, scale, gate = jnp.split(mod, 3, axis=-1)
        mod_c = jax.nn.silu(c_ctx) @ w_mod[l] + b_mod[l]
        shift_c, scale_c, gate_c = jnp.split(mod_c, 3, axis=-1)

        h = _rms(x, norm_g[l]) * (1.0 + scale[:, None, :]) + shift[:, None, :]
        hc = _rms(ctx, norm_g[l]) * (1.0 + scale_c) + shift_c
        u = h @ w_in[l]
        uc = hc @ w_in[l]

        q, k, v = _mla_qkv(u, q_lora_g[l], w_uq[l], kv_lora_g[l], w_ukv[l],
                           q_norm_g[l], k_norm_g[l], rope)
        qc, kc, vc = _mla_qkv(uc, q_lora_g[l], w_uq[l], kv_lora_g[l], w_ukv[l],
                              q_norm_g[l], k_norm_g[l], None)
        k_all = jnp.concatenate([kc, k], axis=2)
        v_all = jnp.concatenate([vc, v], axis=2)
        attn = _attend(q, k_all, v_all)
        y = _branches(u, attn, w_pool[l], pool_scale[l]) @ w_out[l]
        x_new = x + gate[:, None, :] * y

        if l < DEPTH_2 - 1:
            attn_c = _attend(qc, kc, vc)
            yc = _branches(uc, attn_c, w_pool[l], pool_scale[l]) @ w_out[l]
            ctx = ctx + gate_c * yc
        x = x_new
    return x


def setup_inputs(seed=0):
    out = dict(first_inputs(seed))
    for name, value in second_inputs(seed + 1).items():
        if name != "x":
            out[name + "_2"] = value
    return out


def reference(
    x, a_w_in, a_conv, a_alog, a_dt_bias, a_norm_g, a_w_out, b_w_in, b_gate_w2, b_gate_b,
    b_norm_g, b_w_out, ln1_g, ln1_b, mlp_w1, mlp_w2, ln2_g, ln2_b, c_2, ctx_2, c_ctx_2, w_mod_2,
    b_mod_2, norm_g_2, w_in_2, q_lora_g_2, w_uq_2, kv_lora_g_2, w_ukv_2, q_norm_g_2, k_norm_g_2,
    w_pool_2, pool_scale_2, w_out_2,
):
    x = first_block(
        x, a_w_in, a_conv, a_alog, a_dt_bias, a_norm_g, a_w_out, b_w_in, b_gate_w2, b_gate_b,
        b_norm_g, b_w_out, ln1_g, ln1_b, mlp_w1, mlp_w2, ln2_g, ln2_b,
    )
    return second_block(
        x, c_2, ctx_2, c_ctx_2, w_mod_2, b_mod_2, norm_g_2, w_in_2, q_lora_g_2, w_uq_2,
        kv_lora_g_2, w_ukv_2, q_norm_g_2, k_norm_g_2, w_pool_2, pool_scale_2, w_out_2,
    )


_drawn_inputs = setup_inputs


def setup_inputs(seed=0):
    import zlib

    import numpy as np

    out = dict(_drawn_inputs(seed))
    spreads = {}
    factors = {'a_norm_g': 8.0,
     'b_gate_b': 6.255,
     'b_norm_g': 8.0,
     'ctx_2': 8.0,
     'c_ctx_2': 4.851,
     'b_mod_2': 5.528,
     'norm_g_2': 3.137,
     'q_lora_g_2': 8.0,
     'w_uq_2': 3.986,
     'kv_lora_g_2': 8.0,
     'q_norm_g_2': 8.0,
     'k_norm_g_2': 8.0,
     'pool_scale_2': 4.465}
    for name, (base, spread) in spreads.items():
        noise = np.random.default_rng([zlib.crc32(name.encode()), seed]).standard_normal(out[name].shape)
        drawn = base * np.exp(spread * noise) if base else spread * noise
        out[name] = __import__('jax').numpy.asarray(drawn.astype(out[name].dtype))
    for name, factor in factors.items():
        out[name] = (out[name] * factor).astype(out[name].dtype)
    return out
```

```python
from contextlib import ExitStack

import numpy as np

import concourse.bass as bass
from concourse import mybir

ALU = mybir.AluOpType
ACT = mybir.ActivationFunctionType
F32 = mybir.dt.float32
BF16 = mybir.dt.bfloat16
U8 = mybir.dt.uint8
AX_X = mybir.AxisListType.X

P = 128
D = 1024
S = 512
ST = S // P
KT = D // P
FF = 4 * D
AH = 8
BH = 4
BDV = 256
RANK = 16
CONV = 5
CTX = 256
CT = CTX // P
LEVELS = 7
ALPHA = 4.0 ** 0.25
LN_EPS = 1e-5
RMS_EPS = 1e-6
QK_DIM = 192
SLAB = 2048
POOL_W = (2, 4, 8, 16)

PH = {}
_n = 0
for _name, _c in (("a_in", 16), ("a_out", 4), ("up0", 16), ("down0", 16), ("b_qk", 4), ("b_v", 4), ("b_r", 4),
                  ("b_out", 4), ("up1", 16), ("down1", 16), ("c_in", 8), ("c_out", 4)):
    PH[_name] = (_n, _c)
    _n += _c
NSLABS = _n

VEC = {}
_n = 0
for _name, _c in (("norm_g", 8), ("b_mod", 16), ("pool_scale", 4), ("q_lora_g", 2), ("kv_lora_g", 1),
                  ("a_norm_g", 1), ("b_norm_g", 2), ("q_norm_g", 2), ("k_norm_g", 2), ("c", 8), ("c_ctx", 8)):
    VEC[_name] = (_n, _c)
    _n += _c
NVEC = _n


def shape_constants():
    t = np.arange(P)
    le = (t[:, None] <= t[None, :]).astype(np.float32)
    gt = (t[:, None] > t[None, :]).astype(np.float32)
    rev = lambda m: m[::-1, ::-1]
    cum = np.zeros((LEVELS + 2, P, P), np.float32)
    pair = np.zeros((LEVELS, P, P), np.float32)
    for l in range(LEVELS):
        b = 1 << l
        mid = t // (2 * b) * 2 * b + b
        second = t >= mid
        cum[l] = np.where(second[None, :], (t[:, None] >= mid[None, :]) & (t[:, None] <= t[None, :]),
                          (t[:, None] > t[None, :]) & (t[:, None] < mid[None, :]))
        pair[l] = (mid[:, None] == mid[None, :]) & ~second[:, None] & second[None, :]
    cum[LEVELS], cum[LEVELS + 1] = le, gt
    both = lambda m: np.stack([m, m[:, ::-1, ::-1]])
    col = lambda m: np.ascontiguousarray(np.moveaxis(m, -2, 0)).reshape(P, -1)
    tri = col(np.stack([le, rev(le), gt, rev(gt)]))
    eye = np.eye(P, dtype=np.float32)
    masks = np.concatenate([both(pair), np.broadcast_to(eye, (2, 1, P, P))], axis=1)
    rows = S // 64
    n = 16
    inv = (10000.0 ** (-np.arange(n, dtype=np.float32) / n)).astype(np.float32)
    row = np.repeat(np.arange(rows, dtype=np.float32), 64)[:, None] * inv
    cl = np.tile(np.arange(64, dtype=np.float32), rows)[:, None] * inv
    ang = np.concatenate([row, row, cl, cl], axis=-1).T
    cos = np.concatenate([np.ones((64, CTX), np.float32), np.cos(ang)], axis=1)
    sin = np.concatenate([np.zeros((64, CTX), np.float32), np.sin(ang)], axis=1)
    rot = np.zeros((64, P), np.float32)
    for base in (0, 32):
        for i in range(16):
            rot[base + 16 + i, base + i] = -1.0
            rot[base + i, base + 16 + i] = 1.0
    tt = np.arange(S)
    inv_count = np.stack([1.0 / (np.clip(tt - w // 2 + w, 0, S) - np.clip(tt - w // 2, 0, S)) for w in POOL_W])
    return {
        "k_eye": eye, "k_tri": tri, "k_negpair": col(-both(pair).reshape(-1, P, P)),
        "k_cum": col(both(cum).reshape(-1, P, P)), "k_masks": col(masks.reshape(-1, P, P)).astype(np.float32),
        "k_cos": cos.astype(np.float32), "k_sin": sin.astype(np.float32), "k_rot": rot,
        "k_invcount": inv_count.astype(np.float32),
    }


def build(nc, a, out):
    ctx = ExitStack()
    with ctx:
        sb = lambda name, shape, dt=F32: ctx.enter_context(nc.sbuf_tensor(name, shape, dt))
        sem = lambda name: ctx.enter_context(nc.semaphore(name))

        X = sb("X", [P, ST, D])
        act_hi = sb("act_hi", [P, KT, S], BF16)
        act_lo = sb("act_lo", [P, KT, S], BF16)
        raw = [sb(f"raw{i}", [P, SLAB]) for i in range(2)]
        whi = [sb(f"whi{i}", [P, SLAB], BF16) for i in range(2)]
        wlo = [sb(f"wlo{i}", [P, SLAB], BF16) for i in range(2)]
        arena = sb("arena", [P, 16384])
        eye = sb("eye", [P, P])
        ones = sb("ones", [P, P])
        cols = sb("cols", [P, NVEC])
        convw = sb("convw", [P, CONV * 24])
        stats = sb("stats", [P, ST + CT, 2, 6])
        mv = sb("mv", [P, ST + CT, 2])
        rstd = sb("rstd", [P, ST + CT, 2])
        modc = sb("modc", [P, 16, 2])
        csil = sb("csil", [P, 16])
        pause = sb("pause", [P, 16])
        work = sb("work", [P, 18560])
        bk = [ctx.enter_context(nc.psum_tensor(f"bk{i}", [P, 512], F32)) for i in range(8)]
        hid_hi = arena[:, 0:8192].bitcast(BF16).rearrange("p (k s) -> p k s", k=32)
        hid_lo = arena[:, 8192:16384].bitcast(BF16).rearrange("p (k s) -> p k s", k=32)
        lnrow = work[:, 16384:18432].rearrange("p (g n) -> p g n", g=2)
        wmod = work[:, 0:8192].rearrange("p (k n) -> p k n", k=KT)
        hsq = work[:, 8192:10240].rearrange("p (j s) -> p j s", j=4)

        def carve(tensor, sizes, start=0):
            views, at = {}, start
            for name, *shape in sizes:
                n = int(np.prod(shape))
                v = tensor[:, at:at + n]
                if len(shape) == 2:
                    v = v.rearrange("p (x y) -> p x y", x=shape[0])
                elif len(shape) == 3:
                    v = v.rearrange("p (x y z) -> p x y z", x=shape[0], y=shape[1])
                views[name] = v
                at += n
            assert at <= tensor.shape[1], (at, tensor.shape)
            return views

        def col(name, i=0):
            r = VEC[name][0] + i
            return cols[:, r:r + 1]

        raw_loaded = [sem(f"raw_loaded{i}") for i in range(2)]
        w_hi_ready = sem("w_hi_ready")
        w_ready = sem("w_ready")
        slab_used = sem("slab_used")
        acc_ready = sem("acc_ready")
        acc_free = sem("acc_free")
        sum_ready = sem("sum_ready")
        sum_added = sem("sum_added")
        x_ready = sem("x_ready")
        xt_ready = sem("xt_ready")
        act_hi_ready = sem("act_hi_ready")
        act_ready = sem("act_ready")
        st_stats = sem("st_stats")
        st_mean = sem("st_mean")
        st_ln = sem("st_ln")
        st_rstd = sem("st_rstd")
        st_center = sem("st_center")
        lnrow_loaded = sem("lnrow_loaded")
        x_loaded = sem("x_loaded")
        const_loaded = sem("const_loaded")
        memset_done = sem("memset_done")
        vec_turned = sem("vec_turned")
        vec_ready = sem("vec_ready")

        FS = {}
        n = 0
        for name in ("a_in", "up0", "b_qk", "b_r", "up1", "c_in"):
            FS[name] = n
            n += PH[name][1]
        TH = {}
        n = 0
        for name in ("a_out", "down0", "b_v", "b_out", "down1", "c_out"):
            TH[name] = n
            n += 2

        def slab_source(name, k2, b):
            w, c0 = {"a_in": (a["a_w_in"][0], 0), "up0": (a["mlp_w1"][0], 0), "up1": (a["mlp_w1"][1], 0),
                     "b_qk": (a["b_w_in"][0], 0), "b_r": (a["b_w_in"][0], 2048), "c_in": (a["w_in_2"][0], -64)}[name]
            return w[:, bass.ds(k2 * 512 + (b * 256 + c0), 256)].rearrange("(k p) n -> p k n", p=P)

        def tok_source(name, half, k2, b):
            w, c0 = {"a_out": (a["a_w_out"][0], 0), "b_out": (a["b_w_out"][0], 0), "c_out": (a["w_out_2"][0], 0),
                     "down0": (a["mlp_w2"][0], 0), "down1": (a["mlp_w2"][1], 0), "b_v": (a["b_w_in"][0], 1024)}[name]
            return w[bass.ds(k2 * 1024 + b * 512, 512), c0 + half * 512:c0 + half * 512 + 512].rearrange(
                "(k p) n -> p k n", p=P)

        def slab_view(t, kts):
            return t[:, 0:SLAB].rearrange("p (k n) -> p k n", k=kts)

        def load_slab(sp, k, b, source, kts=KT):
            if not (isinstance(k, int) and k == 0):
                sp.wait_ge(w_ready, k * 2 + (b - 1))
            dst = slab_view(raw[b], kts)
            if source.shape[2] != SLAB // kts:
                dst = raw[b][:, 0:kts * source.shape[2]].rearrange("p (k n) -> p k n", k=kts)
            sp.dma_start(dst, source).then_inc(raw_loaded[b], 16)

        def split_hi(act, k, b):
            act.wait_ge(raw_loaded[b], k * 16 + 16)
            if not (isinstance(k, int) and k == 0):
                act.wait_ge(slab_used, k * 2 + (b - 1))
            nc.scalar.activation(whi[b][:, :], raw[b][:, :], ACT.Copy).then_inc(w_hi_ready, 1)

        def split_lo(dve, k, b):
            dve.wait_ge(w_hi_ready, k * 2 + (b + 1))
            nc.vector.tensor_tensor(wlo[b][:, :], raw[b][:, :], whi[b][:, :], ALU.subtract).then_inc(w_ready, 1)

        def next_pair(name, k2):
            return k2 + (PH[name][0] // 2 + 1)

        def mm3(acc, lhs_hi, lhs_lo, rhs_hi, rhs_lo, first, last):
            nc.tensor.matmul(acc, lhs_hi, rhs_hi, start=first, stop=False, skip_group_check=True)
            nc.tensor.matmul(acc, lhs_hi, rhs_lo, start=False, stop=False, skip_group_check=True)
            return nc.tensor.matmul(acc, lhs_lo, rhs_hi, start=False, stop=last, skip_group_check=True)

        def pe_feature_slab(pe, name, k2, b, width=256):
            pe.wait_ge(w_ready, k2 * 2 + (PH[name][0] + b + 1))
            wd = 256 if width == 256 else width
            hi, lo = (t[b][:, 0:KT * wd].rearrange("p (k n) -> p k n", k=KT) for t in (whi, wlo))
            for j in range(2):
                if not (isinstance(k2, int) and 2 * FS[name] + 4 * k2 + 2 * b + j < 4):
                    pe.wait_ge(acc_free, k2 * 4 + (2 * FS[name] + 2 * b + j - 3))
                m = min(P, wd - j * P)
                c = slice(j * P, j * P + m)
                for kt in range(KT):
                    mm = mm3(bk[2 * b + j][0:m, :], hi[:, kt, c], lo[:, kt, c], act_hi[:, kt, :], act_lo[:, kt, :],
                             kt == 0, kt == KT - 1)
                mm.then_inc(acc_ready if j == 0 else slab_used, 1)

        def wait_tile(eng, name, k2, b, j):
            if j == 0:
                eng.wait_ge(acc_ready, k2 * 2 + (FS[name] + b + 1))
            else:
                eng.wait_ge(slab_used, k2 * 2 + (PH[name][0] + b + 1))

        def pe_token_slab(pe, name, half, k2, b, pair0, src_hi, src_lo, first, last):
            pe.wait_ge(w_ready, k2 * 2 + (PH[name][0] + 2 * pair0 + b + 1))
            hi, lo = slab_view(whi[b], 4), slab_view(wlo[b], 4)
            for st in range(ST):
                tok = slice(st * P, st * P + P)
                for kt in range(4):
                    if isinstance(k2, int):
                        f = k2 * 8 + b * 4 + kt
                        l_hi, l_lo = src_hi[:, f, tok], src_lo[:, f, tok]
                    else:
                        f = bass.ds(k2 * 8 + (b * 4 + kt), 1)
                        l_hi, l_lo = src_hi[:, f, tok].squeeze(1), src_lo[:, f, tok].squeeze(1)
                    mm = mm3(bk[4 * half + st][:, :], l_hi, l_lo, hi[:, kt, :], lo[:, kt, :],
                             first and kt == 0, last and kt == 3)
                if st == 3:
                    mm.then_inc(slab_used, 1)
                elif last:
                    mm.then_inc(sum_ready, 1)

        def wait_sum(eng, name, half, st):
            if st < 3:
                eng.wait_ge(sum_ready, 3 * (TH[name] + half) + st + 1)
            else:
                eng.wait_ge(slab_used, PH[name][0] + PH[name][1] // 2 * (half + 1))

        def pe_token_layer(pe, name, src_hi, src_lo):
            pairs = PH[name][1] // 4
            for half in range(2):
                pair0 = half * pairs
                if pairs == 1:
                    pe_token_slab(pe, name, half, 0, 0, pair0, src_hi, src_lo, True, False)
                    pe_token_slab(pe, name, half, 0, 1, pair0, src_hi, src_lo, False, True)
                    continue
                for b in range(2):
                    pe_token_slab(pe, name, half, 0, b, pair0, src_hi, src_lo, b == 0, False)
                with pe.Fori(1, pairs - 1) as k2:
                    for b in range(2):
                        pe_token_slab(pe, name, half, k2, b, pair0, src_hi, src_lo, False, False)
                for b in range(2):
                    pe_token_slab(pe, name, half, pairs - 1, b, pair0, src_hi, src_lo, False, b == 1)

        def pe_turn(pe, e, half0_moved=None):
            if half0_moved is not None:
                pe.wait_ge(sum_added, half0_moved)
            for st in range(ST):
                pe.wait_ge(x_ready, 4 * (e - 1) + st + 1)
                for hf in range(2):
                    if st >= 2:
                        pe.wait_ge(act_ready, 8 * e + 2 * (st - 2) + hf + 1)
                    for k in range(4):
                        kt = 4 * hf + k
                        mm = nc.tensor.transpose(bk[2 * (st % 2) + hf][:, k * P:k * P + P],
                                                 X[:, st, kt * P:kt * P + P], eye[:, :])
                    mm.then_inc(xt_ready, 1)

        def act_turned(act, e, tiles=range(ST)):
            for st in tiles:
                for hf in range(2):
                    act.wait_ge(xt_ready, 8 * e + 2 * st + hf + 1)
                    nc.scalar.activation(act_hi[:, 4 * hf:4 * hf + 4, st * P:st * P + P],
                                         bk[2 * (st % 2) + hf][:, :].rearrange("p (k s) -> p k s", k=4),
                                         ACT.Copy).then_inc(act_hi_ready, 1)

        def dve_turned(dve, e, st):
            for hf in range(2):
                dve.wait_ge(act_hi_ready, 8 * e + 2 * st + hf + 1)
                c = (slice(None), slice(4 * hf, 4 * hf + 4), slice(st * P, st * P + P))
                nc.vector.tensor_tensor(act_lo[c], bk[2 * (st % 2) + hf][:, :].rearrange("p (k s) -> p k s", k=4),
                                        act_hi[c], ALU.subtract).then_inc(act_ready, 1)

        def dve_add_half(dve, name, half, st):
            wait_sum(dve, name, half, st)
            xs = X[:, st, half * 512:half * 512 + 512]
            nc.vector.scalar_tensor_tensor(out=xs, in0=xs, scalar=ALPHA, in1=bk[4 * half + st][:, :],
                                           op0=ALU.mult, op1=ALU.add).then_inc(sum_added, 1)

        def dve_norm(dve, name, e):
            done = 4 * TH[name]
            def finish(st):
                dve.wait_ge(st_rstd, 4 * (e - 1) + st + 1)
                if st == 0:
                    dve.wait_ge(lnrow_loaded, 32 * e)
                nc.vector.scalar_tensor_tensor(out=X[:, st, :], in0=X[:, st, :], scalar=mv[:, st, 0:1],
                                               in1=lnrow[:, 0, :], op0=ALU.subtract, op1=ALU.mult).then_inc(st_center, 1)
                dve.wait_ge(st_center, 4 * (e - 1) + st + 1)
                nc.vector.scalar_tensor_tensor(out=X[:, st, :], in0=X[:, st, :], scalar=rstd[:, st, 1:2],
                                               in1=lnrow[:, 1, :], op0=ALU.mult, op1=ALU.add).then_inc(x_ready, 1)
            for st in range(ST):
                dve_add_half(dve, name, 1, st)
                dve.wait_ge(sum_added, done + 4 + st + 1)
                for hf in range(2):
                    nc.vector.bn_stats(stats[:, st, hf, :], X[:, st, hf * 512:hf * 512 + 512]).then_inc(st_stats, 1)
                dve.wait_ge(st_stats, 8 * (e - 1) + 2 * st + 2)
                nc.vector.bn_aggr(mv[:, st, :], stats[:, st, :, :]).then_inc(st_mean, 1)
                if st >= 1:
                    finish(st - 1)
                if st >= 2 and e < 4:
                    dve_turned(dve, e, st - 2)
            finish(3)
            if e < 4:
                dve_turned(dve, e, 2)
                dve_turned(dve, e, 3)

        def act_norm(act, e):
            for st in range(ST):
                act.wait_ge(st_mean, 4 * (e - 1) + st + 1)
                nc.scalar.activation(rstd[:, st, 0:1], mv[:, st, 1:2], ACT.Ln, bias=LN_EPS).then_inc(st_ln, 1)
                act.wait_ge(st_ln, 4 * (e - 1) + st + 1)
                nc.scalar.activation(rstd[:, st, 1:2], rstd[:, st, 0:1], ACT.Exp, scale=-0.5).then_inc(st_rstd, 1)
                if st >= 2 and e < 4:
                    act_turned(act, e, [st - 2])
            if e < 4:
                act_turned(act, e, [2, 3])

        def act_splits(act, name, first, last):
            with act.Fori(first // 2, last // 2) as k2:
                for b in range(2):
                    split_hi(act, next_pair(name, k2), b)

        def dve_splits(dve, name, first, last):
            with dve.Fori(first // 2, last // 2) as k2:
                for b in range(2):
                    split_lo(dve, next_pair(name, k2), b)

        def act_token_layer(act, name, e):
            n = PH[name][1]
            act_splits(act, name, 0, n - 2)
            split_hi(act, next_pair(name, n // 2 - 1), 0)
            act_norm(act, e)
            split_hi(act, next_pair(name, n // 2 - 1), 1)

        def dve_token_layer(dve, name, e):
            n = PH[name][1]
            dve_splits(dve, name, 0, n // 2)
            for st in range(ST):
                dve_add_half(dve, name, 0, st)
            if n > 4:
                dve_splits(dve, name, n // 2, n - 2)
            split_lo(dve, next_pair(name, n // 2 - 1), 0)
            dve_norm(dve, name, e)
            split_lo(dve, next_pair(name, n // 2 - 1), 1)

        def sp_feature(sp, name, first=0):
            with sp.Fori(first, PH[name][1] // 2) as k2:
                for b in range(2):
                    load_slab(sp, k2 + PH[name][0] // 2, b, slab_source(name, k2, b))

        def sp_token(sp, name):
            pairs = PH[name][1] // 4
            for half in range(2):
                if pairs == 1:
                    for b in range(2):
                        load_slab(sp, PH[name][0] // 2 + half, b, tok_source(name, half, 0, b), 4)
                else:
                    with sp.Fori(0, pairs) as k2:
                        for b in range(2):
                            load_slab(sp, k2 + (PH[name][0] // 2 + half * pairs), b, tok_source(name, half, k2, b), 4)

        a_qkvT = arena[:, 0:12288].rearrange("p (n s) -> p n s", n=24)
        a_zT = arena[:, 12288:16384].rearrange("p (n s) -> p n s", n=AH)
        A = carve(work, [("tri", 4, P), ("negpair", 14, P), ("beta", ST, 16), ("g", ST, 16), ("bexp", ST, 16),
                         ("kdec", ST, 16), ("glast", ST, 16), ("t1", ST, 16), ("t2", ST, 16),
                         ("sq", 2, S), ("rs", 2, S), ("qn", S), ("kn", S), ("vst", S), ("ktok", ST, P),
                         *[(f"{n}{d}", ST, P) for d in range(2) for n in ("GL", "GG", "A", "PT", "qd", "kbe", "kd",
                                                                          "vb", "X", "Y")],
                         ("vn0", P), ("vn1", P), ("S0", P), ("S1", P)])
        CB = carve(work, [("cbuf", 4, S + 4), ("cacc", 4, S)], start=2752)
        gwv = carve(work, [("raw", KT, 32), ("hl", 256), ("dt", 16), ("alog", 16), ("ea", 16)], start=17856)
        gw_raw = gwv["raw"]
        gw_hi, gw_lo = (gwv["hl"][:, i * 128:i * 128 + 128].bitcast(BF16).rearrange("p (k n) -> p k n", k=KT)
                        for i in range(2))
        vrow = carve(work, [("conv", P), ("vec", P)], start=7000)

        def bc_tok(t):
            return t.broadcast_to([P, ST, P])

        def bc_mat(t):
            return t.unsqueeze(1).broadcast_to([P, ST, P])

        def chunks(b):
            return b[:, :].rearrange("p (c s) -> p c s", c=ST)

        conv_step = sem("conv_step")
        conv_silu = sem("conv_silu")
        z_ready = sem("z_ready")
        G = {n: sem("g_" + n) for n in (
            "w_loaded w_hi w_ready gate_mm gate_exp beta1 beta2 logit absd expd softplus1 softplus g1 g "
            "cum_mm cum_exp bexp l2_sq l2_sum l2_ln l2_rs qkn v_copied turned k_tok kk gl decay_mm decay_exp pt_mask "
            "vb ed a pt qd kx p1 t2 p2 y0 y turned_y x w_mm w pv vn ps s o_done o_sq o_sum o_ln o_rs of1 of "
            "o_hi o_out").split()}

        def sp_start(sp):
            for b in range(2):
                load_slab(sp, 0, b, slab_source("a_in", 0, b))

        def act_start(act):
            for st in range(ST):
                act.dma_start(X[:, st, :], a["x"][0, st * P:st * P + P, :]).then_inc(x_loaded, 16)

        NCONST = 5
        def pool_start(pool):
            nc.gpsimd.memset(vrow["vec"], 0.0).then_inc(memset_done, 1)
            nc.gpsimd.memset(ones[:, :], 1.0).then_inc(memset_done, 1)
            nc.gpsimd.memset(CB["cbuf"], 0.0).then_inc(memset_done, 1)
            nc.gpsimd.memset(stats[:, :, :, :], 0.0).then_inc(hid_ready, 4)
            nc.gpsimd.memset(mv[:, :, :], 0.0).then_inc(B["exp"], 3)
            nc.gpsimd.memset(rstd[:, :, :], 0.0).then_inc(B["st"], 2)
            credits = ((G["o_out"], 1), (G["o_done"], 1), (B["o_out"], 2), (B["o_done"], 1), (B["e_mm"], 1), (HT.sem, 1), (HV.sem, 1))
            for i, (s, n) in enumerate(credits):
                nc.gpsimd.memset(pause[:, 8 + i:9 + i], 0.0).then_inc(s, n)
            pool.dma_start(eye[:, :], a["k_eye"]).then_inc(const_loaded, 16)
            pool.dma_start(vrow["conv"][0:CONV * 24, :], a["a_conv"][0].rearrange("k (n p) -> (k n) p", p=P)
                           ).then_inc(const_loaded, 16)
            pool.dma_start(gw_raw, a["a_w_in"][0, :, 4096:4128].rearrange("(k p) n -> p k n", p=P)).then_inc(const_loaded, 16)
            pool.dma_start(A["tri"], a["k_tri"].rearrange("p (m s) -> p m s", m=4)).then_inc(const_loaded, 16)
            pool.dma_start(A["negpair"], a["k_negpair"].rearrange("p (m s) -> p m s", m=14)).then_inc(const_loaded, 16)
            pool.dma_start(gwv["dt"], a["a_dt_bias"][0].rearrange("d h -> (d h)").partition_broadcast(P)
                           ).then_inc(G["w_loaded"], 16)
            pool.dma_start(gwv["alog"], a["a_alog"][0].rearrange("d h -> (d h)").partition_broadcast(P)
                           ).then_inc(G["w_loaded"], 16)
            pool.wait_ge(memset_done, 1)
            rows = [("norm_g", a["norm_g_2"][0]), ("b_mod", a["b_mod_2"][0, 0:2048]), ("pool_scale", a["pool_scale_2"][0]),
                    ("q_lora_g", a["q_lora_g_2"][0]), ("kv_lora_g", a["kv_lora_g_2"][0]), ("a_norm_g", a["a_norm_g"][0]),
                    ("b_norm_g", a["b_norm_g"][0]), ("c", a["c_2"][0]), ("c_ctx", a["c_ctx_2"])]
            for name, v in rows:
                r, n = VEC[name]
                pool.dma_start(vrow["vec"][r:r + n, :], v.rearrange("(n p) -> n p", p=P)).then_inc(vec_loaded, 16)
            for name in ("q_norm_g", "k_norm_g"):
                r, v = VEC[name][0], a[name + "_2"]
                pool.dma_start(vrow["vec"][r:r + 1, :], v[:, 0:P]).then_inc(vec_loaded, 16)
                pool.dma_start(vrow["vec"][r + 1:r + 2, 0:64], v[:, P:QK_DIM]).then_inc(vec_loaded, 16)
        vec_loaded = sem("vec_loaded")
        NV_DMA = 13

        def pe_start(pe):
            pe.wait_ge(const_loaded, 16 * NCONST)
            nc.tensor.transpose(bk[4][:, 0:CONV * 24], vrow["conv"][0:CONV * 24, :], eye[0:CONV * 24, 0:CONV * 24]
                                ).then_inc(vec_turned, 1)
            pe.wait_ge(vec_loaded, 16 * NV_DMA)
            nc.tensor.transpose(bk[5][:, 0:NVEC], vrow["vec"][0:NVEC, :], eye[0:NVEC, 0:NVEC]).then_inc(vec_turned, 1)
            for st in range(ST):
                pe.wait_ge(x_loaded, 16 * (st + 1) if st == 3 else 64)
                for hf in range(2):
                    if st >= 2:
                        pe.wait_ge(act_ready, 2 * (st - 2) + hf + 1)
                    for k in range(4):
                        kt = 4 * hf + k
                        mm = nc.tensor.transpose(bk[2 * (st % 2) + hf][:, k * P:k * P + P],
                                                 X[:, st, kt * P:kt * P + P], eye[:, :])
                    mm.then_inc(xt_ready, 1)

        def dve_start(dve):
            dve.wait_ge(vec_turned, 1)
            nc.vector.tensor_copy(convw[:, :], bk[4][:, 0:CONV * 24]).then_inc(vec_ready, 1)
            dve.wait_ge(vec_turned, 2)
            nc.vector.tensor_copy(cols[:, :], bk[5][:, 0:NVEC]).then_inc(vec_ready, 1)
            for st in range(ST):
                dve_turned(dve, 0, st)
            for b in range(2):
                split_lo(dve, 0, b)
            dve.wait_ge(G["w_hi"], 1)
            nc.vector.tensor_tensor(gw_lo, gw_raw, gw_hi, ALU.subtract).then_inc(G["w_ready"], 1)
            dve.wait_ge(vec_ready, 2)

        def act_begin(act):
            act_turned(act, 0)
            for b in range(2):
                split_hi(act, 0, b)
            act.wait_ge(const_loaded, 16 * NCONST)
            nc.scalar.activation(gw_hi, gw_raw, ACT.Copy).then_inc(G["w_hi"], 1)
            act.wait_ge(memset_done, 3)
            act.wait_ge(vec_ready, 2)
            r = VEC["c"][0]
            nc.scalar.activation(csil[:, :], cols[:, r:r + 16], ACT.Silu).then_inc(vec_ready, 1)

        def pe_a_in(pe):
            pe.wait_ge(act_ready, 8)
            for b in range(2):
                pe_feature_slab(pe, "a_in", 0, b)
            with pe.Fori(1, 8) as k2:
                for b in range(2):
                    pe_feature_slab(pe, "a_in", k2, b)

        def act_a_in(act):
            def conv_pair(k2, b):
                for j in range(2):
                    wait_tile(act, "a_in", k2, b, j)
                    if not isinstance(k2, int):
                        act.wait_ge(conv_step, k2 * 20 + (10 * b - 10))
                    nc.scalar.activation(CB["cbuf"][:, 2 * b + j, 2:2 + S], bk[2 * b + j][:, :], ACT.Copy).then_inc(acc_free, 1)
                split_hi(act, next_pair("a_in", k2), b)
                for j in range(2):
                    act.wait_ge(conv_step, k2 * 20 + (10 * b + 9 + j))
                    nc.scalar.activation(a_qkvT[:, bass.ds(k2 * 4 + (2 * b + j), 1), :].squeeze(1), CB["cacc"][:, 2 * b + j, :],
                                         ACT.Silu).then_inc(conv_silu, 1)
            for b in range(2):
                conv_pair(0, b)
            with act.Fori(1, 6) as k2:
                for b in range(2):
                    conv_pair(k2, b)
            with act.Fori(6, 8) as k2:
                for b in range(2):
                    for j in range(2):
                        wait_tile(act, "a_in", k2, b, j)
                        nc.scalar.activation(a_zT[:, bass.ds(k2 * 4 + (2 * b + j - 24), 1), :].squeeze(1), bk[2 * b + j][:, :],
                                             ACT.Silu).then_inc(acc_free, 1)
                    split_hi(act, next_pair("a_in", k2), b)

        def dve_a_in(dve):
            def conv_pair(k2, b):
                for k in range(CONV):
                    for j in range(2):
                        src = CB["cbuf"][:, 2 * b + j, k:k + S]
                        acc = CB["cacc"][:, 2 * b + j, :]
                        wk = convw[:, bass.ds(k2 * 4 + (k * 24 + 2 * b + j), 1)]
                        if k == 0:
                            dve.wait_ge(acc_free, k2 * 4 + (2 * b + j + 1))
                            if not isinstance(k2, int):
                                dve.wait_ge(conv_silu, k2 * 4 + (2 * b + j - 3))
                            nc.vector.tensor_scalar(acc, src, wk, None, ALU.mult).then_inc(conv_step, 1)
                        else:
                            dve.wait_ge(conv_step, k2 * 20 + (10 * b + 2 * k + j - 1))
                            nc.vector.scalar_tensor_tensor(out=acc, in0=src, scalar=wk, in1=acc, op0=ALU.mult,
                                                           op1=ALU.add).then_inc(conv_step, 1)
                split_lo(dve, next_pair("a_in", k2), b)
            for b in range(2):
                conv_pair(0, b)
            with dve.Fori(1, 6) as k2:
                for b in range(2):
                    conv_pair(k2, b)
            with dve.Fori(6, 8) as k2:
                for b in range(2):
                    split_lo(dve, next_pair("a_in", k2), b)

        def pe_a_gates(pe):
            pe.wait_ge(G["w_ready"], 1)
            for st in range(ST):
                for kt in range(KT):
                    tok = slice(st * P, st * P + P)
                    mm = mm3(bk[4][:, st * 32:st * 32 + 32], act_hi[:, kt, tok], act_lo[:, kt, tok],
                             gw_hi[:, kt, :], gw_lo[:, kt, :], kt == 0, kt == KT - 1)
            mm.then_inc(G["gate_mm"], 1)
            pe.wait_ge(G["g"], 1)
            gates = bk[5][:, 0:192].rearrange("p (k c n) -> p k c n", k=3, c=ST)
            for d in range(2):
                dd = slice(8 * d, 8 * d + 8)
                nc.tensor.matmul(gates[:, 0, :, dd], A["tri"][:, d, :], A["g"][:, :, dd], start=True, stop=True, skip_group_check=True)
                nc.tensor.matmul(gates[:, 1, :, dd], A["tri"][:, 2 + d, :], A["g"][:, :, dd], start=True, stop=True, skip_group_check=True)
            nc.tensor.matmul(gates[:, 2, :, :], ones[:, :], A["g"], start=True, stop=True, skip_group_check=True
                             ).then_inc(G["cum_mm"], 1)

        def act_a_gates(act):
            logits = bk[4][:, 0:128].rearrange("p (c n) -> p c n", c=ST)
            act.wait_ge(G["gate_mm"], 1)
            nc.scalar.activation(A["beta"], logits[:, :, 0:16], ACT.Exp, scale=-1.0).then_inc(G["gate_exp"], 1)
            act.wait_ge(G["w_loaded"], 32)
            nc.scalar.activation(gwv["ea"], gwv["alog"], ACT.Exp).then_inc(G["gate_exp"], 1)
            act.wait_ge(G["logit"], 1)
            nc.scalar.activation(A["t2"], A["t1"], ACT.Abs).then_inc(G["absd"], 1)
            act.wait_ge(G["absd"], 1)
            nc.scalar.activation(A["t2"], A["t2"], ACT.Exp, scale=-1.0).then_inc(G["expd"], 1)
            act.wait_ge(G["expd"], 1)
            nc.scalar.activation(A["t2"], A["t2"], ACT.Ln, bias=1.0).then_inc(G["softplus1"], 1)
            gates = bk[5][:, 0:192].rearrange("p (k c n) -> p k c n", k=3, c=ST)
            act.wait_ge(G["cum_mm"], 1)
            for k, n in enumerate(("bexp", "kdec", "glast")):
                nc.scalar.activation(A[n], gates[:, k, :, :], ACT.Exp).then_inc(G["cum_exp"], 1)

        def dve_a_gates(dve):
            logits = bk[4][:, 0:128].rearrange("p (c n) -> p c n", c=ST)
            dve.wait_ge(G["gate_exp"], 1)
            dve.wait_ge(G["w_loaded"], 32)
            nc.vector.tensor_tensor(A["t1"], logits[:, :, 16:32], gwv["dt"].unsqueeze(1).broadcast_to([P, ST, 16]),
                                    ALU.add).then_inc(G["logit"], 1)
            dve.wait_ge(G["gate_exp"], 2)
            nc.vector.tensor_scalar(A["beta"], A["beta"], 1.0, None, ALU.add).then_inc(G["beta1"], 1)
            dve.wait_ge(G["beta1"], 1)
            nc.vector.reciprocal(A["beta"], A["beta"]).then_inc(G["beta2"], 1)
            dve.wait_ge(G["softplus1"], 1)
            nc.vector.scalar_tensor_tensor(out=A["t1"], in0=A["t1"], scalar=0.0, in1=A["t2"], op0=ALU.max,
                                           op1=ALU.add).then_inc(G["softplus"], 1)
            dve.wait_ge(G["softplus"], 1)
            nc.vector.scalar_tensor_tensor(out=A["g"], in0=A["t1"], scalar=-1.0,
                                           in1=gwv["ea"].unsqueeze(1).broadcast_to([P, ST, 16]), op0=ALU.mult,
                                           op1=ALU.mult).then_inc(G["g"], 1)
            dve.wait_ge(G["cum_exp"], 3)
            dve.wait_ge(G["beta2"], 1)
            nc.vector.tensor_tensor(A["bexp"], A["bexp"], A["beta"], ALU.mult).then_inc(G["bexp"], 1)

        def chunk_of(cc, d):
            return cc if d == 0 else ST - 1 - cc

        def pe_a_head(pe, h):
            for i, bank in ((0, 0), (1, 2)):
                pe.wait_ge(G["l2_sq"], h * 2 + (i + 1))
                nc.tensor.matmul(bk[bank][:, :], ones[:, :], A["sq"][:, i, :], start=True, stop=True).then_inc(G["l2_sum"], 1)
            pe.wait_ge(G["qkn"], h * 2 + 1)
            for c in range(ST):
                mm = nc.tensor.transpose(bk[1][:, c * P:c * P + P], A["kn"][:, c * P:c * P + P], eye[:, :])
            mm.then_inc(G["turned"], 1)
            pe.wait_ge(G["v_copied"], h + 1)
            for c in range(ST):
                mm = nc.tensor.transpose(bk[3][:, c * P:c * P + P], A["vst"][:, c * P:c * P + P], eye[:, :])
            mm.then_inc(G["turned"], 1)
            for bank, r in ((4, "kn"), (5, "qn")):
                if r == "qn":
                    pe.wait_ge(G["qkn"], h * 2 + 2)
                for c in range(ST):
                    cs = slice(c * P, c * P + P)
                    mm = nc.tensor.matmul(bk[bank][:, cs], A["kn"][:, cs], A[r][:, cs], start=True, stop=True, skip_group_check=True)
                mm.then_inc(G["kk"], 1)
            pe.wait_ge(G["k_tok"], h + 1)
            pe.wait_ge(G["vb"], h * 2 + 2)
            pe.wait_ge(G["o_out"], h + 1)
            for d in range(2):
                pe.wait_ge(G["gl"], h * 4 + (2 * d + 2))
                for bank, lhs, rhs in ((2 * d, A["tri"][:, 2 + d, :], "GL"), (2 * d + 1, A["tri"][:, d, :], "GG"),
                                       (6 + d, ones[:, :], "GL")):
                    nc.tensor.matmul(bk[bank][:, :], lhs, A[f"{rhs}{d}"], start=True, stop=True).then_inc(G["decay_mm"], 1)
            for l in range(LEVELS):
                for d in range(2):
                    if l == 0:
                        pe.wait_ge(G["a"], h * 2 + (d + 1))
                    else:
                        pe.wait_ge(G["y"], h * 14 + (2 * (l - 1) + d + 1))
                    for c in range(ST):
                        cs = slice(c * P, c * P + P)
                        if l == 0:
                            mm = nc.tensor.transpose(bk[2 * d][:, cs], A[f"A{d}"][:, c, :], eye[:, :])
                        else:
                            mm = nc.tensor.matmul(bk[2 * d][:, cs], A[f"A{d}"][:, c, :], A[f"Y{d}"][:, c, :],
                                                  start=True, stop=True, skip_group_check=True)
                    mm.then_inc(G["p1"], 1)
                if l > 0:
                    for d in range(2):
                        pe.wait_ge(G["t2"], h * 12 + (2 * (l - 1) + d + 1))
                        pe.wait_ge(G["x"], h * 12 + (2 * (l - 1) + d + 1))
                        for c in range(ST):
                            mm = nc.tensor.matmul(bk[2 * d + 1][:, c * P:c * P + P], A[f"X{d}"][:, c, :], A[f"GG{d}"][:, c, :],
                                                  start=True, stop=True, skip_group_check=True)
                        mm.then_inc(G["p2"], 1)
                if l < LEVELS - 1:
                    for d in range(2):
                        pe.wait_ge(G["y"], h * 14 + (2 * l + d + 1))
                        for c in range(ST):
                            mm = nc.tensor.transpose(bk[2 * d + 1][:, c * P:c * P + P], A[f"Y{d}"][:, c, :], eye[:, :])
                        mm.then_inc(G["turned_y"], 1)
            pe.wait_ge(G["kx"], h * 4 + 4)
            for d in range(2):
                pe.wait_ge(G["y"], h * 14 + (2 * (LEVELS - 1) + d + 1))
                for c in range(ST):
                    mm = nc.tensor.matmul(bk[2 * d][:, c * P:c * P + P], A[f"kbe{d}"][:, c, :], A[f"Y{d}"][:, c, :],
                                          start=True, stop=True, skip_group_check=True)
                mm.then_inc(G["w_mm"], 1)
            pe.wait_ge(G["pt"], h * 2 + 2)
            pe.wait_ge(G["qd"], h * 2 + 2)
            for cc in range(ST):
                for d in range(2):
                    c = chunk_of(cc, d)
                    if cc == 0:
                        pe.wait_ge(G["w"], h * 2 + (d + 1))
                    mm = nc.tensor.matmul(bk[2 * d][:, 0:P], A[f"Y{d}"][:, c, :], A[f"vb{d}"][:, c, :], start=True,
                                          stop=cc == 0, skip_group_check=True)
                    if cc > 0:
                        pe.wait_ge(G["s"], h * 6 + (2 * (cc - 1) + d + 1))
                        mm = nc.tensor.matmul(bk[2 * d][:, 0:P], A[f"GL{d}"][:, c, :], A[f"S{d}"], start=False,
                                              stop=True, skip_group_check=True)
                    mm.then_inc(G["pv"], 1)
                for d in range(2):
                    c = chunk_of(cc, d)
                    cs = slice(c * P, c * P + P)
                    if cc > 0:
                        nc.tensor.matmul(bk[6][:, cs], A[f"S{d}"], A[f"qd{d}"][:, c, :], start=False, stop=False,
                                         skip_group_check=True)
                    pe.wait_ge(G["vn"], h * 8 + (2 * cc + d + 1))
                    mm = nc.tensor.matmul(bk[6][:, cs], A[f"vn{d}"], A[f"PT{d}"][:, c, :], start=cc == 0 and d == 0,
                                          stop=cc == 3, skip_group_check=True)
                    if cc < 3:
                        mm = nc.tensor.matmul(bk[2 * d + 1][:, 0:P], A[f"kd{d}"][:, c, :], A[f"vn{d}"], start=True,
                                              stop=True, skip_group_check=True)
                        mm.then_inc(G["ps"], 1)
                    elif d == 1:
                        mm.then_inc(G["o_done"], 1)
            pe.wait_ge(G["o_sq"], h + 1)
            nc.tensor.matmul(bk[7][:, :], ones[:, :], A["sq"][:, 0, :], start=True, stop=True).then_inc(G["o_sum"], 1)

        def head_tile(t, h, off=0):
            return t[:, bass.ds(h + off, 1), :].squeeze(1)

        def act_a_head(act, h):
            act.wait_ge(G["o_out"], h + 1)
            for i, off in ((0, 8), (1, 0)):
                nc.scalar.activation(A["sq"][:, i, :], head_tile(a_qkvT, h, off), ACT.Square).then_inc(G["l2_sq"], 1)
            for i, bank in ((0, 0), (1, 2)):
                act.wait_ge(G["l2_sum"], h * 2 + (i + 1))
                nc.scalar.activation(A["rs"][:, i, :], bk[bank][:, :], ACT.Ln, bias=1e-6).then_inc(G["l2_ln"], 1)
            for i in range(2):
                act.wait_ge(G["l2_ln"], h * 2 + (i + 1))
                nc.scalar.activation(A["rs"][:, i, :], A["rs"][:, i, :], ACT.Exp, scale=-0.5).then_inc(G["l2_rs"], 1)
            act.wait_ge(G["turned"], h * 2 + 1)
            nc.scalar.activation(A["ktok"], chunks(bk[1]), ACT.Copy).then_inc(G["k_tok"], 1)
            for d in range(2):
                for i, (bank, n) in enumerate(((2 * d, "PT"), (2 * d + 1, "A"), (6 + d, "qd"))):
                    act.wait_ge(G["decay_mm"], h * 6 + (3 * d + i + 1))
                    nc.scalar.activation(A[f"{n}{d}"], chunks(bk[bank]), ACT.Exp).then_inc(G["decay_exp"], 1)
            for l in range(LEVELS - 1):
                for d in range(2):
                    act.wait_ge(G["turned_y"], h * 12 + (2 * l + d + 1))
                    nc.scalar.activation(A[f"X{d}"], chunks(bk[2 * d + 1]), ACT.Copy).then_inc(G["x"], 1)
            for d in range(2):
                act.wait_ge(G["w_mm"], h * 2 + (d + 1))
                nc.scalar.activation(A[f"GL{d}"], chunks(bk[2 * d]), ACT.Copy, scale=-1.0).then_inc(G["w"], 1)
            act.wait_ge(G["o_done"], h + 2)
            nc.scalar.activation(A["sq"][:, 0, :], bk[6][:, :], ACT.Square).then_inc(G["o_sq"], 1)
            act.wait_ge(G["o_sum"], h + 1)
            nc.scalar.activation(A["rs"][:, 0, :], bk[7][:, :], ACT.Ln, bias=RMS_EPS, scale=1.0 / P).then_inc(G["o_ln"], 1)
            act.wait_ge(G["o_ln"], h + 1)
            nc.scalar.activation(A["rs"][:, 0, :], A["rs"][:, 0, :], ACT.Exp, scale=-0.5).then_inc(G["o_rs"], 1)
            act.wait_ge(G["of"], h + 1)
            nc.scalar.activation(head_tile(act_hi, h), A["sq"][:, 1, :], ACT.Copy).then_inc(G["o_hi"], 1)

        def dve_a_head(dve, h):
            dve.wait_ge(G["l2_rs"], h * 2 + 1)
            nc.vector.tensor_tensor(A["kn"], head_tile(a_qkvT, h, 8), A["rs"][:, 0, :], ALU.mult).then_inc(G["qkn"], 1)
            dve.wait_ge(G["l2_rs"], h * 2 + 2)
            nc.vector.scalar_tensor_tensor(out=A["qn"], in0=head_tile(a_qkvT, h), scalar=float(P) ** -0.5,
                                           in1=A["rs"][:, 1, :], op0=ALU.mult, op1=ALU.mult).then_inc(G["qkn"], 1)
            dve.wait_ge(G["turned"], h * 2 + 2)
            for d in range(2):
                nc.vector.tensor_tensor(A[f"vb{d}"], chunks(bk[3]), bc_tok(A["beta"][:, :, bass.ds(h + 8 * d, 1)]),
                                        ALU.mult).then_inc(G["vb"], 1)
            dve.wait_ge(G["kk"], h * 2 + 2)
            for d in range(2):
                dve.wait_ge(G["decay_exp"], h * 6 + (3 * d + 2))
                nc.vector.tensor_tensor(A[f"A{d}"], A[f"A{d}"], chunks(bk[4]), ALU.mult).then_inc(G["ed"], 1)
                dve.wait_ge(G["ed"], h * 2 + (d + 1))
                nc.vector.tensor_tensor(A[f"A{d}"], A[f"A{d}"], bc_tok(A["beta"][:, :, bass.ds(h + 8 * d, 1)]),
                                        ALU.mult).then_inc(G["a"], 1)
            for d in range(2):
                dve.wait_ge(G["pt_mask"], h * 2 + (d + 1))
                nc.vector.tensor_tensor(A[f"PT{d}"], A[f"PT{d}"], chunks(bk[5]), ALU.mult).then_inc(G["pt"], 1)
                dve.wait_ge(G["decay_exp"], h * 6 + (3 * d + 3))
                nc.vector.tensor_tensor(A[f"qd{d}"], A[f"qd{d}"], A["qn"].rearrange("p (c s) -> p c s", c=ST),
                                        ALU.mult).then_inc(G["qd"], 1)
            for l in range(LEVELS):
                for d in range(2):
                    dve.wait_ge(G["p1"], h * 14 + (2 * l + d + 1))
                    dst = A[f"Y{d}"] if l == 0 else A[f"GG{d}"]
                    nc.vector.tensor_tensor(dst, chunks(bk[2 * d]), bc_mat(A["negpair"][:, LEVELS * d + l, :]),
                                            ALU.mult).then_inc(G["y0"] if l == 0 else G["t2"], 1)
                for d in range(2):
                    if l == 0:
                        dve.wait_ge(G["y0"], h * 2 + (d + 1))
                        nc.vector.tensor_tensor(A[f"Y{d}"], A[f"Y{d}"], bc_mat(eye[:, :]), ALU.add).then_inc(G["y"], 1)
                    else:
                        dve.wait_ge(G["p2"], h * 12 + (2 * (l - 1) + d + 1))
                        nc.vector.tensor_tensor(A[f"Y{d}"], A[f"Y{d}"], chunks(bk[2 * d + 1]), ALU.add).then_inc(G["y"], 1)
            for cc in range(ST):
                for d in range(2):
                    dve.wait_ge(G["pv"], h * 8 + (2 * cc + d + 1))
                    nc.vector.tensor_copy(A[f"vn{d}"], bk[2 * d][:, 0:P]).then_inc(G["vn"], 1)
                if cc == 3:
                    break
                for d in range(2):
                    dve.wait_ge(G["ps"], h * 6 + (2 * cc + d + 1))
                    if cc == 0:
                        nc.vector.tensor_copy(A[f"S{d}"], bk[2 * d + 1][:, 0:P]).then_inc(G["s"], 1)
                    else:
                        dve.wait_ge(G["s"], h * 6 + (2 * (cc - 1) + d + 1))
                        nc.vector.scalar_tensor_tensor(out=A[f"S{d}"], in0=A[f"S{d}"],
                                                       scalar=A["glast"][:, chunk_of(cc, d), bass.ds(h + 8 * d, 1)],
                                                       in1=bk[2 * d + 1][:, 0:P], op0=ALU.mult, op1=ALU.add
                                                       ).then_inc(G["s"], 1)
            dve.wait_ge(G["o_rs"], h + 1)
            nc.vector.tensor_tensor(A["sq"][:, 1, :], bk[6][:, :], A["rs"][:, 0, :], ALU.mult).then_inc(G["of1"], 1)
            dve.wait_ge(G["of1"], h + 1)
            nc.vector.scalar_tensor_tensor(out=A["sq"][:, 1, :], in0=A["sq"][:, 1, :], scalar=col("a_norm_g"),
                                           in1=head_tile(a_zT, h), op0=ALU.mult, op1=ALU.mult).then_inc(G["of"], 1)
            dve.wait_ge(G["o_hi"], h + 1)
            nc.vector.tensor_tensor(head_tile(act_lo, h), A["sq"][:, 1, :], head_tile(act_hi, h), ALU.subtract
                                    ).then_inc(G["o_out"], 1)

        def pool_a_head(pool, h):
            pool.wait_ge(G["o_done"], h + 1)
            gap(pool)
            nc.gpsimd.tensor_copy(A["vst"], head_tile(a_qkvT, h, 16)).then_inc(G["v_copied"], 1)
            for d in range(2):
                for n, m in (("GL", d), ("GG", 2 + d)):
                    nc.gpsimd.tensor_tensor(A[f"{n}{d}"], bc_mat(A["tri"][:, m, :]), bc_tok(A["g"][:, :, bass.ds(h + 8 * d, 1)]),
                                            ALU.mult).then_inc(G["gl"], 1)
            pool.wait_ge(G["k_tok"], h + 1)
            gap(pool)
            for n, s in (("kbe", "bexp"), ("kd", "kdec")):
                for d in range(2):
                    nc.gpsimd.tensor_tensor(A[f"{n}{d}"], A["ktok"], bc_tok(A[s][:, :, bass.ds(h + 8 * d, 1)]),
                                            ALU.mult).then_inc(G["kx"], 1)
            for d in range(2):
                pool.wait_ge(G["decay_exp"], h * 6 + (3 * d + 1))
                nc.gpsimd.tensor_tensor(A[f"PT{d}"], A[f"PT{d}"], bc_mat(A["tri"][:, d, :]), ALU.mult).then_inc(G["pt_mask"], 1)

        def gap(eng):
            eng.wait_ge(memset_done, 1)

        sq_ready = sem("sq_ready")
        hid_hi_ready = sem("hid_hi_ready")
        hid_ready = sem("hid_ready")
        wmod_loaded = sem("wmod_loaded")
        mod_mm = sem("mod_mm")
        mod_read = sem("mod_read")
        gate_row_mm = sem("gate_row_mm")

        def pe_up(pe, L, e):
            pe.wait_ge(act_ready, 8 * (e + 1))
            with pe.Fori(0, 8) as k2:
                for b in range(2):
                    pe_feature_slab(pe, f"up{L}", k2, b)

        def act_up(act, L):
            with act.Fori(0, 8) as k2:
                for b in range(2):
                    for j in range(2):
                        wait_tile(act, f"up{L}", k2, b, j)
                        act.wait_ge(hid_ready, k2 * 4 + (32 * L + 2 * b + j + 1))
                        nc.scalar.activation(hsq[:, 2 * b + j, :], bk[2 * b + j][:, :], ACT.Relu).then_inc(acc_free, 1)
                    for j in range(2):
                        act.wait_ge(sq_ready, k2 * 4 + (32 * L + 2 * b + j + 1))
                        gap(act)
                        nc.scalar.activation(head_tile(hid_hi, k2 * 4, 2 * b + j), hsq[:, 2 * b + j, :], ACT.Copy
                                             ).then_inc(hid_hi_ready, 1)
                    split_hi(act, next_pair(f"up{L}", k2), b)

        def dve_up(dve, L):
            with dve.Fori(0, 8) as k2:
                for b in range(2):
                    for j in range(2):
                        dve.wait_ge(acc_free, k2 * 4 + (2 * FS[f"up{L}"] + 2 * b + j + 1))
                        nc.vector.tensor_tensor(hsq[:, 2 * b + j, :], hsq[:, 2 * b + j, :], hsq[:, 2 * b + j, :],
                                                ALU.mult).then_inc(sq_ready, 1)
                    for j in range(2):
                        dve.wait_ge(hid_hi_ready, k2 * 4 + (32 * L + 2 * b + j + 1))
                        nc.vector.tensor_tensor(head_tile(hid_lo, k2 * 4, 2 * b + j), hsq[:, 2 * b + j, :],
                                                head_tile(hid_hi, k2 * 4, 2 * b + j), ALU.subtract).then_inc(hid_ready, 1)
                    split_lo(dve, next_pair(f"up{L}", k2), b)

        def pe_down(pe, L):
            pe.wait_ge(hid_ready, 4 + 32 * (L + 1))
            pe_token_layer(pe, f"down{L}", hid_hi, hid_lo)

        def load_lnrow(pool, e, g, b):
            for i, v in enumerate((g, b)):
                pool.dma_start(lnrow[:, i, :], v.partition_broadcast(P)).then_inc(lnrow_loaded, 16)

        def load_wmod(pool, third):
            pool.dma_start(wmod, a["w_mod_2"][0, :, third * D:third * D + D].rearrange("(k p) n -> p k n", p=P)
                           ).then_inc(wmod_loaded, 16)

        def pe_mod(pe, third, name):
            pe.wait_ge(sum_added, 4 * TH[name] + 5)
            pe.wait_ge(wmod_loaded, 16 * (third + 1))
            rhs = csil[:, :].rearrange("p (w k) -> p k w", w=2)
            pe.wait_ge(vec_ready, 3)
            for n in range(8):
                for kt in range(KT):
                    mm = nc.tensor.matmul(bk[4][:, 2 * n:2 * n + 2], wmod[:, kt, n * P:n * P + P], rhs[:, kt, :],
                                          start=kt == 0, stop=kt == KT - 1, skip_group_check=True)
            mm.then_inc(mod_mm, 1)

        def dve_mod(dve, third):
            dve.wait_ge(mod_mm, third + 1)
            r = VEC["b_mod"][0] + 8 * third
            nc.vector.tensor_tensor(modc[:, 8 * third:8 * third + 8, :], bk[4][:, 0:16].rearrange("p (n w) -> p n w", w=2),
                                    cols[:, r:r + 8].unsqueeze(2).broadcast_to([P, 8, 2]), ALU.add).then_inc(mod_read, 1)

        b_qT = arena[:, 0:2048].rearrange("p (n s) -> p n s", n=BH)
        b_kT = arena[:, 2048:4096].rearrange("p (n s) -> p n s", n=BH)
        b_v = arena[:, 4096:8192].rearrange("p (c n) -> p c n", c=ST)
        b_rT = arena[:, 8192:12288].rearrange("p (n s) -> p n s", n=2 * BH)
        b_la = arena[:, 12288:16384].rearrange("p (n k) -> p n k", n=2 * ST)
        NL = LEVELS + 2
        BB = carve(work, [("cum", 2 * NL, P), ("masks", 512), ("E0", NL, S), ("E1", NL, S), ("las", ST, P),
                          ("vs", ST, BDV), ("kh", S), ("ST0", ST, P), ("ST1", ST, P), ("kdt0", ST, P), ("kdt1", ST, P),
                          ("S0", BDV), ("S1", BDV), ("o", 2, S), ("rs", S), ("gl", 8)])
        b_masks = BB["masks"].bitcast(U8).rearrange("p (d l s) -> p d l s", d=2, l=LEVELS + 1)
        b_masks_f = BB["E1"].rearrange("p l s -> p (l s)")[:, 0:2 * (LEVELS + 1) * P]
        BG = carve(work, [("glT", S), ("w2", 2, S), ("t", 2, S)], start=2816)
        B = {n: sem("b_" + n) for n in (
            "w_loaded gate_loaded masks_loaded masks_ready gate_set w_hi w_ready gl_mm gl la_mm absd expd ln la kv las e_mm exp gl_col zk zq sc st kd_turned "
            "kdt u s o_done o_sq o_sum o_ln o_rs of1 of o_hi o_out").split()}

        def pool_b_load(pool):
            pool.wait_ge(x_ready, 8)
            pool.wait_ge(slab_used, PH["b_qk"][0])
            nc.gpsimd.memset(BG["glT"][0:33, :], 1.0).then_inc(B["gate_set"], 1)
            nc.gpsimd.memset(BG["w2"][0:33, :, :], 0.0).then_inc(B["gate_set"], 1)
            pool.wait_ge(B["gate_set"], 2)
            pool.dma_start(gw_raw, a["b_w_in"][0, :, 3072:3104].rearrange("(k p) n -> p k n", p=P)).then_inc(B["w_loaded"], 16)
            for n in range(2):
                pool.dma_start(BG["w2"][RANK * n:RANK * n + RANK, n, :], a["b_gate_w2"][0, n]).then_inc(B["gate_loaded"], 16)
            pool.dma_start(BG["w2"][32:33, :, :], a["b_gate_b"]).then_inc(B["gate_loaded"], 16)
            pool.dma_start(BB["cum"], a["k_cum"].rearrange("p (m s) -> p m s", m=2 * NL)).then_inc(B["gate_loaded"], 16)
            pool.dma_start(b_masks_f, a["k_masks"]).then_inc(B["masks_loaded"], 16)

        def pe_b_in(pe):
            pe.wait_ge(act_ready, 24)
            for k2 in range(2):
                for b in range(2):
                    pe_feature_slab(pe, "b_qk", k2, b)
            pe.wait_ge(acc_free, 2 * (FS["b_qk"] + 4))
            pe_token_layer(pe, "b_v", act_hi, act_lo)
            pe.wait_ge(sum_added, 4 * TH["b_v"] + 4)
            for k2 in range(2):
                for b in range(2):
                    pe_feature_slab(pe, "b_r", k2, b)
            pe.wait_ge(sum_added, 4 * TH["b_v"] + 8)
            pe.wait_ge(B["w_ready"], 1)
            for kt in range(KT):
                mm = mm3(bk[4][0:32, :], gw_hi[:, kt, :], gw_lo[:, kt, :], act_hi[:, kt, :], act_lo[:, kt, :],
                         kt == 0, kt == KT - 1)
            mm.then_inc(B["gl_mm"], 1)
            pe.wait_ge(B["gl"], 1)
            pe.wait_ge(B["gate_loaded"], 16 * 4)
            for n in range(2):
                for st in range(ST):
                    t = ST * n + st
                    if t >= 2:
                        pe.wait_ge(B["la"], t - 1)
                    nc.tensor.matmul(bk[6 + t % 2][:, :], BG["glT"][0:33, st * P:st * P + P], BG["w2"][0:33, n, :],
                                     start=True, stop=True).then_inc(B["la_mm"], 1)

        def act_b_in(act):
            for k2 in range(2):
                for b in range(2):
                    for j in range(2):
                        wait_tile(act, "b_qk", k2, b, j)
                        dst = (b_qT, b_kT)[k2][:, 2 * b + j, :]
                        nc.scalar.activation(dst, bk[2 * b + j][:, :], ACT.Copy, scale=float(P) ** -0.5 if k2 == 0 else 1.0
                                             ).then_inc(acc_free, 1)
                    split_hi(act, next_pair("b_qk", k2), b)
            for half in range(2):
                for b in range(2):
                    split_hi(act, next_pair("b_v", half), b)
                for st in range(ST):
                    wait_sum(act, "b_v", half, st)
                    nc.scalar.activation(b_v[:, st, half * 512:half * 512 + 512], bk[4 * half + st][:, :], ACT.Copy
                                         ).then_inc(sum_added, 1)
            for k2 in range(2):
                for b in range(2):
                    for j in range(2):
                        wait_tile(act, "b_r", k2, b, j)
                        nc.scalar.activation(b_rT[:, 4 * k2 + 2 * b + j, :], bk[2 * b + j][:, :], ACT.Silu).then_inc(acc_free, 1)
                    split_hi(act, next_pair("b_r", k2), b)
            act.wait_ge(B["gl_mm"], 1)
            act.wait_ge(B["gate_set"], 2)
            nc.scalar.activation(BG["glT"][0:32, :], bk[4][0:32, :], ACT.Copy).then_inc(B["gl"], 1)
            for t in range(2 * ST):
                tb = BG["t"][:, t % 2, :]
                act.wait_ge(B["la_mm"], t + 1)
                if t >= 2:
                    act.wait_ge(B["la"], t - 1)
                nc.scalar.activation(tb, bk[6 + t % 2][:, :], ACT.Abs).then_inc(B["absd"], 1)
                act.wait_ge(B["absd"], t + 1)
                nc.scalar.activation(tb, tb, ACT.Exp, scale=-1.0).then_inc(B["expd"], 1)
                act.wait_ge(B["expd"], t + 1)
                nc.scalar.activation(tb, tb, ACT.Ln, bias=1.0).then_inc(B["ln"], 1)
            act.wait_ge(B["masks_ready"], 1)

        def act_b_gate_weights(act):
            act.wait_ge(B["w_loaded"], 16)
            nc.scalar.activation(gw_hi, gw_raw, ACT.Copy).then_inc(B["w_hi"], 1)

        def dve_b_in(dve):
            dve.wait_ge(B["w_hi"], 1)
            nc.vector.tensor_tensor(gw_lo, gw_raw, gw_hi, ALU.subtract).then_inc(B["w_ready"], 1)
            with dve.Fori(0, 6) as k2:
                for b in range(2):
                    split_lo(dve, next_pair("b_qk", k2), b)
            dve.wait_ge(B["masks_loaded"], 16)
            nc.vector.tensor_copy(BB["masks"].bitcast(U8), b_masks_f).then_inc(B["masks_ready"], 1)
            for t in range(2 * ST):
                dve.wait_ge(B["ln"], t + 1)
                nc.vector.scalar_tensor_tensor(out=b_la[:, t, :], in0=bk[6 + t % 2][:, :], scalar=0.0,
                                               in1=BG["t"][:, t % 2, :], op0=ALU.min, op1=ALU.subtract).then_inc(B["la"], 1)

        def halves(t, l):
            return t.rearrange("p (n t b) -> p n t b", t=2, b=1 << l)

        def pool_b_head(pool, h):
            pool.wait_ge(B["o_done"], h + 1)
            gap(pool)
            nc.gpsimd.tensor_copy(BB["kh"], head_tile(b_kT, h)).then_inc(B["kv"], 1)
            nc.gpsimd.tensor_copy(BB["vs"], b_v[:, :, bass.ds(h * BDV, BDV)]).then_inc(B["kv"], 1)
            for d in range(2):
                pool.wait_ge(B["e_mm"], h * 18 + (9 * d + 1))
                gap(pool)
                nc.gpsimd.tensor_copy(BB["las"], b_la[:, ST * d:ST * d + ST, bass.ds(h * P, P)]).then_inc(B["las"], 1)
                if d == 0:
                    pool.wait_ge(B["kv"], h * 2 + 2)
                for l in range(LEVELS):
                    pool.wait_ge(B["exp"], 3 + 18 * h + (9 * d + (4 if l < 4 else 8)))
                    e = halves(BB[f"E{d}"][:, l, :], l)[:, :, d, :]
                    nc.gpsimd.tensor_tensor(e, e, halves(BB["kh"], l)[:, :, d, :], ALU.mult).then_inc(B["zk"], 1)
                pool.wait_ge(B["exp"], 3 + 18 * h + (9 * d + 9))
                e = BB[f"E{d}"][:, LEVELS + 1, :]
                nc.gpsimd.tensor_tensor(e, e, BB["kh"], ALU.mult).then_inc(B["zk"], 1)

        def act_b_head(act, h):
            act.wait_ge(B["o_done"], h + 1)
            for d in range(2):
                E = BB[f"E{d}"]
                for i in range(9):
                    act.wait_ge(B["e_mm"], h * 18 + (9 * d + i + 2))
                    if i < 8:
                        c = i % 4
                        dst = E[:, 4 * (i // 4):4 * (i // 4) + 4, c * P:c * P + P]
                        src = chunks(bk[i % 3])
                    else:
                        dst, src = E[:, LEVELS + 1, :], bk[i % 3][:, :]
                    nc.scalar.activation(dst, src, ACT.Exp, scale=1.0 / 16.0).then_inc(B["exp"], 1)
                act.wait_ge(B["kd_turned"], h * 2 + (d + 1))
                nc.scalar.activation(BB[f"kdt{d}"], chunks(bk[3]), ACT.Copy).then_inc(B["kdt"], 1)
            act.wait_ge(B["o_done"], h + 2)
            for e in range(2):
                nc.scalar.activation(BB["o"][:, e, :], bk[6 + e][:, :], ACT.Square).then_inc(B["o_sq"], 1)
            act.wait_ge(B["o_sum"], h + 1)
            nc.scalar.activation(BB["rs"], bk[5][:, :], ACT.Ln, bias=RMS_EPS, scale=1.0 / BDV).then_inc(B["o_ln"], 1)
            act.wait_ge(B["o_ln"], h + 1)
            nc.scalar.activation(BB["rs"], BB["rs"], ACT.Exp, scale=-0.5).then_inc(B["o_rs"], 1)
            for e in range(2):
                act.wait_ge(B["of"], h * 2 + (e + 1))
                gap(act)
                nc.scalar.activation(head_tile(act_hi, h * 2, e), BB["o"][:, e, :], ACT.Copy).then_inc(B["o_hi"], 1)

        def pe_b_head(pe, h):
            for d in range(2):
                E = BB[f"E{d}"]
                pe.wait_ge(B["las"], h * 2 + (d + 1))
                for i in range(9):
                    pe.wait_ge(B["exp"], h * 18 + (9 * d + i + 1))
                    if i < 8:
                        m0 = NL * d + 4 * (i // 4)
                        mm = nc.tensor.matmul(chunks(bk[i % 3]), BB["las"][:, i % 4, :], BB["cum"][:, m0:m0 + 4, :],
                                              start=True, stop=True)
                    else:
                        for c in range(ST):
                            mm = nc.tensor.matmul(bk[i % 3][:, c * P:c * P + P], BB["las"][:, c, :],
                                                  BB["cum"][:, NL * d + NL - 1, :], start=True, stop=True, skip_group_check=True)
                    mm.then_inc(B["e_mm"], 1)
                if d == 0:
                    pe.wait_ge(B["kv"], h * 2 + 2)
                for i in range(8):
                    pe.wait_ge(B["st"], h * 16 + (8 * d + i + 1))
                    if i > 0:
                        pe.wait_ge(B["zk"], h * 16 + (8 * d + i))
                        pe.wait_ge(B["zq"], h * 16 + (8 * d + i))
                    for c in range(ST):
                        cs = slice(c * P, c * P + P)
                        if i == 0:
                            l_, r_ = BB["kh"][:, cs], b_qT[:, bass.ds(h, 1), cs].squeeze(1)
                        else:
                            l_ = r_ = E[:, i - 1, cs]
                        mm = nc.tensor.matmul(bk[4 + i % 2][:, cs], l_, r_, start=True, stop=True, skip_group_check=True)
                    mm.then_inc(B["sc"], 1)
                pe.wait_ge(B["zk"], h * 16 + (8 * d + 8))
                if d == 0:
                    pe.wait_ge(B["o_out"], h * 2 + 2)
                else:
                    pe.wait_ge(B["kdt"], h * 2 + 1)
                for c in range(ST):
                    mm = nc.tensor.transpose(bk[3][:, c * P:c * P + P], E[:, LEVELS + 1, c * P:c * P + P], eye[:, :])
                mm.then_inc(B["kd_turned"], 1)
            pe.wait_ge(B["kdt"], h * 2 + 2)
            pe.wait_ge(B["st"], 2 + 16 * h + 16)
            pe.wait_ge(B["zq"], h * 16 + 16)
            for cc in range(ST):
                for d in range(2):
                    c = chunk_of(cc, d)
                    cs = slice(c * P, c * P + P)
                    if cc > 0:
                        pe.wait_ge(B["s"], h * 6 + (2 * (cc - 1) + d + 1))
                    for e in range(2):
                        es = slice(e * P, e * P + P)
                        if cc > 0:
                            nc.tensor.matmul(bk[6 + e][:, cs], BB[f"S{d}"][:, es], BB[f"E{d}"][:, LEVELS, cs], start=False,
                                             stop=False, skip_group_check=True)
                        mm = nc.tensor.matmul(bk[6 + e][:, cs], BB["vs"][:, c, es], BB[f"ST{d}"][:, c, :],
                                              start=cc == 0 and d == 0, stop=cc == 3, skip_group_check=True)
                    if cc < 3:
                        nc.tensor.matmul(bk[3 * (1 - d)][:, 0:BDV], BB[f"kdt{d}"][:, c, :], BB["vs"][:, c, :], start=True,
                                         stop=True, skip_group_check=True).then_inc(B["u"], 1)
            mm.then_inc(B["o_done"], 1)
            for e in range(2):
                pe.wait_ge(B["o_sq"], h * 2 + (e + 1))
                mm = nc.tensor.matmul(bk[5][:, :], ones[:, :], BB["o"][:, e, :], start=e == 0, stop=e == 1)
            mm.then_inc(B["o_sum"], 1)

        def dve_b_head(dve, h):
            for d in range(2):
                E = BB[f"E{d}"]
                for l in range(LEVELS):
                    dve.wait_ge(B["exp"], 3 + 18 * h + (9 * d + (4 if l < 4 else 8)))
                    e = halves(E[:, l, :], l)[:, :, 1 - d, :]
                    nc.vector.tensor_tensor(e, e, halves(head_tile(b_qT, h), l)[:, :, 1 - d, :], ALU.mult).then_inc(B["zq"], 1)
                nc.vector.tensor_copy(BB["gl"][:, 4 * d:4 * d + 4],
                                      E[:, LEVELS, (P - 1 if d == 0 else 0)::P]).then_inc(B["gl_col"], 1)
                dve.wait_ge(B["gl_col"], h * 2 + (d + 1))
                nc.vector.tensor_tensor(E[:, LEVELS, :], E[:, LEVELS, :], head_tile(b_qT, h), ALU.mult).then_inc(B["zq"], 1)
                for i in range(8):
                    dve.wait_ge(B["sc"], h * 16 + (8 * d + i + 1))
                    src = chunks(bk[4 + i % 2])
                    if i == 0:
                        nc.vector.tensor_tensor(BB[f"ST{d}"], src, bc_mat(eye[:, :]), ALU.mult).then_inc(B["st"], 1)
                    else:
                        dve.wait_ge(B["st"], 2 + 16 * h + (8 * d + i))
                        nc.vector.memset(pause[:, i:i + 1], 0.0)
                        nc.vector.copy_predicated(BB[f"ST{d}"], bc_mat(b_masks[:, d, i - 1, :]), src).then_inc(B["st"], 1)
            for cc in range(ST - 1):
                for d in range(2):
                    dve.wait_ge(B["u"], h * 6 + (2 * cc + d + 1))
                    s, u = BB[f"S{d}"], bk[3 * (1 - d)][:, 0:BDV]
                    if cc == 0:
                        nc.vector.tensor_copy(s, u).then_inc(B["s"], 1)
                    else:
                        c = chunk_of(cc, d)
                        dve.wait_ge(B["s"], h * 6 + (2 * (cc - 1) + d + 1))
                        nc.vector.scalar_tensor_tensor(out=s, in0=s, scalar=BB["gl"][:, 4 * d + c:4 * d + c + 1], in1=u,
                                                       op0=ALU.mult, op1=ALU.add).then_inc(B["s"], 1)
            dve.wait_ge(B["o_rs"], h + 1)
            for e in range(2):
                nc.vector.tensor_tensor(BB["o"][:, e, :], bk[6 + e][:, :], BB["rs"], ALU.mult).then_inc(B["of1"], 1)
            for e in range(2):
                dve.wait_ge(B["of1"], h * 2 + (e + 1))
                nc.vector.scalar_tensor_tensor(out=BB["o"][:, e, :], in0=BB["o"][:, e, :], scalar=col("b_norm_g", e),
                                               in1=head_tile(b_rT, h * 2, e), op0=ALU.mult, op1=ALU.mult).then_inc(B["of"], 1)
            for e in range(2):
                dve.wait_ge(B["o_hi"], h * 2 + (e + 1))
                nc.vector.tensor_tensor(head_tile(act_lo, h * 2, e), BB["o"][:, e, :], head_tile(act_hi, h * 2, e),
                                        ALU.subtract).then_inc(B["o_out"], 1)

        N = S + CTX
        c_ga = arena[:, 0:2048].rearrange("p (n s) -> p n s", n=4)
        c_gp = arena[:, 2048:4096].rearrange("p (n s) -> p n s", n=4)
        c_pin = arena[:, 4096:6208].rearrange("p (n s) -> p n s", n=4)
        c_cq = arena[:, 6208:7232].rearrange("p (n s) -> p n s", n=2)
        c_ckv = arena[:, 7232:8000]
        c_kr = arena[0:64, 8000:8768]
        c_v = arena[:, 8768:11840].rearrange("p (c n) -> p c n", c=6)
        ctx_hi, ctx_lo = (arena[:, 11840 + 1024 * i:12864 + 1024 * i].bitcast(BF16).rearrange("p (k s) -> p k s", k=KT)
                          for i in range(2))
        c_tmp = arena[:, 13888:14912].rearrange("p (i s) -> p i s", i=2)
        c_PT = arena[:, 11840:14912].rearrange("p (k s) -> p k s", k=6)
        c_rs = arena[:, 14912:15680]
        c_invc = work[:, 0:2048].rearrange("p (g s) -> p g s", g=4)
        c_gate = work[:, 2048:3072]
        c_gbias = work[:, 3072:4096]
        c_xn = work[:, 4096:8192].rearrange("p (c n) -> p c n", c=ST)
        c_ctx = work[:, 8192:10240].rearrange("p (c n) -> p c n", c=CT)
        CW = carve(work, [("uq", 2, 4 * QK_DIM), ("ukv", D), ("pool", 4, P), ("cos", N), ("sin", N), ("rot", P),
                          ("csb", KT, P), ("ga", KT, 2)], start=10240)
        CL = carve(work, [("sqq", 2, S), ("sqk", N), ("rsq", S), ("rsk", N)], start=4096)
        CH = carve(work, [("qn", S), ("qr", S), ("kn", N), ("kr", N), ("p", 2, N), ("vh", 6, P), ("pa", S + 16),
                          ("pb", S + 16)], start=4096)
        CS = carve(work, [("sqn", S), ("sqr", S), ("m", 2, 4), ("acc", 2, 4), ("r", 4), ("o", S)], start=16384)
        CT_ = carve(arena, [("rsq", S), ("rsk", N), ("rt", N)], start=11840)
        CWH = carve(arena, [("uq", 2, QK_DIM), ("uk", P)], start=15680)
        c_fin = arena[:, 0:4096].rearrange("p (c n) -> p c n", c=ST)

        class Steps:
            def __init__(self, name, what, credit=0):
                self.sem, self.what, self.n, self.credit = sem(name), what, 0, credit

            def at(self, what, i=0, h=None):
                v = [k for k, w in enumerate(self.what) if w == what][i] + 1 + self.credit
                return v if h is None else h * len(self.what) + v

            def inc(self, instruction, what):
                assert self.what[self.n % len(self.what)] == what, (self.n, what)
                self.n += 1
                instruction.then_inc(self.sem, 1)

        def lst(*parts):
            return [n for names, k in parts for n in names.split() * k]

        V = Steps("c_vector", lst(("gate", 1), ("stats stats mean ms", 6), ("xn", 6), ("ga1 ga", 1), ("tmp lo", 16), ("lat", 3)))
        K = Steps("c_scalar", lst(("csb", 1), ("ln rs", 6), ("hi", 16), ("ckv kr", 1), ("sq", 3),
                                  ("ln2 rs2", 3), ("v", 6)))
        T = Steps("c_tensor", lst(("gate", 1), ("turned", 16), ("ctx ctx", 1), ("sum", 3), ("v", 6)))
        Q = Steps("c_pool", lst(("pads", 1), *[(" ".join(["add"] * (g + 1)) + " mul pooled", 1) for g in range(4)]))
        HV = Steps("h_vector", lst(("q q", 1), ("k k k", 1), ("rt", 1), ("cos", 1), ("q_roped", 1), ("rt rt", 1), ("cos", 1), ("k_roped", 1),
                                   ("max max nmax sum rsum p pt", 4), ("o lo", 1)), 1)
        HK = Steps("h_scalar", lst(("sqq sqq sqk sqk sqk", 1), ("ln ln ln", 1), ("rs rs rs", 1), ("e e pt", 4), ("hi", 1)))
        HT = Steps("h_tensor", lst(("q q k k", 1), ("sum_q sum_k sum_k", 1), ("rot rot rot", 1), ("score score", 2),
                                   ("turned turned score score", 2), ("turned turned", 2), ("o", 1)), 1)
        HQ = Steps("h_pool", lst(("w w vh", 1)))
        c_const = sem("c_const")
        ctx_loaded = sem("ctx_loaded")
        inv_loaded = sem("inv_loaded")
        br_mm = sem("br_mm")
        br_f = sem("br_f")
        br_hi = sem("br_hi")
        br_lo = sem("br_lo")
        fin1 = sem("fin1")
        fin = sem("fin")
        stored = sem("stored")
        x_src = [(c_ctx, 0), (c_ctx, 1)] + [(X, t) for t in range(ST)]
        xn_dst = [(c_ctx, 0), (c_ctx, 1)] + [(c_xn, t) for t in range(ST)]

        def pool_c_load(pool):
            uq, ukv = a["w_uq_2"][0], a["w_ukv_2"][0]
            for dst, src in ((CW["uq"], uq.rearrange("(k p) n -> p k n", p=P)), (CW["ukv"], ukv),
                             (CW["pool"], a["w_pool_2"][0].rearrange("g c d -> c g d")), (CW["cos"][0:64, :], a["k_cos"]),
                             (CW["sin"][0:64, :], a["k_sin"]), (CW["rot"][0:64, :], a["k_rot"])):
                pool.dma_start(dst, src).then_inc(c_const, 16)
            pool.wait_ge(hid_ready, 4 + 64)
            pool.dma_start(c_ctx, a["ctx_2"][0].rearrange("(c p) n -> p c n", p=P)).then_inc(ctx_loaded, 16)
            pool.wait_ge(T.sem, T.at("gate"))
            pool.dma_start(c_invc, a["k_invcount"].rearrange("g s -> (g s)").partition_broadcast(P)).then_inc(inv_loaded, 16)
            pool.dma_start(c_gbias, a["b_mod_2"][0, 2 * D:3 * D].partition_broadcast(P)).then_inc(inv_loaded, 16)
            Q.inc(nc.gpsimd.memset(arena[:, 4096:6208], 0.0), "pads")

        def pe_c_gate(pe):
            pe.wait_ge(wmod_loaded, 48)
            pe.wait_ge(K.sem, K.at("csb"))
            pe.wait_ge(sum_added, 4 * TH["down1"] + 8)
            for half in range(2):
                for kt in range(KT):
                    mm = nc.tensor.matmul(bk[6 + half][:, :], CW["csb"][:, kt, :], wmod[:, kt, half * 512:half * 512 + 512],
                                          start=kt == 0, stop=kt == KT - 1)
            T.inc(mm, "gate")

        def act_c_csb(act):
            act.wait_ge(c_const, 16 * 6)
            K.inc(nc.scalar.activation(CW["csb"], csil[:, 0:KT].unsqueeze(2).broadcast_to([P, KT, P]), ACT.Copy), "csb")

        def dve_c_norm(dve):
            dve.wait_ge(T.sem, T.at("gate"))
            dve.wait_ge(inv_loaded, 32)
            for half in range(2):
                hs = slice(half * 512, half * 512 + 512)
                i = nc.vector.tensor_tensor(c_gate[:, hs], bk[6 + half][:, :], c_gbias[:, hs], ALU.add)
            V.inc(i, "gate")
            dve.wait_ge(x_ready, 16)
            dve.wait_ge(ctx_loaded, 16)
            for t, (src, n) in enumerate(x_src):
                for hf in range(2):
                    V.inc(nc.vector.bn_stats(stats[:, t, hf, :], src[:, n, hf * 512:hf * 512 + 512]), "stats")
                dve.wait_ge(V.sem, V.at("stats", 2 * t + 1))
                V.inc(nc.vector.bn_aggr(mv[:, t, :], stats[:, t, :, :]), "mean")
                dve.wait_ge(V.sem, V.at("mean", t))
                V.inc(nc.vector.scalar_tensor_tensor(out=mv[:, t, 0:1], in0=mv[:, t, 0:1], scalar=mv[:, t, 0:1],
                                                     in1=mv[:, t, 1:2], op0=ALU.mult, op1=ALU.add), "ms")
            for t, ((src, n), (dst, m)) in enumerate(zip(x_src, xn_dst)):
                dve.wait_ge(K.sem, K.at("rs", t))
                V.inc(nc.vector.tensor_scalar(dst[:, m, :], src[:, n, :], rstd[:, t, 1:2], None, ALU.mult), "xn")
            r = VEC["norm_g"][0]
            dve.wait_ge(mod_read, 2)
            V.inc(nc.vector.tensor_scalar(CW["ga"], modc[:, 8:16, :], 1.0, None, ALU.add), "ga1")
            dve.wait_ge(V.sem, V.at("ga1"))
            V.inc(nc.vector.tensor_tensor(CW["ga"], CW["ga"], cols[:, r:r + 8].unsqueeze(2).broadcast_to([P, KT, 2]),
                                          ALU.mult), "ga")
            dve.wait_ge(V.sem, V.at("ga"))
            for i in range(16):
                kt, w = i % 8, 1 if i < 8 else 0
                tmp, src, hi, lo = c_turned(i)
                dve.wait_ge(T.sem, T.at("turned", i))
                V.inc(nc.vector.tensor_scalar(tmp, src, CW["ga"][:, kt, w:w + 1], modc[:, kt, w:w + 1], ALU.mult, ALU.add), "tmp")
                dve.wait_ge(K.sem, K.at("hi", i))
                V.inc(nc.vector.tensor_tensor(lo, tmp, hi, ALU.subtract), "lo")

        def c_turned(i):
            kt = i % 8
            if i < 8:
                return (c_tmp[:, i % 2, 0:CTX], bk[4 + kt % 2][:, 0:CTX], ctx_hi[:, kt, :], ctx_lo[:, kt, :])
            return c_tmp[:, i % 2, :], bk[kt % 4][:, :], act_hi[:, kt, :], act_lo[:, kt, :]

        def act_c_norm(act):
            for t in range(6):
                act.wait_ge(V.sem, V.at("ms", t))
                K.inc(nc.scalar.activation(rstd[:, t, 0:1], mv[:, t, 0:1], ACT.Ln, bias=RMS_EPS), "ln")
                act.wait_ge(K.sem, K.at("ln", t))
                K.inc(nc.scalar.activation(rstd[:, t, 1:2], rstd[:, t, 0:1], ACT.Exp, scale=-0.5), "rs")
            for i in range(16):
                tmp, _, hi, _ = c_turned(i)
                act.wait_ge(V.sem, V.at("tmp", i))
                K.inc(nc.scalar.activation(hi, tmp, ACT.Copy), "hi")

        def pe_c_turn(pe):
            for i in range(16):
                kt = i % 8
                if i == 0:
                    pe.wait_ge(V.sem, V.at("xn", 1))
                    pe.wait_ge(sum_added, 4 * TH["down1"] + 8)
                if i == 8:
                    pe.wait_ge(V.sem, V.at("xn", 5))
                if 2 <= i < 8:
                    pe.wait_ge(V.sem, V.at("tmp", i - 2))
                if i >= 12:
                    pe.wait_ge(V.sem, V.at("tmp", i - 4))
                for t in range(CT if i < 8 else ST):
                    src, n = xn_dst[t if i < 8 else t + 2]
                    mm = nc.tensor.transpose(c_turned(i)[1][:, t * P:t * P + P], src[:, n, kt * P:kt * P + P], eye[:, :])
                T.inc(mm, "turned")

        def sp_c_in(sp):
            w = a["w_in_2"][0].rearrange("(k p) n -> p k n", p=P)
            k0 = PH["c_in"][0] // 2
            load_slab(sp, k0, 0, w[:, :, 0:256])
            load_slab(sp, k0, 1, w[:, :, 256:448])
            with sp.Fori(1, 4) as k2:
                for b in range(2):
                    load_slab(sp, k2 + k0, b, slab_source("c_in", k2, b))

        def pe_c_in(pe):
            pe.wait_ge(V.sem, V.at("lo", 15))
            pe_feature_slab(pe, "c_in", 0, 0)
            pe.wait_ge(w_ready, PH["c_in"][0] + 2)
            hi, lo = (t[1][:, 0:KT * 192].rearrange("p (k n) -> p k n", k=KT) for t in (whi, wlo))
            for j, m in enumerate((P, 64)):
                for kt in range(KT):
                    c = slice(j * P, j * P + m)
                    mm = mm3(bk[4 + j][0:m, 0:CTX], hi[:, kt, c], lo[:, kt, c], ctx_hi[:, kt, :], ctx_lo[:, kt, :],
                             kt == 0, kt == KT - 1)
                T.inc(mm, "ctx")
            pe_feature_slab(pe, "c_in", 0, 1, 192)
            for k2 in range(1, 4):
                for b in range(2):
                    pe_feature_slab(pe, "c_in", k2, b)

        def act_c_in(act):
            for j in range(2):
                wait_tile(act, "c_in", 0, 0, j)
                i = nc.scalar.activation(c_cq[:, j, :], bk[j][:, :], ACT.Copy)
                i.then_inc(acc_free, 1)
            split_hi(act, next_pair("c_in", 0), 0)
            act.wait_ge(T.sem, T.at("ctx", 1))
            K.inc(nc.scalar.activation(c_ckv[:, 0:CTX], bk[4][:, 0:CTX], ACT.Copy), "ckv")
            K.inc(nc.scalar.activation(c_kr[:, 0:CTX], bk[5][0:64, 0:CTX], ACT.Copy), "kr")
            for j, (dst, m) in enumerate(((c_ckv, P), (c_kr, 64))):
                wait_tile(act, "c_in", 0, 1, j)
                nc.scalar.activation(dst[:, CTX:N], bk[2 + j][0:m, :], ACT.Copy).then_inc(acc_free, 1)
            split_hi(act, next_pair("c_in", 0), 1)
            act.wait_ge(Q.sem, Q.at("pads"))
            for k2 in range(1, 4):
                for b in range(2):
                    for j in range(2):
                        n = 2 * b + j
                        wait_tile(act, "c_in", k2, b, j)
                        dst = (c_ga[:, n, :], c_pin[:, n, 8:8 + S], c_gp[:, n, :])[k2 - 1]
                        nc.scalar.activation(dst, bk[n][:, :], ACT.Copy if k2 == 2 else ACT.Silu).then_inc(acc_free, 1)
                    split_hi(act, next_pair("c_in", k2), b)
            act.wait_ge(acc_free, 2 * FS["c_in"] + 4)
            for dst, src in ((CL["sqq"][:, 0, :], c_cq[:, 0, :]), (CL["sqq"][:, 1, :], c_cq[:, 1, :]), (CL["sqk"], c_ckv)):
                K.inc(nc.scalar.activation(dst, src, ACT.Square), "sq")
            for i, (dst, bank, n, width) in enumerate(((CL["rsq"], 0, S, 256), (CL["rsk"][:, 0:S], 1, S, P),
                                                       (CL["rsk"][:, S:N], 2, CTX, P))):
                act.wait_ge(T.sem, T.at("sum", i))
                K.inc(nc.scalar.activation(dst, bk[bank][:, 0:n], ACT.Ln, bias=RMS_EPS, scale=1.0 / width), "ln2")
                act.wait_ge(K.sem, K.at("ln2", i))
                K.inc(nc.scalar.activation(dst, dst, ACT.Exp, scale=-0.5), "rs2")
            for t in range(6):
                act.wait_ge(T.sem, T.at("v", t))
                K.inc(nc.scalar.activation(c_v[:, t, :], bk[4 + t % 2][:, :], ACT.Copy), "v")

        def dve_c_in(dve):
            with dve.Fori(0, 4) as k2:
                for b in range(2):
                    split_lo(dve, next_pair("c_in", k2), b)
            dve.wait_ge(acc_free, 2 * FS["c_in"] + 4)
            for i, (x, rs, g) in enumerate(((c_cq[:, 0, :], CL["rsq"], col("q_lora_g", 0)), (c_cq[:, 1, :], CL["rsq"], col("q_lora_g", 1)),
                                            (c_ckv, CL["rsk"], col("kv_lora_g")))):
                dve.wait_ge(K.sem, K.at("rs2", 0 if i < 2 else 2))
                V.inc(nc.vector.scalar_tensor_tensor(out=x, in0=x, scalar=g, in1=rs, op0=ALU.mult, op1=ALU.mult), "lat")

        def pe_c_latent(pe):
            pe.wait_ge(K.sem, K.at("sq", 1))
            pe.wait_ge(acc_free, 2 * FS["c_in"] + 16)
            for i in range(2):
                mm = nc.tensor.matmul(bk[0][:, :], ones[:, :], CL["sqq"][:, i, :], start=i == 0, stop=i == 1)
            T.inc(mm, "sum")
            pe.wait_ge(K.sem, K.at("sq", 2))
            T.inc(nc.tensor.matmul(bk[1][:, :], ones[:, :], CL["sqk"][:, 0:S], start=True, stop=True), "sum")
            T.inc(nc.tensor.matmul(bk[2][:, 0:CTX], ones[:, :], CL["sqk"][:, S:N], start=True, stop=True), "sum")
            pe.wait_ge(V.sem, V.at("lat", 2))
            wv = CW["ukv"].rearrange("p (h t n) -> p h t n", h=4, t=2)[:, :, 1, :]
            pe.wait_ge(c_const, 16 * 6)
            for t in range(6):
                if t >= 2:
                    pe.wait_ge(K.sem, K.at("v", t - 2))
                T.inc(nc.tensor.matmul(bk[4 + t % 2][:, :].rearrange("p (h n) -> p h n", h=4), c_ckv[:, t * P:t * P + P], wv,
                                       start=True, stop=True), "v")

        def pool_c_pooling(pool):
            pool.wait_ge(acc_free, 2 * FS["c_in"] + 12)
            pool.wait_ge(inv_loaded, 32)
            pool.wait_ge(V.sem, V.at("lo", 15))
            n_add = 0
            for g in range(4):
                src, width = c_pin[:, g, :], S + 16
                for j in range(g + 1):
                    dst = CH["pa"] if j % 2 == 0 else CH["pb"]
                    width -= 1 << j
                    if n_add:
                        pool.wait_ge(Q.sem, Q.at("add", n_add - 1) if j else Q.at("pooled", g - 1))
                    Q.inc(nc.gpsimd.tensor_tensor(dst[:, 0:width], src[:, 0:width], src[:, (1 << j):(1 << j) + width], ALU.add), "add")
                    n_add += 1
                    src = dst
                w = POOL_W[g]
                other = CH["pb"] if g % 2 == 0 else CH["pa"]
                pool.wait_ge(Q.sem, Q.at("add", n_add - 1))
                Q.inc(nc.gpsimd.tensor_tensor(other[:, 0:S], src[:, 8 - w // 2:8 - w // 2 + S], c_invc[:, g, :], ALU.mult), "mul")
                pool.wait_ge(Q.sem, Q.at("mul", g))
                x = c_pin[:, g, 8:8 + S]
                Q.inc(nc.gpsimd.tensor_tensor(x, other[:, 0:S], x, ALU.subtract), "pooled")

        SCALE = float(QK_DIM) ** -0.5
        def pool_c_head(pool, h):
            pool.wait_ge(HT.sem, h * len(HT.what) + 1)
            gap(pool)
            HQ.inc(nc.gpsimd.tensor_copy(CWH["uq"], CW["uq"][:, :, bass.ds(h * QK_DIM, QK_DIM)]), "w")
            HQ.inc(nc.gpsimd.tensor_copy(CWH["uk"], CW["ukv"][:, bass.ds(h * 2 * P, P)]), "w")
            HQ.inc(nc.gpsimd.tensor_copy(CH["vh"], c_v[:, :, bass.ds(h * P, P)]), "vh")

        def pe_c_head(pe, h):
            pe.wait_ge(HQ.sem, HQ.at("vh", 0, h))
            pe.wait_ge(HV.sem, h * len(HV.what) + 1)
            for j, m in enumerate((P, 64)):
                for kt in range(2):
                    mm = nc.tensor.matmul(bk[j][0:m, :], CWH["uq"][:, kt, j * P:j * P + m], c_cq[:, kt, :], start=kt == 0, stop=kt == 1)
                HT.inc(mm, "q")
            HT.inc(nc.tensor.matmul(bk[2][:, :], CWH["uk"], c_ckv[:, 0:S], start=True, stop=True), "k")
            HT.inc(nc.tensor.matmul(bk[3][:, 0:CTX], CWH["uk"], c_ckv[:, S:N], start=True, stop=True), "k")
            pe.wait_ge(HK.sem, HK.at("sqq", 1, h))
            nc.tensor.matmul(bk[4][:, :], ones[:, :], CS["sqn"], start=True, stop=False)
            HT.inc(nc.tensor.matmul(bk[4][:, :], ones[0:64, :], CS["sqr"][0:64, :], start=False, stop=True), "sum_q")
            pe.wait_ge(HK.sem, HK.at("sqk", 2, h))
            for bank, ts in ((5, slice(0, S)), (6, slice(S, N))):
                n = ts.stop - ts.start
                nc.tensor.matmul(bk[bank][:, 0:n], ones[:, :], CH["p"][:, 0, ts], start=True, stop=False)
                HT.inc(nc.tensor.matmul(bk[bank][:, 0:n], ones[0:64, :], CH["p"][0:64, 1, ts], start=False, stop=True), "sum_k")
            pe.wait_ge(HV.sem, HV.at("q", 1, h))
            HT.inc(nc.tensor.matmul(bk[1][:, :], CW["rot"][0:64, :], CH["qr"][0:64, :], start=True, stop=True), "rot")
            pe.wait_ge(HV.sem, HV.at("k", 2, h))
            HT.inc(nc.tensor.matmul(bk[2][:, :], CW["rot"][0:64, :], CH["kr"][0:64, 0:S], start=True, stop=True), "rot")
            HT.inc(nc.tensor.matmul(bk[3][:, 0:CTX], CW["rot"][0:64, :], CH["kr"][0:64, S:N], start=True, stop=True), "rot")
            pe.wait_ge(HV.sem, HV.at("k_roped", 0, h))

            def scores(qt):
                if qt >= 2:
                    pe.wait_ge(HK.sem, HK.at("e", 2 * (qt - 2) + 1, h))
                qs = slice(qt * P, qt * P + P)
                for half, (ts, n) in enumerate(((slice(0, S), S), (slice(S, N), CTX))):
                    dst = bk[2 * (qt % 2) + half][:, 0:n]
                    nc.tensor.matmul(dst, CH["qn"][:, qs], CH["kn"][:, ts], start=True, stop=False)
                    HT.inc(nc.tensor.matmul(dst, CH["qr"][0:64, qs], CH["kr"][0:64, ts], start=False, stop=True), "score")

            def turn(qt):
                pe.wait_ge(HV.sem, HV.at("p", qt, h))
                if qt > 0:
                    pe.wait_ge(HK.sem, HK.at("pt", qt - 1, h))
                    pe.wait_ge(HV.sem, HV.at("pt", qt - 1, h))
                for k in range(6):
                    mm = nc.tensor.transpose(bk[4 + k // 4][:, (k % 4) * P:(k % 4) * P + P], CH["p"][:, qt % 2, k * P:k * P + P], eye[:, :])
                    if k in (3, 5):
                        HT.inc(mm, "turned")

            scores(0)
            for qt in range(ST):
                if qt + 1 < ST:
                    scores(qt + 1)
                turn(qt)
            pe.wait_ge(HK.sem, HK.at("pt", 3, h))
            pe.wait_ge(HV.sem, HV.at("pt", 3, h))
            for k in range(6):
                mm = nc.tensor.matmul(bk[7][:, :], CH["vh"][:, k, :], c_PT[:, k, :], start=k == 0, stop=k == 5)
            HT.inc(mm, "o")

        def act_c_head(act, h):
            act.wait_ge(HV.sem, h * len(HV.what) + 1)
            act.wait_ge(HT.sem, HT.at("q", 0, h))
            HK.inc(nc.scalar.activation(CS["sqn"], bk[0][:, :], ACT.Square), "sqq")
            act.wait_ge(HT.sem, HT.at("q", 1, h))
            HK.inc(nc.scalar.activation(CS["sqr"][0:64, :], bk[1][0:64, :], ACT.Square), "sqq")
            act.wait_ge(HT.sem, HT.at("k", 0, h))
            HK.inc(nc.scalar.activation(CH["p"][:, 0, 0:S], bk[2][:, :], ACT.Square), "sqk")
            act.wait_ge(HT.sem, HT.at("k", 1, h))
            HK.inc(nc.scalar.activation(CH["p"][:, 0, S:N], bk[3][:, 0:CTX], ACT.Square), "sqk")
            HK.inc(nc.scalar.activation(CH["p"][0:64, 1, :], c_kr, ACT.Square), "sqk")
            jobs = ((CT_["rsq"], 4, S), (CT_["rsk"][:, 0:S], 5, S), (CT_["rsk"][:, S:N], 6, CTX))
            for i, (dst, bank, n) in enumerate(jobs):
                act.wait_ge(HT.sem, HT.at("sum_q", 0, h) if i == 0 else HT.at("sum_k", i - 1, h))
                HK.inc(nc.scalar.activation(dst, bk[bank][:, 0:n], ACT.Ln, bias=RMS_EPS, scale=1.0 / QK_DIM), "ln")
            for i, (dst, bank, n) in enumerate(jobs):
                act.wait_ge(HK.sem, HK.at("ln", i, h))
                HK.inc(nc.scalar.activation(dst, dst, ACT.Exp, scale=-0.5), "rs")

            for qt in range(ST):
                act.wait_ge(HV.sem, HV.at("nmax", qt, h))
                if qt >= 2:
                    act.wait_ge(HT.sem, HT.at("turned", 2 * (qt - 2) + 1, h))
                for half, (ts, n) in enumerate(((slice(0, S), S), (slice(S, N), CTX))):
                    HK.inc(nc.scalar.activation(CH["p"][:, qt % 2, ts], bk[2 * (qt % 2) + half][:, 0:n], ACT.Exp, scale=SCALE,
                                                bias=CS["m"][:, 0, qt:qt + 1], accum_out=CS["acc"][:, half, qt:qt + 1]), "e")
                act.wait_ge(HT.sem, HT.at("turned", 2 * qt, h))
                HK.inc(nc.scalar.activation(c_PT[:, 0:4, qt * P:qt * P + P], chunks(bk[4]), ACT.Copy), "pt")
            act.wait_ge(HV.sem, HV.at("o", 0, h))
            gap(act)
            HK.inc(nc.scalar.activation(head_tile(act_hi, h), CS["o"], ACT.Copy), "hi")

        def dve_c_head(dve, h):
            stt = lambda out, x, g, rs: nc.vector.scalar_tensor_tensor(out=out, in0=x, scalar=g, in1=rs, op0=ALU.mult, op1=ALU.mult)
            qg, kg = [col("q_norm_g", 0), col("q_norm_g", 1)[0:64, :]], [col("k_norm_g", 0), col("k_norm_g", 1)[0:64, :]]
            dve.wait_ge(HK.sem, HK.at("rs", 0, h))
            HV.inc(stt(CH["qn"], bk[0][:, :], qg[0], CT_["rsq"]), "q")
            HV.inc(stt(CH["qr"][0:64, :], bk[1][0:64, :], qg[1], CT_["rsq"][0:64, :]), "q")
            dve.wait_ge(HK.sem, HK.at("rs", 2, h))
            HV.inc(stt(CH["kn"][:, 0:S], bk[2][:, :], kg[0], CT_["rsk"][:, 0:S]), "k")
            HV.inc(stt(CH["kn"][:, S:N], bk[3][:, 0:CTX], kg[0], CT_["rsk"][:, S:N]), "k")
            HV.inc(stt(CH["kr"][0:64, :], c_kr, kg[1], CT_["rsk"][0:64, :]), "k")
            rt = CT_["rt"][0:64, :]
            for i, (x, off, parts) in enumerate(((CH["qr"][0:64, :], CTX, ((1, 0, S),)),
                                                 (CH["kr"][0:64, :], 0, ((2, 0, S), (3, S, N))))):
                cos, sin = CW["cos"][0:64, off:N], CW["sin"][0:64, off:N]
                width = N - off
                if i == 1:
                    dve.wait_ge(HV.sem, HV.at("q_roped", 0, h))
                for j, (bank, t0, t1) in enumerate(parts):
                    dve.wait_ge(HT.sem, HT.at("rot", i + j, h))
                    HV.inc(nc.vector.tensor_tensor(rt[:, t0:t1], bk[bank][0:64, 0:t1 - t0], sin[:, t0:t1], ALU.mult), "rt")
                HV.inc(nc.vector.tensor_tensor(x, x, cos, ALU.mult), "cos")
                dve.wait_ge(HV.sem, HV.at("cos", i, h))
                HV.inc(nc.vector.tensor_tensor(x, x, rt[:, 0:width], ALU.add), ("q_roped", "k_roped")[i])
            for qt in range(ST):
                for half, n in enumerate((S, CTX)):
                    dve.wait_ge(HT.sem, HT.at("score", 2 * qt + half, h))
                    HV.inc(nc.vector.reduce_max(CS["m"][:, half, qt:qt + 1], bk[2 * (qt % 2) + half][:, 0:n], AX_X), "max")
                dve.wait_ge(HV.sem, HV.at("max", 2 * qt + 1, h))
                HV.inc(nc.vector.tensor_scalar(CS["m"][:, 0, qt:qt + 1], CS["m"][:, 0, qt:qt + 1], CS["m"][:, 1, qt:qt + 1],
                                               -SCALE, ALU.max, ALU.mult), "nmax")
                dve.wait_ge(HK.sem, HK.at("e", 2 * qt + 1, h))
                HV.inc(nc.vector.tensor_tensor(CS["r"][:, qt:qt + 1], CS["acc"][:, 0, qt:qt + 1], CS["acc"][:, 1, qt:qt + 1],
                                               ALU.add), "sum")
                dve.wait_ge(HV.sem, HV.at("sum", qt, h))
                HV.inc(nc.vector.reciprocal(CS["r"][:, qt:qt + 1], CS["r"][:, qt:qt + 1]), "rsum")
                dve.wait_ge(HV.sem, HV.at("rsum", qt, h))
                HV.inc(nc.vector.tensor_scalar(CH["p"][:, qt % 2, :], CH["p"][:, qt % 2, :], CS["r"][:, qt:qt + 1], None,
                                               ALU.mult), "p")
                dve.wait_ge(HT.sem, HT.at("turned", 2 * qt + 1, h))
                HV.inc(nc.vector.tensor_copy(c_PT[:, 4:6, qt * P:qt * P + P],
                                             bk[5][:, 0:CTX].rearrange("p (k s) -> p k s", k=2)), "pt")
            dve.wait_ge(HT.sem, HT.at("o", 0, h))
            at_token = lambda v: v.rearrange("p (i b) -> p b i", b=ST)
            HV.inc(nc.vector.tensor_tensor(at_token(CS["o"]), bk[7][:, :].rearrange("p (b i) -> p b i", b=ST),
                                           at_token(head_tile(c_ga, h)), ALU.mult), "o")
            dve.wait_ge(HK.sem, HK.at("hi", 0, h))
            HV.inc(nc.vector.tensor_tensor(head_tile(act_lo, h), CS["o"], head_tile(act_hi, h), ALU.subtract), "lo")

        def pe_c_pool(pe):
            pe.wait_ge(Q.sem, Q.at("pooled", 3))
            pe.wait_ge(HV.sem, 4 * len(HV.what) + 1)
            for g in range(4):
                nc.tensor.matmul(bk[g][:, :], CW["pool"][:, g, :], c_pin[:, g, 8:8 + S], start=True, stop=True).then_inc(br_mm, 1)
            pe.wait_ge(br_lo, 4)

        def dve_c_pool(dve):
            for g in range(4):
                dve.wait_ge(br_mm, g + 1)
                nc.vector.scalar_tensor_tensor(out=c_gp[:, g, :], in0=bk[g][:, :], scalar=col("pool_scale", g), in1=c_gp[:, g, :],
                                               op0=ALU.mult, op1=ALU.mult).then_inc(br_f, 1)
            for g in range(4):
                dve.wait_ge(br_hi, g + 1)
                nc.vector.tensor_tensor(act_lo[:, 4 + g, :], c_gp[:, g, :], act_hi[:, 4 + g, :], ALU.subtract).then_inc(br_lo, 1)

        def act_c_pool(act):
            for g in range(4):
                act.wait_ge(br_f, g + 1)
                nc.scalar.activation(act_hi[:, 4 + g, :], c_gp[:, g, :], ACT.Copy).then_inc(br_hi, 1)

        def dve_c_out(dve):
            for b in range(2):
                split_lo(dve, next_pair("c_out", 0), b)
            n = 0
            for half in range(2):
                for st in range(ST):
                    hs = slice(half * 512, half * 512 + 512)
                    wait_sum(dve, "c_out", half, st)
                    nc.vector.tensor_tensor(c_fin[:, st, hs], bk[4 * half + st][:, :], c_gate[:, hs], ALU.mult).then_inc(fin1, 1)
                    n += 1
                    dve.wait_ge(fin1, n)
                    nc.vector.tensor_tensor(X[:, st, hs], X[:, st, hs], c_fin[:, st, hs], ALU.add).then_inc(fin, 1)

        def act_c_out(act):
            for b in range(2):
                split_hi(act, next_pair("c_out", 0), b)

        def sp_store(sp):
            for st in range(ST):
                sp.wait_ge(fin, 4 + st + 1)
                sp.dma_start(out[0, st * P:st * P + P, :], X[:, st, :]).then_inc(stored, 16)
            sp.wait_ge(stored, 16 * ST)

        block = ctx.enter_context(nc.Block())

        @block.sync
        def _(sp):
            sp_start(sp)
            sp_feature(sp, "a_in", 1)
            sp_token(sp, "a_out")
            sp_feature(sp, "up0")
            sp_token(sp, "down0")
            sp_feature(sp, "b_qk")
            sp_token(sp, "b_v")
            sp_feature(sp, "b_r")
            sp_token(sp, "b_out")
            sp_feature(sp, "up1")
            sp_token(sp, "down1")
            sp_c_in(sp)
            sp_token(sp, "c_out")
            sp_store(sp)

        @block.gpsimd
        def _(pool):
            pool_start(pool)
            pool.wait_ge(G["bexp"], 1)
            with pool.Fori(0, AH) as h:
                pool_a_head(pool, h)
            pool.wait_ge(G["o_out"], AH + 1)
            load_lnrow(pool, 1, a["ln1_g"][0], a["ln1_b"][0])
            load_wmod(pool, 0)
            pool.wait_ge(x_ready, 4)
            load_lnrow(pool, 2, a["ln2_g"][0], a["ln2_b"][0])
            pool_b_load(pool)
            pool.wait_ge(B["la"], 2 * ST)
            with pool.Fori(0, BH) as h:
                pool_b_head(pool, h)
            pool.wait_ge(B["o_out"], 2 * BH + 2)
            load_lnrow(pool, 3, a["ln1_g"][1], a["ln1_b"][1])
            load_wmod(pool, 1)
            pool.wait_ge(x_ready, 12)
            load_lnrow(pool, 4, a["ln2_g"][1], a["ln2_b"][1])
            pool.wait_ge(mod_mm, 2)
            load_wmod(pool, 2)
            pool_c_load(pool)
            pool_c_pooling(pool)
            pool.wait_ge(K.sem, K.at("v", 5))
            with pool.Fori(0, 4) as h:
                pool_c_head(pool, h)

        @block.scalar
        def _(act):
            act_start(act)
            act_begin(act)
            act_a_in(act)
            act_a_gates(act)
            with act.Fori(0, AH) as h:
                act_a_head(act, h)
            act_token_layer(act, "a_out", 1)
            act_up(act, 0)
            act_token_layer(act, "down0", 2)
            act_b_gate_weights(act)
            act_b_in(act)
            with act.Fori(0, BH) as h:
                act_b_head(act, h)
            act_token_layer(act, "b_out", 3)
            act_up(act, 1)
            act_c_csb(act)
            act_token_layer(act, "down1", 4)
            act_c_norm(act)
            act_c_in(act)
            with act.Fori(0, 4) as h:
                act_c_head(act, h)
            act_c_pool(act)
            act_c_out(act)

        @block.vector
        def _(dve):
            dve_start(dve)
            dve_a_in(dve)
            dve_a_gates(dve)
            with dve.Fori(0, AH) as h:
                dve_a_head(dve, h)
            dve_token_layer(dve, "a_out", 1)
            dve_mod(dve, 0)
            dve_up(dve, 0)
            dve_token_layer(dve, "down0", 2)
            dve_b_in(dve)
            with dve.Fori(0, BH) as h:
                dve_b_head(dve, h)
            dve_token_layer(dve, "b_out", 3)
            dve_mod(dve, 1)
            dve_up(dve, 1)
            dve_token_layer(dve, "down1", 4)
            dve_c_norm(dve)
            dve_c_in(dve)
            with dve.Fori(0, 4) as h:
                dve_c_head(dve, h)
            dve_c_pool(dve)
            dve_c_out(dve)

        @block.tensor
        def _(pe):
            pe_start(pe)
            pe_a_in(pe)
            pe_a_gates(pe)
            with pe.Fori(0, AH) as h:
                pe_a_head(pe, h)
            pe.wait_ge(G["o_out"], AH + 1)
            pe_token_layer(pe, "a_out", act_hi, act_lo)
            pe_turn(pe, 1, 4 * (TH["a_out"] + 1))
            pe_mod(pe, 0, "a_out")
            pe_up(pe, 0, 1)
            pe_down(pe, 0)
            pe_turn(pe, 2, 4 * (TH["down0"] + 1))
            pe_b_in(pe)
            with pe.Fori(0, BH) as h:
                pe_b_head(pe, h)
            pe.wait_ge(B["o_out"], 2 * BH + 2)
            pe_token_layer(pe, "b_out", act_hi, act_lo)
            pe_turn(pe, 3, 4 * (TH["b_out"] + 1))
            pe_mod(pe, 1, "b_out")
            pe_up(pe, 1, 3)
            pe_down(pe, 1)
            pe_c_gate(pe)
            pe_c_turn(pe)
            pe_c_in(pe)
            pe_c_latent(pe)
            with pe.Fori(0, 4) as h:
                pe_c_head(pe, h)
            pe_c_pool(pe)
            pe_token_layer(pe, "c_out", act_hi, act_lo)


_INS = ["x", "a_w_in", "a_conv", "a_alog", "a_dt_bias", "a_norm_g", "a_w_out", "b_w_in", "b_gate_w2", "b_gate_b",
        "b_norm_g", "b_w_out", "ln1_g", "ln1_b", "mlp_w1", "mlp_w2", "ln2_g", "ln2_b", "c_2", "ctx_2", "c_ctx_2",
        "w_mod_2", "b_mod_2", "norm_g_2", "w_in_2", "q_lora_g_2", "w_uq_2", "kv_lora_g_2", "w_ukv_2", "q_norm_g_2",
        "k_norm_g_2", "w_pool_2", "pool_scale_2", "w_out_2"]


def kernel(**inputs):
    import concourse.bacc as bacc
    from concourse.bass_utils import run_bass_kernel_spmd

    nc = bacc.Bacc("TRN2", target_bir_lowering=False, num_devices=1)
    arrays, aps = {}, {}
    given = {n: inputs[n] for n in _INS}
    given.update(shape_constants())
    for name, v in given.items():
        v = np.ascontiguousarray(v)
        arrays[f"in_{name}"] = v
        aps[name] = nc.dram_tensor(f"in_{name}", v.shape, mybir.dt.from_np(v.dtype), kind="ExternalInput").ap()
    out = nc.dram_tensor("out", (1, S, D), F32, kind="ExternalOutput").ap()
    build(nc, aps, out)
    r = run_bass_kernel_spmd(nc, [arrays], core_ids=[0])
    return r.results[0]["out"]
```

```python
from contextlib import ExitStack

import numpy as np

import concourse.bass as bass
from concourse import mybir

ALU = mybir.AluOpType
ACT = mybir.ActivationFunctionType
F32 = mybir.dt.float32
F32R = mybir.dt.float32r
U8 = mybir.dt.uint8
AX_X = mybir.AxisListType.X

P = 128
D = 1024
S = 512
ST = S // P
KT = D // P
FF = 4 * D
AH = 8
BH = 4
BDV = 256
RANK = 16
CONV = 5
CTX = 256
CT = CTX // P
LEVELS = 7
ALPHA = 4.0 ** 0.25
LN_EPS = 1e-5
RMS_EPS = 1e-6
QK_DIM = 192
SLAB = 2048
POOL_W = (2, 4, 8, 16)

PH = {}
_n = 0
for _name, _c in (("a_in", 16), ("a_out", 4), ("up0", 16), ("down0", 16), ("b_qk", 4), ("b_v", 4), ("b_r", 4),
                  ("b_out", 4), ("up1", 16), ("down1", 16), ("c_in", 8), ("c_out", 4)):
    PH[_name] = (_n, _c)
    _n += _c
NSLABS = _n

VEC = {}
_n = 0
for _name, _c in (("norm_g", 8), ("b_mod", 16), ("pool_scale", 4), ("q_lora_g", 2), ("kv_lora_g", 1),
                  ("a_norm_g", 1), ("b_norm_g", 2), ("q_norm_g", 2), ("k_norm_g", 2), ("c", 8), ("c_ctx", 8)):
    VEC[_name] = (_n, _c)
    _n += _c
NVEC = _n


def shape_constants():
    t = np.arange(P)
    le = (t[:, None] <= t[None, :]).astype(np.float32)
    gt = (t[:, None] > t[None, :]).astype(np.float32)
    rev = lambda m: m[::-1, ::-1]
    cum = np.zeros((LEVELS + 2, P, P), np.float32)
    pair = np.zeros((LEVELS, P, P), np.float32)
    for l in range(LEVELS):
        b = 1 << l
        mid = t // (2 * b) * 2 * b + b
        second = t >= mid
        cum[l] = np.where(second[None, :], (t[:, None] >= mid[None, :]) & (t[:, None] <= t[None, :]),
                          (t[:, None] > t[None, :]) & (t[:, None] < mid[None, :]))
        pair[l] = (mid[:, None] == mid[None, :]) & ~second[:, None] & second[None, :]
    cum[LEVELS], cum[LEVELS + 1] = le, gt
    both = lambda m: np.stack([m, m[:, ::-1, ::-1]])
    col = lambda m: np.ascontiguousarray(np.moveaxis(m, -2, 0)).reshape(P, -1)
    tri = col(np.stack([le, rev(le), gt, rev(gt)]))
    eye = np.eye(P, dtype=np.float32)
    masks = np.concatenate([both(pair), np.broadcast_to(eye, (2, 1, P, P))], axis=1)
    rows = S // 64
    n = 16
    inv = (10000.0 ** (-np.arange(n, dtype=np.float32) / n)).astype(np.float32)
    row = np.repeat(np.arange(rows, dtype=np.float32), 64)[:, None] * inv
    cl = np.tile(np.arange(64, dtype=np.float32), rows)[:, None] * inv
    ang = np.concatenate([row, row, cl, cl], axis=-1).T
    cos = np.concatenate([np.ones((64, CTX), np.float32), np.cos(ang)], axis=1)
    sin = np.concatenate([np.zeros((64, CTX), np.float32), np.sin(ang)], axis=1)
    rot = np.zeros((64, P), np.float32)
    for base in (0, 32):
        for i in range(16):
            rot[base + 16 + i, base + i] = -1.0
            rot[base + i, base + 16 + i] = 1.0
    tt = np.arange(S)
    inv_count = np.stack([1.0 / (np.clip(tt - w // 2 + w, 0, S) - np.clip(tt - w // 2, 0, S)) for w in POOL_W])
    return {
        "k_eye": eye, "k_tri": tri, "k_negpair": col(-both(pair).reshape(-1, P, P)),
        "k_cum": col(both(cum).reshape(-1, P, P)), "k_masks": col(masks.reshape(-1, P, P)).astype(np.float32),
        "k_cos": cos.astype(np.float32), "k_sin": sin.astype(np.float32), "k_rot": rot,
        "k_invcount": inv_count.astype(np.float32),
    }


def build(nc, a, out):
    ctx = ExitStack()
    with ctx:
        sb = lambda name, shape, dt=F32: ctx.enter_context(nc.sbuf_tensor(name, shape, dt))
        sem = lambda name: ctx.enter_context(nc.semaphore(name))

        X = sb("X", [P, ST, D])
        raw = [sb(f"raw{i}", [P, SLAB // 2]) for i in range(2)]
        whi = [sb(f"whi{i}", [P, SLAB], F32R) for i in range(2)]
        wlo = [sb(f"wlo{i}", [P, SLAB], F32R) for i in range(2)]
        with nc.sbuf_tensor("arena", [P, 16384], F32) as arena:
            pass
        ctx_hi = sb("ctx_hi", [P, KT, CTX], F32R)
        ctx_lo = sb("ctx_lo", [P, KT, CTX], F32R)
        sb("arena_rest", [P, 16384 - 2 * KT * CTX])
        eye = sb("eye", [P, P])
        ones = sb("ones", [P, P])
        cols = sb("cols", [P, NVEC])
        convw = sb("convw", [P, CONV * 24])
        stats = sb("stats", [P, ST + CT, 2, 6])
        mv = sb("mv", [P, ST + CT, 2])
        rstd = sb("rstd", [P, ST + CT, 2])
        modc = sb("modc", [P, 16, 2])
        modg = sb("modg", [P, KT, 2])
        csil = sb("csil", [P, 16])
        pause = sb("pause", [P, 16])
        bk = [ctx.enter_context(nc.psum_tensor(f"bk{i}", [P, 512], F32)) for i in range(8)]
        WORK, GATE_W = 17664, 10048
        with nc.sbuf_tensor("act_f", [P, KT, S], F32) as act_f:
            with nc.sbuf_tensor("work", [P, WORK], F32) as work:
                pass
        act_lo = sb("act_lo", [P, KT, S], F32R)
        sb("work_0", [P, GATE_W])
        gate_w = sb("gate_w", [P, 2, KT, 32], F32R)
        sb("work_1", [P, WORK - KT * S - GATE_W - 512])
        act_hi = sb("act_hi", [P, KT, S], F32R)
        hid = arena[:, :].rearrange("p (k s) -> p k s", k=32)
        lnrow = work[:, 11520:13568].rearrange("p (g n) -> p g n", g=2)
        wmod = work[:, 0:8192].rearrange("p (k n) -> p k n", k=KT)

        def carve(tensor, sizes, start=0):
            views, at = {}, start
            for name, *shape in sizes:
                n = int(np.prod(shape))
                v = tensor[:, at:at + n]
                if len(shape) == 2:
                    v = v.rearrange("p (x y) -> p x y", x=shape[0])
                elif len(shape) == 3:
                    v = v.rearrange("p (x y z) -> p x y z", x=shape[0], y=shape[1])
                views[name] = v
                at += n
            assert at <= tensor.shape[1], (at, tensor.shape)
            return views

        def col(name, i=0):
            r = VEC[name][0] + i
            return cols[:, r:r + 1]

        raw_loaded = [sem(f"raw_loaded{i}") for i in range(2)]
        w_hi_ready = sem("w_hi_ready")
        w_ready = sem("w_ready")
        hid_ready = sem("hid_ready")
        stage_hi_ready = sem("stage_hi_ready")
        stage_ready = sem("stage_ready")
        mix_hi_ready = sem("mix_hi_ready")
        mix_ready = sem("mix_ready")
        slab_used = sem("slab_used")
        acc_ready = sem("acc_ready")
        acc_free = sem("acc_free")
        sum_ready = sem("sum_ready")
        sum_added = sem("sum_added")
        x_ready = sem("x_ready")
        xt_ready = sem("xt_ready")
        act_hi_ready = sem("act_hi_ready")
        act_ready = sem("act_ready")
        st_stats = sem("st_stats")
        st_mean = sem("st_mean")
        st_ln = sem("st_ln")
        st_rstd = sem("st_rstd")
        st_center = sem("st_center")
        lnrow_loaded = sem("lnrow_loaded")
        x_loaded = sem("x_loaded")
        const_loaded = sem("const_loaded")
        memset_done = sem("memset_done")
        vec_turned = sem("vec_turned")
        vec_ready = sem("vec_ready")

        FS = {}
        n = 0
        for name in ("a_in", "up0", "b_qk", "b_r", "up1", "c_in"):
            FS[name] = n
            n += PH[name][1]
        TH = {}
        n = 0
        for name in ("a_out", "down0", "b_v", "b_out", "down1", "c_out"):
            TH[name] = n
            n += 2

        def slab_source(name, k2, b):
            w, c0 = {"a_in": (a["a_w_in"][0], 0), "up0": (a["mlp_w1"][0], 0), "up1": (a["mlp_w1"][1], 0),
                     "b_qk": (a["b_w_in"][0], 0), "b_r": (a["b_w_in"][0], 2048), "c_in": (a["w_in_2"][0], -64)}[name]
            return w[:, bass.ds(k2 * 512 + (b * 256 + c0), 256)].rearrange("(k p) n -> p k n", p=P)

        def tok_source(name, half, k2, b):
            w, c0 = {"a_out": (a["a_w_out"][0], 0), "b_out": (a["b_w_out"][0], 0), "c_out": (a["w_out_2"][0], 0),
                     "down0": (a["mlp_w2"][0], 0), "down1": (a["mlp_w2"][1], 0), "b_v": (a["b_w_in"][0], 1024)}[name]
            return w[bass.ds(k2 * 1024 + b * 512, 512), c0 + half * 512:c0 + half * 512 + 512].rearrange(
                "(k p) n -> p k n", p=P)

        def slab_view(t, kts):
            return t[:, :].rearrange("p (k n) -> p k n", k=kts)

        def load_slab(sp, k, b, source, kts=KT):
            for hf in range(2):
                if not (isinstance(k, int) and k == 0 and b == 0):
                    sp.wait_ge(w_ready, k * 4 + (2 * b - 1 + hf))
                ks = slice(hf * kts // 2, (hf + 1) * kts // 2)
                sp.dma_start(slab_view(raw[hf], kts // 2)[:, :, 0:source.shape[2]], source[:, ks, :]
                             ).then_inc(raw_loaded[hf], 16)

        def split_hi(act, k, b):
            for hf in range(2):
                act.wait_ge(raw_loaded[hf], k * 32 + (16 * b + 16))
                if hf == 0 and not (isinstance(k, int) and k == 0):
                    act.wait_ge(slab_used, k * 2 + (b - 1))
                hs = slice(hf * SLAB // 2, (hf + 1) * SLAB // 2)
                nc.scalar.activation(whi[b][:, hs], raw[hf][:, :], ACT.Copy).then_inc(w_hi_ready, 1)

        def split_lo(dve, k, b):
            for hf in range(2):
                dve.wait_ge(w_hi_ready, k * 4 + (2 * b + hf + 1))
                hs = slice(hf * SLAB // 2, (hf + 1) * SLAB // 2)
                nc.vector.tensor_tensor(wlo[b][:, hs], raw[hf][:, :], whi[b][:, hs], ALU.subtract).then_inc(w_ready, 1)

        def next_pair(name, k2):
            return k2 + (PH[name][0] // 2 + 1)

        def mm3(acc, lhs_hi, lhs_lo, rhs_hi, rhs_lo, first, last):
            nc.tensor.matmul(acc, lhs_hi, rhs_hi, start=first, stop=False, skip_group_check=True)
            nc.tensor.matmul(acc, lhs_hi, rhs_lo, start=False, stop=False, skip_group_check=True)
            return nc.tensor.matmul(acc, lhs_lo, rhs_hi, start=False, stop=last, skip_group_check=True)

        def pe_feature_slab(pe, name, k2, b, width=256):
            pe.wait_ge(w_ready, k2 * 4 + 2 * (PH[name][0] + b + 1))
            hi, lo = slab_view(whi[b], KT), slab_view(wlo[b], KT)
            for j in range(2):
                if not (isinstance(k2, int) and 2 * FS[name] + 4 * k2 + 2 * b + j < 4):
                    pe.wait_ge(acc_free, k2 * 4 + (2 * FS[name] + 2 * b + j - 3))
                m = min(P, width - j * P)
                c = slice(j * P, j * P + m)
                for kt in range(KT):
                    mm = mm3(bk[2 * b + j][0:m, :], hi[:, kt, c], lo[:, kt, c], act_hi[:, kt, :], act_lo[:, kt, :],
                             kt == 0, kt == KT - 1)
                mm.then_inc(acc_ready if j == 0 else slab_used, 1)

        def wait_tile(eng, name, k2, b, j):
            if j == 0:
                eng.wait_ge(acc_ready, k2 * 2 + (FS[name] + b + 1))
            else:
                eng.wait_ge(slab_used, k2 * 2 + (PH[name][0] + b + 1))

        def pe_token_slab(pe, name, half, k2, b, pair0, first, last):
            pe.wait_ge(w_ready, k2 * 4 + 2 * (PH[name][0] + 2 * pair0 + b + 1))
            if PH[name][1] > 4:
                pe.wait_ge(stage_ready, k2 * 2 + (STAGED[name] + 2 * pair0 + b + 1))
            elif name in MIXED and half == 0:
                pe.wait_ge(mix_ready, MIXED[name] + 4 * b + 4)
            hi, lo = slab_view(whi[b], 4), slab_view(wlo[b], 4)
            for st in range(ST):
                tok = slice(st * P, st * P + P)
                for kt in range(4):
                    f = b * 4 + kt
                    mm = mm3(bk[4 * half + st][:, :], act_hi[:, f, tok], act_lo[:, f, tok], hi[:, kt, :], lo[:, kt, :],
                             first and kt == 0, last and kt == 3)
                if st == 3:
                    mm.then_inc(slab_used, 1)
                elif last:
                    mm.then_inc(sum_ready, 1)

        def wait_sum(eng, name, half, st):
            if st < 3:
                eng.wait_ge(sum_ready, 3 * (TH[name] + half) + st + 1)
            else:
                eng.wait_ge(slab_used, PH[name][0] + PH[name][1] // 2 * (half + 1))

        STAGED = {"down0": 0, "down1": 16}
        MIXED = {"a_out": 0, "b_out": 8, "c_out": 16}

        def pe_token_layer(pe, name):
            pairs = PH[name][1] // 4
            for half in range(2):
                pair0 = half * pairs
                if pairs == 1:
                    pe_token_slab(pe, name, half, 0, 0, pair0, True, False)
                    pe_token_slab(pe, name, half, 0, 1, pair0, False, True)
                    continue
                for b in range(2):
                    pe_token_slab(pe, name, half, 0, b, pair0, b == 0, False)
                with pe.Fori(1, pairs - 1) as k2:
                    for b in range(2):
                        pe_token_slab(pe, name, half, k2, b, pair0, False, False)
                for b in range(2):
                    pe_token_slab(pe, name, half, pairs - 1, b, pair0, False, b == 1)

        def pe_turn(pe, e, half0_moved=None):
            if half0_moved is not None:
                pe.wait_ge(sum_added, half0_moved)
            for st in range(ST):
                pe.wait_ge(x_ready, 4 * (e - 1) + st + 1)
                for hf in range(2):
                    if st >= 2:
                        pe.wait_ge(act_ready, 8 * e + 2 * (st - 2) + hf + 1)
                    for k in range(4):
                        kt = 4 * hf + k
                        mm = nc.tensor.transpose(bk[2 * (st % 2) + hf][:, k * P:k * P + P],
                                                 X[:, st, kt * P:kt * P + P], eye[:, :])
                    mm.then_inc(xt_ready, 1)

        def act_turned(act, e, tiles=range(ST)):
            for st in tiles:
                for hf in range(2):
                    act.wait_ge(xt_ready, 8 * e + 2 * st + hf + 1)
                    nc.scalar.activation(act_hi[:, 4 * hf:4 * hf + 4, st * P:st * P + P],
                                         bk[2 * (st % 2) + hf][:, :].rearrange("p (k s) -> p k s", k=4),
                                         ACT.Copy).then_inc(act_hi_ready, 1)

        def dve_turned(dve, e, st):
            for hf in range(2):
                dve.wait_ge(act_hi_ready, 8 * e + 2 * st + hf + 1)
                c = (slice(None), slice(4 * hf, 4 * hf + 4), slice(st * P, st * P + P))
                nc.vector.tensor_tensor(act_lo[c], bk[2 * (st % 2) + hf][:, :].rearrange("p (k s) -> p k s", k=4),
                                        act_hi[c], ALU.subtract).then_inc(act_ready, 1)

        def dve_add_half(dve, name, half, st):
            wait_sum(dve, name, half, st)
            xs = X[:, st, half * 512:half * 512 + 512]
            nc.vector.scalar_tensor_tensor(out=xs, in0=xs, scalar=ALPHA, in1=bk[4 * half + st][:, :],
                                           op0=ALU.mult, op1=ALU.add).then_inc(sum_added, 1)

        def dve_norm(dve, name, e):
            done = 4 * TH[name]
            def finish(st):
                dve.wait_ge(st_rstd, 4 * (e - 1) + st + 1)
                if st == 0:
                    dve.wait_ge(lnrow_loaded, 32 * e)
                nc.vector.scalar_tensor_tensor(out=X[:, st, :], in0=X[:, st, :], scalar=mv[:, st, 0:1],
                                               in1=lnrow[:, 0, :], op0=ALU.subtract, op1=ALU.mult).then_inc(st_center, 1)
                dve.wait_ge(st_center, 4 * (e - 1) + st + 1)
                nc.vector.scalar_tensor_tensor(out=X[:, st, :], in0=X[:, st, :], scalar=rstd[:, st, 1:2],
                                               in1=lnrow[:, 1, :], op0=ALU.mult, op1=ALU.add).then_inc(x_ready, 1)
            for st in range(ST):
                dve_add_half(dve, name, 1, st)
                dve.wait_ge(sum_added, done + 4 + st + 1)
                nc.vector.bn_stats(stats[:, st, 1, :], X[:, st, 512:1024]).then_inc(st_stats, 1)
                dve.wait_ge(st_stats, 8 * (e - 1) + 4 + st + 1)
                nc.vector.bn_aggr(mv[:, st, :], stats[:, st, :, :]).then_inc(st_mean, 1)
                if st >= 1:
                    finish(st - 1)
                if st >= 2 and e < 4:
                    dve_turned(dve, e, st - 2)
            finish(3)
            if e < 4:
                dve_turned(dve, e, 2)
                dve_turned(dve, e, 3)

        def act_norm(act, e):
            for st in range(ST):
                act.wait_ge(st_mean, 4 * (e - 1) + st + 1)
                nc.scalar.activation(rstd[:, st, 0:1], mv[:, st, 1:2], ACT.Ln, bias=LN_EPS).then_inc(st_ln, 1)
                act.wait_ge(st_ln, 4 * (e - 1) + st + 1)
                nc.scalar.activation(rstd[:, st, 1:2], rstd[:, st, 0:1], ACT.Exp, scale=-0.5).then_inc(st_rstd, 1)
                if st >= 2 and e < 4:
                    act_turned(act, e, [st - 2])
            if e < 4:
                act_turned(act, e, [2, 3])

        def stage(t, b):
            return t[:, 4 * b:4 * b + 4, :]

        def hid_group(pair, b):
            return hid[:, bass.ds(pair * 8 + 4 * b, 4), :]

        def act_stage(act, b, pair):
            nc.scalar.activation(stage(act_hi, b), hid_group(pair, b), ACT.Copy).then_inc(stage_hi_ready, 1)

        def dve_stage(dve, name, k, b, pair):
            dve.wait_ge(stage_hi_ready, k * 2 + (STAGED[name] + b + 1))
            gap(dve)
            nc.vector.tensor_tensor(stage(act_lo, b), hid_group(pair, b), stage(act_hi, b), ALU.subtract
                                    ).then_inc(stage_ready, 1)

        def act_token_steps(act, name, k2, pair):
            for b in range(2):
                split_hi(act, next_pair(name, k2), b)
                gap(act)
                act_stage(act, b, pair)

        def dve_token_steps(dve, name, k2, pair):
            for b in range(2):
                split_lo(dve, next_pair(name, k2), b)
                dve_stage(dve, name, k2 + 1, b, pair)

        def act_token_layer(act, name, e):
            n = PH[name][1]
            if n > 4:
                act.wait_ge(slab_used, PH[name][0])
                act.wait_ge(hid_ready, STAGED[name] * 2 + 32)
                for b in range(2):
                    act_stage(act, b, 0)
                with act.Fori(0, 3) as k2:
                    act_token_steps(act, name, k2, k2 + 1)
                act_token_steps(act, name, 3, 0)
                with act.Fori(4, 7) as k2:
                    act_token_steps(act, name, k2, k2 - 3)
            else:
                for b in range(2):
                    split_hi(act, next_pair(name, 0), b)
            split_hi(act, next_pair(name, n // 2 - 1), 0)
            act_norm(act, e)
            split_hi(act, next_pair(name, n // 2 - 1), 1)

        def dve_token_layer(dve, name, e):
            n = PH[name][1]
            if n > 4:
                for b in range(2):
                    dve_stage(dve, name, 0, b, 0)
                with dve.Fori(0, 3) as k2:
                    dve_token_steps(dve, name, k2, k2 + 1)
                dve_token_steps(dve, name, 3, 0)
            else:
                for b in range(2):
                    split_lo(dve, next_pair(name, 0), b)
            for st in range(ST):
                dve_add_half(dve, name, 0, st)
            dve.wait_ge(sum_added, 4 * TH[name] + 4)
            for st in range(ST):
                nc.vector.bn_stats(stats[:, st, 0, :], X[:, st, 0:512]).then_inc(st_stats, 1)
            if n > 4:
                with dve.Fori(4, 7) as k2:
                    dve_token_steps(dve, name, k2, k2 - 3)
            split_lo(dve, next_pair(name, n // 2 - 1), 0)
            dve_norm(dve, name, e)
            split_lo(dve, next_pair(name, n // 2 - 1), 1)

        def act_mixed(act, done, value, name):
            act.wait_ge(done, value)
            for k in range(KT):
                nc.scalar.activation(act_hi[:, k, :], act_f[:, k, :], ACT.Copy).then_inc(mix_hi_ready, 1)

        def dve_mixed(dve, name):
            for k in range(KT):
                dve.wait_ge(mix_hi_ready, MIXED[name] + k + 1)
                nc.vector.tensor_tensor(act_lo[:, k, :], act_f[:, k, :], act_hi[:, k, :], ALU.subtract).then_inc(mix_ready, 1)

        def sp_feature(sp, name, first=0):
            with sp.Fori(first, PH[name][1] // 2) as k2:
                for b in range(2):
                    load_slab(sp, k2 + PH[name][0] // 2, b, slab_source(name, k2, b))

        def sp_token(sp, name):
            pairs = PH[name][1] // 4
            for half in range(2):
                if pairs == 1:
                    for b in range(2):
                        load_slab(sp, PH[name][0] // 2 + half, b, tok_source(name, half, 0, b), 4)
                else:
                    with sp.Fori(0, pairs) as k2:
                        for b in range(2):
                            load_slab(sp, k2 + (PH[name][0] // 2 + half * pairs), b, tok_source(name, half, k2, b), 4)

        a_qkvT = arena[:, 0:12288].rearrange("p (n s) -> p n s", n=24)
        a_zT = arena[:, 12288:16384].rearrange("p (n s) -> p n s", n=AH)
        A = carve(work, [("tri", 4, P), ("negpair", 14, P), ("beta17", ST, 17), ("g17", ST, 17), ("bexp", ST, 16),
                         ("kdec", ST, 16), ("glast", ST, 16), ("t1", ST, 16), ("t2", ST, 16), ("gh", ST, 2),
                         ("sq", 2, S), ("rs", 2, S), ("qn", S), ("kn", S), ("vst", S), ("ktok", ST, P),
                         *[(f"{n}{d}", ST, P) for d in range(2) for n in ("GL", "GG", "A", "PT", "qd", "kbe", "kd",
                                                                          "vb", "X", "Y")],
                         ("vn0", P), ("vn1", P), ("S0", P), ("S1", P)])
        A["g"], A["beta"] = A["g17"][:, :, 0:16], A["beta17"][:, :, 0:16]
        a_tiles = arena[:, :].rearrange("p (n s) -> p n s", n=32)
        CB = carve(work, [("cbuf", 4, S + 4), ("cacc", 4, S)], start=2776)
        gwv = carve(work, [("raw", KT, 32), ("dt", 16), ("alog", 16), ("ea", 16)],
                    start=9600)
        gw_raw = gwv["raw"]
        gw_hi, gw_lo = gate_w[:, 0], gate_w[:, 1]
        vrow = carve(work, [("conv", P), ("vec", P)], start=7000)

        def bc_tok(t):
            return t.broadcast_to([P, ST, P])

        def bc_mat(t):
            return t.unsqueeze(1).broadcast_to([P, ST, P])

        def chunks(b):
            return b[:, :].rearrange("p (c s) -> p c s", c=ST)

        conv_step = sem("conv_step")
        conv_silu = sem("conv_silu")
        G = {n: sem("g_" + n) for n in (
            "w_loaded w_hi w_ready gate_mm gate_exp beta1 beta2 logit absd expd softplus1 softplus g "
            "cum_mm cum_exp bexp l2_sq l2_sum l2_ln l2_rs qkn v_copied turned k_tok kk gl decay_mm decay_exp pt_mask "
            "vb ed a pt qd kx p1 t2 p2 y0 y turned_y x w_mm w pv vn ps s o_done o_sq o_sum o_ln o_rs of1 "
            "o_out pad g_head").split()}

        def sp_start(sp):
            for b in range(2):
                load_slab(sp, 0, b, slab_source("a_in", 0, b))

        def act_start(act):
            for st in range(ST):
                act.dma_start(X[:, st, :], a["x"][0, st * P:st * P + P, :]).then_inc(x_loaded, 16)

        NCONST = 4
        def pool_start(pool):
            pool.dma_start(eye[:, :], a["k_eye"]).then_inc(eye_loaded, 16)
            nc.gpsimd.memset(vrow["vec"], 0.0).then_inc(memset_done, 1)
            nc.gpsimd.memset(ones[:, :], 1.0).then_inc(memset_done, 1)
            nc.gpsimd.memset(CB["cbuf"], 0.0).then_inc(memset_done, 1)
            nc.gpsimd.memset(mv[:, :, :], 0.0).then_inc(B["exp"], 3)
            nc.gpsimd.memset(rstd[:, :, :], 0.0).then_inc(B["st"], 2)
            credits = ((G["o_out"], 1), (G["o_done"], 1), (B["o_out"], 2), (B["o_done"], 1), (B["e_mm"], 1), (HT.sem, 1), (HV.sem, 1))
            for i, (s, n) in enumerate(credits):
                nc.gpsimd.memset(pause[:, 8 + i:9 + i], 0.0).then_inc(s, n)
            pool.dma_start(vrow["conv"][0:CONV * 24, :], a["a_conv"][0].rearrange("k (n p) -> (k n) p", p=P)
                           ).then_inc(const_loaded, 16)
            pool.dma_start(gw_raw, a["a_w_in"][0, :, 4096:4128].rearrange("(k p) n -> p k n", p=P)).then_inc(const_loaded, 16)
            pool.dma_start(A["tri"], a["k_tri"].rearrange("p (m s) -> p m s", m=4)).then_inc(const_loaded, 16)
            pool.dma_start(A["negpair"], a["k_negpair"].rearrange("p (m s) -> p m s", m=14)).then_inc(const_loaded, 16)
            pool.dma_start(gwv["dt"], a["a_dt_bias"][0].rearrange("d h -> (d h)").partition_broadcast(P)
                           ).then_inc(G["w_loaded"], 16)
            pool.dma_start(gwv["alog"], a["a_alog"][0].rearrange("d h -> (d h)").partition_broadcast(P)
                           ).then_inc(G["w_loaded"], 16)
            pool.wait_ge(memset_done, 1)
            rows = [("norm_g", a["norm_g_2"][0]), ("b_mod", a["b_mod_2"][0, 0:2048]), ("pool_scale", a["pool_scale_2"][0]),
                    ("q_lora_g", a["q_lora_g_2"][0]), ("kv_lora_g", a["kv_lora_g_2"][0]), ("a_norm_g", a["a_norm_g"][0]),
                    ("b_norm_g", a["b_norm_g"][0]), ("c", a["c_2"][0]), ("c_ctx", a["c_ctx_2"])]
            for name, v in rows:
                r, n = VEC[name]
                pool.dma_start(vrow["vec"][r:r + n, :], v.rearrange("(n p) -> n p", p=P)).then_inc(vec_loaded, 16)
            for name in ("q_norm_g", "k_norm_g"):
                r, v = VEC[name][0], a[name + "_2"]
                pool.dma_start(vrow["vec"][r:r + 1, :], v[:, 0:P]).then_inc(vec_loaded, 16)
                pool.dma_start(vrow["vec"][r + 1:r + 2, 0:64], v[:, P:QK_DIM]).then_inc(vec_loaded, 16)
        vec_loaded = sem("vec_loaded")
        eye_loaded = sem("eye_loaded")
        NV_DMA = 13

        def pe_start(pe):
            pe.wait_ge(eye_loaded, 16)
            for st in range(ST):
                pe.wait_ge(x_loaded, 16 * (st + 1) if st == 3 else 64)
                for hf in range(2):
                    if st >= 2:
                        pe.wait_ge(act_ready, 2 * (st - 2) + hf + 1)
                    for k in range(4):
                        kt = 4 * hf + k
                        mm = nc.tensor.transpose(bk[2 * (st % 2) + hf][:, k * P:k * P + P],
                                                 X[:, st, kt * P:kt * P + P], eye[:, :])
                    mm.then_inc(xt_ready, 1)
            pe.wait_ge(const_loaded, 16 * NCONST)
            nc.tensor.transpose(bk[4][:, 0:CONV * 24], vrow["conv"][0:CONV * 24, :], eye[0:CONV * 24, 0:CONV * 24]
                                ).then_inc(vec_turned, 1)
            pe.wait_ge(vec_loaded, 16 * NV_DMA)
            nc.tensor.transpose(bk[5][:, 0:NVEC], vrow["vec"][0:NVEC, :], eye[0:NVEC, 0:NVEC]).then_inc(vec_turned, 1)

        def dve_start(dve):
            split_lo(dve, 0, 0)
            for st in range(ST):
                dve_turned(dve, 0, st)
            split_lo(dve, 0, 1)
            dve.wait_ge(G["w_hi"], 1)
            nc.vector.tensor_tensor(gw_lo, gw_raw, gw_hi, ALU.subtract).then_inc(G["w_ready"], 1)
            dve.wait_ge(vec_turned, 1)
            nc.vector.tensor_copy(convw[:, :], bk[4][:, 0:CONV * 24]).then_inc(vec_ready, 1)
            dve.wait_ge(vec_turned, 2)
            nc.vector.tensor_copy(cols[:, :], bk[5][:, 0:NVEC]).then_inc(vec_ready, 1)
            dve.wait_ge(vec_ready, 2)

        def log_exp_table():
            nc.scalar.preload_act_table_set("natural_log_exp_and_others")

        def act_begin(act):
            split_hi(act, 0, 0)
            act_turned(act, 0)
            split_hi(act, 0, 1)
            act.wait_ge(const_loaded, 16 * NCONST)
            nc.scalar.activation(gw_hi, gw_raw, ACT.Copy).then_inc(G["w_hi"], 1)
            act.wait_ge(memset_done, 3)
            act.wait_ge(vec_ready, 2)
            r = VEC["c"][0]
            nc.scalar.activation(csil[:, :], cols[:, r:r + 16], ACT.Silu).then_inc(vec_ready, 1)

        def pe_a_in(pe):
            pe.wait_ge(act_ready, 8)
            for b in range(2):
                pe_feature_slab(pe, "a_in", 0, b)
                if b == 0:
                    pe_a_gates(pe)
            with pe.Fori(1, 7) as k2:
                for b in range(2):
                    pe_feature_slab(pe, "a_in", k2, b)
            pe_a_norms(pe, 0, 0)
            pe_feature_slab(pe, "a_in", 7, 0)
            pe_a_decay_sums(pe)
            pe_feature_slab(pe, "a_in", 7, 1)
            pe.wait_ge(acc_free, 32)
            pe_a_products(pe, 0, 0)

        def act_a_in(act):
            def conv_pair(k2, b):
                for j in range(2):
                    wait_tile(act, "a_in", k2, b, j)
                    if not isinstance(k2, int):
                        act.wait_ge(conv_step, k2 * 20 + (10 * b - 10))
                    nc.scalar.activation(CB["cbuf"][:, 2 * b + j, 2:2 + S], bk[2 * b + j][:, :], ACT.Copy).then_inc(acc_free, 1)
                split_hi(act, next_pair("a_in", k2), b)
                for j in range(2):
                    act.wait_ge(conv_step, k2 * 20 + (10 * b + 9 + j))
                    nc.scalar.activation(a_qkvT[:, bass.ds(k2 * 4 + (2 * b + j), 1), :].squeeze(1), CB["cacc"][:, 2 * b + j, :],
                                         ACT.Silu).then_inc(conv_silu, 1)
            for b in range(2):
                conv_pair(0, b)
            with act.Fori(1, 6) as k2:
                for b in range(2):
                    conv_pair(k2, b)
            act_a_squares(act, 0, 0)
            for k2 in (6, 7):
                if k2 == 7:
                    act_a_rsqrt(act, 0, 0)
                for b in range(2):
                    for j in range(2):
                        wait_tile(act, "a_in", k2, b, j)
                        nc.scalar.activation(a_zT[:, k2 * 4 + (2 * b + j - 24), :], bk[2 * b + j][:, :],
                                             ACT.Silu).then_inc(acc_free, 1)
                    split_hi(act, next_pair("a_in", k2), b)

        def dve_a_in(dve):
            def conv_pair(k2, b):
                for k in range(CONV):
                    for j in range(2):
                        src = CB["cbuf"][:, 2 * b + j, k:k + S]
                        acc = CB["cacc"][:, 2 * b + j, :]
                        wk = convw[:, bass.ds(k2 * 4 + (k * 24 + 2 * b + j), 1)]
                        if k == 0:
                            dve.wait_ge(acc_free, k2 * 4 + (2 * b + j + 1))
                            if not isinstance(k2, int):
                                dve.wait_ge(conv_silu, k2 * 4 + (2 * b + j - 3))
                            nc.vector.tensor_scalar(acc, src, wk, None, ALU.mult).then_inc(conv_step, 1)
                        else:
                            dve.wait_ge(conv_step, k2 * 20 + (10 * b + 2 * k + j - 1))
                            nc.vector.scalar_tensor_tensor(out=acc, in0=src, scalar=wk, in1=acc, op0=ALU.mult,
                                                           op1=ALU.add).then_inc(conv_step, 1)
                split_lo(dve, next_pair("a_in", k2), b)
            for b in range(2):
                conv_pair(0, b)
            with dve.Fori(1, 6) as k2:
                for b in range(2):
                    conv_pair(k2, b)
            for k2 in (6, 7):
                if k2 == 7:
                    dve_a_norms(dve, 0, 0)
                for b in range(2):
                    split_lo(dve, next_pair("a_in", k2), b)

        def pe_a_gates(pe):
            pe.wait_ge(G["w_ready"], 1)
            pe.wait_ge(vec_ready, 2)
            for st in range(ST):
                for kt in range(KT):
                    tok = slice(st * P, st * P + P)
                    mm = mm3(bk[4][:, st * 32:st * 32 + 32], act_hi[:, kt, tok], act_lo[:, kt, tok],
                             gw_hi[:, kt, :], gw_lo[:, kt, :], kt == 0, kt == KT - 1)
            mm.then_inc(G["gate_mm"], 1)

        def pe_a_decay_sums(pe):
            pe.wait_ge(G["g"], 1)
            gates = bk[7][:, 0:192].rearrange("p (k c n) -> p k c n", k=3, c=ST)
            for d in range(2):
                dd = slice(8 * d, 8 * d + 8)
                nc.tensor.matmul(gates[:, 0, :, dd], A["tri"][:, d, :], A["g"][:, :, dd], start=True, stop=True, skip_group_check=True)
                nc.tensor.matmul(gates[:, 1, :, dd], A["tri"][:, 2 + d, :], A["g"][:, :, dd], start=True, stop=True, skip_group_check=True)
            nc.tensor.matmul(gates[:, 2, :, :], ones[:, :], A["g"], start=True, stop=True, skip_group_check=True
                             ).then_inc(G["cum_mm"], 1)

        def act_a_gates(act):
            logits = bk[4][:, 0:128].rearrange("p (c n) -> p c n", c=ST)
            log_exp_table()
            act.wait_ge(G["gate_mm"], 1)
            nc.scalar.activation(A["beta"], logits[:, :, 0:16], ACT.Exp, scale=-1.0).then_inc(G["gate_exp"], 1)
            act.wait_ge(G["w_loaded"], 32)
            nc.scalar.activation(gwv["ea"], gwv["alog"], ACT.Exp).then_inc(G["gate_exp"], 1)
            act.wait_ge(G["logit"], 1)
            nc.scalar.activation(A["t2"], A["t1"], ACT.Abs).then_inc(G["absd"], 1)
            act.wait_ge(G["absd"], 1)
            nc.scalar.activation(A["t2"], A["t2"], ACT.Exp, scale=-1.0).then_inc(G["expd"], 1)
            act.wait_ge(G["expd"], 1)
            nc.scalar.activation(A["t2"], A["t2"], ACT.Ln, bias=1.0).then_inc(G["softplus1"], 1)

        def act_a_decays(act):
            gates = bk[7][:, 0:192].rearrange("p (k c n) -> p k c n", k=3, c=ST)
            act.wait_ge(G["cum_mm"], 1)
            for k, n in enumerate(("bexp", "kdec", "glast")):
                nc.scalar.activation(A[n], gates[:, k, :, :], ACT.Exp).then_inc(G["cum_exp"], 1)

        def dve_a_gates(dve):
            logits = bk[4][:, 0:128].rearrange("p (c n) -> p c n", c=ST)
            dve.wait_ge(G["gate_exp"], 1)
            dve.wait_ge(G["w_loaded"], 32)
            nc.vector.tensor_tensor(A["t1"], logits[:, :, 16:32], gwv["dt"].unsqueeze(1).broadcast_to([P, ST, 16]),
                                    ALU.add).then_inc(G["logit"], 1)
            dve.wait_ge(G["gate_exp"], 2)
            nc.vector.tensor_scalar(A["beta"], A["beta"], 1.0, None, ALU.add).then_inc(G["beta1"], 1)
            dve.wait_ge(G["beta1"], 1)
            nc.vector.reciprocal(A["beta"], A["beta"]).then_inc(G["beta2"], 1)
            dve.wait_ge(G["softplus1"], 1)
            nc.vector.scalar_tensor_tensor(out=A["t1"], in0=A["t1"], scalar=0.0, in1=A["t2"], op0=ALU.max,
                                           op1=ALU.add).then_inc(G["softplus"], 1)
            dve.wait_ge(G["softplus"], 1)
            nc.vector.scalar_tensor_tensor(out=A["g"], in0=A["t1"], scalar=-1.0,
                                           in1=gwv["ea"].unsqueeze(1).broadcast_to([P, ST, 16]), op0=ALU.mult,
                                           op1=ALU.mult).then_inc(G["g"], 1)

        def dve_a_decays(dve):
            dve.wait_ge(G["cum_exp"], 3)
            dve.wait_ge(G["beta2"], 1)
            nc.vector.tensor_tensor(A["bexp"], A["bexp"], A["beta"], ALU.mult).then_inc(G["bexp"], 1)

        def chunk_of(cc, d):
            return cc if d == 0 else ST - 1 - cc

        def later(t, l, d):
            if len(t.shape) == 3:
                return t.rearrange("p c (n t b) -> p c n t b", t=2, b=1 << l)[:, :, :, 1 - d, :]
            return t.rearrange("p (n t b) -> p n t b", t=2, b=1 << l)[:, :, 1 - d, :]

        def pe_a_norms(pe, h, ahead):
            for i in range(2):
                pe.wait_ge(G["l2_sq"], h * 2 + (2 * ahead + i + 1))
                nc.tensor.matmul(bk[4 + i][:, :], ones[:, :], A["sq"][:, i, :], start=True, stop=True).then_inc(G["l2_sum"], 1)

        def pe_a_products(pe, h, ahead):
            pe.wait_ge(G["qkn"], h * 2 + (2 * ahead + 1))
            for c in range(ST):
                mm = nc.tensor.transpose(bk[1][:, c * P:c * P + P], A["kn"][:, c * P:c * P + P], eye[:, :])
            mm.then_inc(G["turned"], 1)
            pe.wait_ge(G["v_copied"], h + (ahead + 1))
            for c in range(ST):
                mm = nc.tensor.transpose(bk[3][:, c * P:c * P + P], A["vst"][:, c * P:c * P + P], eye[:, :])
            mm.then_inc(G["turned"], 1)
            for bank, r in ((4, "kn"), (5, "qn")):
                if r == "qn":
                    pe.wait_ge(G["qkn"], h * 2 + (2 * ahead + 2))
                for c in range(ST):
                    cs = slice(c * P, c * P + P)
                    mm = nc.tensor.matmul(bk[bank][:, cs], A["kn"][:, cs], A[r][:, cs], start=True, stop=True, skip_group_check=True)
                mm.then_inc(G["kk"], 1)

        def pe_a_head(pe, h):
            pe.wait_ge(G["k_tok"], h + 1)
            pe.wait_ge(G["vb"], h * 2 + 2)
            pe.wait_ge(G["gl"], h * 4 + 4)
            for k, (lhs, rhs) in enumerate(((lambda d: A["tri"][:, d, :], "GG"), (lambda d: A["tri"][:, 2 + d, :], "GL"),
                                            (lambda d: ones[:, :], "GL"))):
                if k == 2:
                    pe.wait_ge(G["o_out"], h + 1)
                for d in range(2):
                    bank = (2 * d + 1, 2 * d, 6 + d)[k]
                    nc.tensor.matmul(bk[bank][:, :], lhs(d), A[f"{rhs}{d}"], start=True, stop=True).then_inc(G["decay_mm"], 1)

            def product(l, d):
                if l == 0:
                    pe.wait_ge(G["a"], h * 2 + (d + 1))
                    if d == 0:
                        pe.wait_ge(G["decay_exp"], h * 6 + 4)
                else:
                    pe.wait_ge(G["y"], h * 14 + (2 * (l - 1) + d + 1))
                for c in range(ST):
                    cs = slice(c * P, c * P + P)
                    if l == 0:
                        mm = nc.tensor.transpose(bk[2 * d][:, cs], A[f"A{d}"][:, c, :], eye[:, :])
                    else:
                        mm = nc.tensor.matmul(later(bk[2 * d][:, cs], l, d), A[f"A{d}"][:, c, :], later(A[f"Y{d}"][:, c, :], l, d),
                                              start=True, stop=True, skip_group_check=True)
                mm.then_inc(G["p1"], 1)

            for d in range(2):
                product(0, d)
            for l in range(LEVELS):
                if l > 0:
                    for d in range(2):
                        pe.wait_ge(G["t2"], h * 12 + (2 * (l - 1) + d + 1))
                        pe.wait_ge(G["x"], h * 12 + (2 * (l - 1) + d + 1))
                        for c in range(ST):
                            mm = nc.tensor.matmul(later(bk[2 * d + 1][:, c * P:c * P + P], l, d), A[f"X{d}"][:, c, :],
                                                  later(A[f"GG{d}"][:, c, :], l, d),
                                                  start=True, stop=True, skip_group_check=True)
                        mm.then_inc(G["p2"], 1)
                if l == 3:
                    pe.wait_ge(G["pt"], h * 2 + 2)
                    pe_a_norms(pe, h, 1)
                if l < LEVELS - 1:
                    for d in range(2):
                        pe.wait_ge(G["y"], h * 14 + (2 * l + d + 1))
                        for c in range(ST):
                            mm = nc.tensor.transpose(bk[2 * d + 1][:, c * P:c * P + P], A[f"Y{d}"][:, c, :], eye[:, :])
                        mm.then_inc(G["turned_y"], 1)
                        product(l + 1, d)
            pe.wait_ge(G["kx"], h * 4 + 4)
            for d in range(2):
                pe.wait_ge(G["y"], h * 14 + (2 * (LEVELS - 1) + d + 1))
                for c in range(ST):
                    mm = nc.tensor.matmul(bk[2 * d][:, c * P:c * P + P], A[f"kbe{d}"][:, c, :], A[f"Y{d}"][:, c, :],
                                          start=True, stop=True, skip_group_check=True)
                mm.then_inc(G["w_mm"], 1)
            pe.wait_ge(G["pt"], h * 2 + 2)
            pe.wait_ge(G["qd"], h * 2 + 2)
            for cc in range(ST):
                for d in range(2):
                    c = chunk_of(cc, d)
                    if cc == 0:
                        pe.wait_ge(G["w"], h * 2 + (d + 1))
                    mm = nc.tensor.matmul(bk[2 * d][:, 0:P], A[f"Y{d}"][:, c, :], A[f"vb{d}"][:, c, :], start=True,
                                          stop=cc == 0, skip_group_check=True)
                    if cc > 0:
                        pe.wait_ge(G["s"], h * 6 + (2 * (cc - 1) + d + 1))
                        mm = nc.tensor.matmul(bk[2 * d][:, 0:P], A[f"X{d}"][:, c, :], A[f"S{d}"], start=False,
                                              stop=True, skip_group_check=True)
                    mm.then_inc(G["pv"], 1)
                for d in range(2):
                    c = chunk_of(cc, d)
                    cs = slice(c * P, c * P + P)
                    if cc > 0:
                        nc.tensor.matmul(bk[6][:, cs], A[f"S{d}"], A[f"qd{d}"][:, c, :], start=False, stop=False,
                                         skip_group_check=True)
                    pe.wait_ge(G["vn"], h * 8 + (2 * cc + d + 1))
                    mm = nc.tensor.matmul(bk[6][:, cs], A[f"vn{d}"], A[f"PT{d}"][:, c, :], start=cc == 0 and d == 0,
                                          stop=cc == 3, skip_group_check=True)
                    if cc < 3:
                        mm = nc.tensor.matmul(bk[2 * d + 1][:, 0:P], A[f"kd{d}"][:, c, :], A[f"vn{d}"], start=True,
                                              stop=True, skip_group_check=True)
                        mm.then_inc(G["ps"], 1)
                    elif d == 1:
                        mm.then_inc(G["o_done"], 1)
            pe_a_products(pe, h, 1)
            pe.wait_ge(G["o_sq"], h + 1)
            nc.tensor.matmul(bk[7][:, :], ones[:, :], head_tile(act_f, h), start=True, stop=True).then_inc(G["o_sum"], 1)

        def head_tile(t, h, off=0):
            return t[:, bass.ds(h + off, 1), :].squeeze(1)

        def act_a_squares(act, h, ahead):
            for i, off in ((0, 8), (1, 0)):
                nc.scalar.activation(A["sq"][:, i, :], head_tile(a_qkvT, h, off + ahead), ACT.Square).then_inc(G["l2_sq"], 1)

        def act_a_rsqrt(act, h, ahead):
            if ahead:
                act.wait_ge(G["o_out"], h + 1)
            for i in range(2):
                act.wait_ge(G["l2_sum"], h * 2 + (2 * ahead + i + 1))
                nc.scalar.activation(A["rs"][:, i, :], bk[4 + i][:, :], ACT.Ln, bias=1e-6).then_inc(G["l2_ln"], 1)
            for i in range(2):
                act.wait_ge(G["l2_ln"], h * 2 + (2 * ahead + i + 1))
                nc.scalar.activation(A["rs"][:, i, :], A["rs"][:, i, :], ACT.Exp, scale=-0.5).then_inc(G["l2_rs"], 1)

        def act_a_k_tok(act, h, ahead):
            act.wait_ge(G["turned"], h * 2 + (2 * ahead + 1))
            nc.scalar.activation(A["ktok"], chunks(bk[1]), ACT.Copy).then_inc(G["k_tok"], 1)

        def act_a_head(act, h):
            for k, n in enumerate(("A", "PT", "qd")):
                for d in range(2):
                    act.wait_ge(G["decay_mm"], h * 6 + (2 * k + d + 1))
                    nc.scalar.activation(A[f"{n}{d}"], chunks(bk[(2 * d + 1, 2 * d, 6 + d)[k]]), ACT.Exp).then_inc(G["decay_exp"], 1)
            for l in range(LEVELS - 1):
                for d in range(2):
                    act.wait_ge(G["turned_y"], h * 12 + (2 * l + d + 1))
                    nc.scalar.activation(A[f"X{d}"], chunks(bk[2 * d + 1]), ACT.Copy).then_inc(G["x"], 1)
                if l == 2:
                    act_a_squares(act, h, 1)
                    act_a_rsqrt(act, h, 1)
            for d in range(2):
                act.wait_ge(G["w_mm"], h * 2 + (d + 1))
                nc.scalar.activation(A[f"X{d}"], chunks(bk[2 * d]), ACT.Copy, scale=-1.0).then_inc(G["w"], 1)
            act.wait_ge(G["o_done"], h + 2)
            act.wait_ge(G["qkn"], h * 2 + 4)
            gap(act)
            nc.scalar.activation(head_tile(act_f, h), bk[6][:, :], ACT.Square).then_inc(G["o_sq"], 1)
            act_a_k_tok(act, h, 1)
            act.wait_ge(G["o_sum"], h + 1)
            nc.scalar.activation(A["rs"][:, 0, :], bk[7][:, :], ACT.Ln, bias=RMS_EPS, scale=1.0 / P).then_inc(G["o_ln"], 1)
            act.wait_ge(G["o_ln"], h + 1)
            nc.scalar.activation(A["rs"][:, 0, :], A["rs"][:, 0, :], ACT.Exp, scale=-0.5).then_inc(G["o_rs"], 1)

        def dve_a_norms(dve, h, ahead):
            dve.wait_ge(G["l2_rs"], h * 2 + (2 * ahead + 1))
            nc.vector.tensor_tensor(A["kn"], head_tile(a_qkvT, h, 8 + ahead), A["rs"][:, 0, :], ALU.mult).then_inc(G["qkn"], 1)
            dve.wait_ge(G["l2_rs"], h * 2 + (2 * ahead + 2))
            nc.vector.scalar_tensor_tensor(out=A["qn"], in0=head_tile(a_qkvT, h, ahead), scalar=float(P) ** -0.5,
                                           in1=A["rs"][:, 1, :], op0=ALU.mult, op1=ALU.mult).then_inc(G["qkn"], 1)

        def dve_a_vb(dve, h, ahead):
            dve.wait_ge(G["pad"], 2)
            dve.wait_ge(G["turned"], h * 2 + (2 * ahead + 2))
            for d in range(2):
                nc.vector.tensor_tensor(A[f"vb{d}"], chunks(bk[3]), bc_tok(A["beta17"][:, :, bass.ds(h + (8 * d + ahead), 1)]),
                                        ALU.mult).then_inc(G["vb"], 1)

        def dve_a_head(dve, h):
            dve.wait_ge(G["kk"], h * 2 + 2)
            for d in range(2):
                dve.wait_ge(G["decay_exp"], h * 6 + (d + 1))
                nc.vector.tensor_tensor(A[f"A{d}"], A[f"A{d}"], chunks(bk[4]), ALU.mult).then_inc(G["ed"], 1)
            for d in range(2):
                dve.wait_ge(G["ed"], h * 2 + (d + 1))
                nc.vector.tensor_tensor(A[f"A{d}"], A[f"A{d}"], bc_tok(A["beta"][:, :, bass.ds(h + 8 * d, 1)]),
                                        ALU.mult).then_inc(G["a"], 1)

            def scores():
                for d in range(2):
                    dve.wait_ge(G["pt_mask"], h * 2 + (d + 1))
                    nc.vector.tensor_tensor(A[f"PT{d}"], A[f"PT{d}"], chunks(bk[5]), ALU.mult).then_inc(G["pt"], 1)
                    dve.wait_ge(G["decay_exp"], h * 6 + (4 + d + 1))
                    nc.vector.tensor_tensor(A[f"qd{d}"], A[f"qd{d}"], A["qn"].rearrange("p (c s) -> p c s", c=ST),
                                            ALU.mult).then_inc(G["qd"], 1)
            for l in range(LEVELS):
                for d in range(2):
                    dve.wait_ge(G["p1"], h * 14 + (2 * l + d + 1))
                    mask = bc_mat(A["negpair"][:, LEVELS * d + l, :])
                    if l == 0:
                        nc.vector.tensor_tensor(A[f"Y{d}"], chunks(bk[2 * d]), mask, ALU.mult).then_inc(G["y0"], 1)
                    else:
                        nc.vector.tensor_tensor(later(A[f"GG{d}"], l, d), later(chunks(bk[2 * d]), l, d),
                                                later(mask, l, d), ALU.mult).then_inc(G["t2"], 1)
                for d in range(2):
                    if l == 0:
                        dve.wait_ge(G["y0"], h * 2 + (d + 1))
                        nc.vector.tensor_tensor(A[f"Y{d}"], A[f"Y{d}"], bc_mat(eye[:, :]), ALU.add).then_inc(G["y"], 1)
                    else:
                        dve.wait_ge(G["p2"], h * 12 + (2 * (l - 1) + d + 1))
                        y = later(A[f"Y{d}"], l, d)
                        nc.vector.tensor_tensor(y, y, later(chunks(bk[2 * d + 1]), l, d), ALU.add).then_inc(G["y"], 1)
                if l == 1:
                    scores()
                if l == 4:
                    dve_a_norms(dve, h, 1)
            for cc in range(ST):
                for d in range(2):
                    dve.wait_ge(G["pv"], h * 8 + (2 * cc + d + 1))
                    nc.vector.tensor_copy(A[f"vn{d}"], bk[2 * d][:, 0:P]).then_inc(G["vn"], 1)
                if cc == 3:
                    break
                for d in range(2):
                    dve.wait_ge(G["ps"], h * 6 + (2 * cc + d + 1))
                    if cc == 0:
                        nc.vector.tensor_copy(A[f"S{d}"], bk[2 * d + 1][:, 0:P]).then_inc(G["s"], 1)
                    else:
                        dve.wait_ge(G["s"], h * 6 + (2 * (cc - 1) + d + 1))
                        nc.vector.scalar_tensor_tensor(out=A[f"S{d}"], in0=A[f"S{d}"],
                                                       scalar=A["glast"][:, chunk_of(cc, d), bass.ds(h + 8 * d, 1)],
                                                       in1=bk[2 * d + 1][:, 0:P], op0=ALU.mult, op1=ALU.add
                                                       ).then_inc(G["s"], 1)
            dve_a_vb(dve, h, 1)
            dve.wait_ge(G["o_rs"], h + 1)
            nc.vector.tensor_tensor(head_tile(act_f, h), bk[6][:, :], A["rs"][:, 0, :], ALU.mult).then_inc(G["of1"], 1)
            dve.wait_ge(G["of1"], h + 1)
            nc.vector.scalar_tensor_tensor(out=head_tile(act_f, h), in0=head_tile(act_f, h), scalar=col("a_norm_g"),
                                           in1=head_tile(a_zT, h), op0=ALU.mult, op1=ALU.mult).then_inc(G["o_out"], 1)

        def pool_a_gate_columns(pool, h, ahead):
            for d in range(2):
                nc.gpsimd.tensor_copy(A["gh"][:, :, d:d + 1], A["g17"][:, :, bass.ds(h + (8 * d + ahead), 1)]
                                      ).then_inc(G["g_head"], 1)

        def pool_a_gates(pool, n, m):
            for d in range(2):
                nc.gpsimd.tensor_tensor(A[f"{n}{d}"], bc_mat(A["tri"][:, m[d], :]), bc_tok(A["gh"][:, :, d:d + 1]),
                                        ALU.mult).then_inc(G["gl"], 1)

        def pool_a_first(pool):
            pool.wait_ge(G["g"], 1)
            pool.wait_ge(conv_silu, 24)
            for n in ("g17", "beta17"):
                nc.gpsimd.memset(A[n][:, :, 16:17], 0.0).then_inc(G["pad"], 1)
            nc.gpsimd.tensor_copy(A["vst"], a_qkvT[:, 16, :]).then_inc(G["v_copied"], 1)
            pool_a_gate_columns(pool, 0, 0)
            pool.wait_ge(G["g_head"], 2)
            pool_a_gates(pool, "GL", (0, 1))
            pool_a_gates(pool, "GG", (2, 3))
            pool.wait_ge(G["pad"], 2)

        def pool_a_head(pool, h):
            pool.wait_ge(G["bexp"], 1)
            pool.wait_ge(G["o_done"], h + 1)
            pool.wait_ge(G["k_tok"], h + 1)
            gap(pool)
            for n, s in (("kbe", "bexp"), ("kd", "kdec")):
                for d in range(2):
                    nc.gpsimd.tensor_tensor(A[f"{n}{d}"], A["ktok"], bc_tok(A[s][:, :, bass.ds(h + 8 * d, 1)]),
                                            ALU.mult).then_inc(G["kx"], 1)
            for d in range(2):
                pool.wait_ge(G["decay_exp"], h * 6 + (2 + d + 1))
                nc.gpsimd.tensor_tensor(A[f"PT{d}"], A[f"PT{d}"], bc_mat(A["tri"][:, d, :]), ALU.mult).then_inc(G["pt_mask"], 1)
            pool.wait_ge(G["decay_mm"], h * 6 + 6)
            gap(pool)
            nc.gpsimd.tensor_copy(A["vst"], head_tile(a_tiles, h, 17)).then_inc(G["v_copied"], 1)
            pool_a_gate_columns(pool, h, 1)
            pool.wait_ge(G["g_head"], h * 2 + 4)
            pool_a_gates(pool, "GL", (0, 1))
            pool.wait_ge(G["p2"], h * 12 + 12)
            pool_a_gates(pool, "GG", (2, 3))

        def gap(eng):
            eng.wait_ge(memset_done, 1)

        wmod_loaded = sem("wmod_loaded")
        mod_mm = sem("mod_mm")
        mod_read = sem("mod_read")

        def pe_up(pe, L, e):
            pe.wait_ge(act_ready, 8 * (e + 1))
            with pe.Fori(0, 8) as k2:
                for b in range(2):
                    pe_feature_slab(pe, f"up{L}", k2, b)

        def act_up(act, L):
            with act.Fori(0, 8) as k2:
                for b in range(2):
                    for j in range(2):
                        wait_tile(act, f"up{L}", k2, b, j)
                        gap(act)
                        nc.scalar.activation(head_tile(hid, k2 * 4, 2 * b + j), bk[2 * b + j][:, :], ACT.Relu
                                             ).then_inc(acc_free, 1)
                    split_hi(act, next_pair(f"up{L}", k2), b)

        def dve_up(dve, L):
            with dve.Fori(0, 8) as k2:
                for b in range(2):
                    for j in range(2):
                        dve.wait_ge(acc_free, k2 * 4 + (2 * FS[f"up{L}"] + 2 * b + j + 1))
                        gap(dve)
                        tile = head_tile(hid, k2 * 4, 2 * b + j)
                        nc.vector.tensor_tensor(tile, tile, tile, ALU.mult).then_inc(hid_ready, 1)
                    split_lo(dve, next_pair(f"up{L}", k2), b)

        def pe_down(pe, L):
            pe_token_layer(pe, f"down{L}")

        def load_lnrow(pool, e, g, b):
            for i, v in enumerate((g, b)):
                pool.dma_start(lnrow[:, i, :], v.partition_broadcast(P)).then_inc(lnrow_loaded, 16)

        def load_wmod(pool, third):
            pool.dma_start(wmod, a["w_mod_2"][0, :, third * D:third * D + D].rearrange("(k p) n -> p k n", p=P)
                           ).then_inc(wmod_loaded, 16)

        def pe_mod(pe, third, name):
            pe.wait_ge(sum_added, 4 * TH[name] + 5)
            pe.wait_ge(wmod_loaded, 16 * (third + 1))
            rhs = csil[:, :].rearrange("p (w k) -> p k w", w=2)
            pe.wait_ge(vec_ready, 3)
            for n in range(8):
                for kt in range(KT):
                    mm = nc.tensor.matmul(bk[4][:, 2 * n:2 * n + 2], wmod[:, kt, n * P:n * P + P], rhs[:, kt, :],
                                          start=kt == 0, stop=kt == KT - 1, skip_group_check=True)
            mm.then_inc(mod_mm, 1)

        def dve_mod(dve, third):
            dve.wait_ge(mod_mm, third + 1)
            r = VEC["b_mod"][0] + 8 * third
            nc.vector.tensor_tensor(modc[:, 8 * third:8 * third + 8, :], bk[4][:, 0:16].rearrange("p (n w) -> p n w", w=2),
                                    cols[:, r:r + 8].unsqueeze(2).broadcast_to([P, 8, 2]), ALU.add).then_inc(mod_read, 1)

        b_qT = arena[:, 0:2048].rearrange("p (n s) -> p n s", n=BH)
        b_kT = arena[:, 2048:4096].rearrange("p (n s) -> p n s", n=BH)
        b_v = arena[:, 4096:8192].rearrange("p (c n) -> p c n", c=ST)
        b_rT = arena[:, 8192:12288].rearrange("p (n s) -> p n s", n=2 * BH)
        b_la = arena[:, 12288:16384].rearrange("p (n k) -> p n k", n=2 * ST)
        NL = LEVELS + 2
        BB = carve(work, [("cum", 2 * NL, P), ("masks", 512), ("E0", NL, S), ("E1", NL, S), ("las", ST, P),
                          ("vs", ST, BDV), ("kh", S), ("ST0", ST, P), ("ST1", ST, P), ("kdt0", ST, P), ("kdt1", ST, P),
                          ("S0", BDV), ("S1", BDV), ("rs", S), ("gl", 8)])
        b_masks = BB["masks"].bitcast(U8).rearrange("p (d l s) -> p d l s", d=2, l=LEVELS + 1)
        b_masks_f = BB["E1"].rearrange("p l s -> p (l s)")[:, 0:2 * (LEVELS + 1) * P]
        BG = carve(work, [("glT", S), ("w2", 2, S), ("t", 2, S)], start=2816)
        B = {n: sem("b_" + n) for n in (
            "w_loaded gate_loaded masks_loaded masks_ready gate_set w_hi w_ready gl_mm gl la_mm absd expd ln la kh vs las e_mm exp gl_col zk zq sc st kd_turned "
            "kdt u s o_done o_sq o_sum o_ln o_rs of1 o_out").split()}

        def pool_b_load(pool):
            pool.wait_ge(x_ready, 8)
            pool.wait_ge(slab_used, PH["b_qk"][0])
            nc.gpsimd.memset(BG["glT"][0:33, :], 1.0).then_inc(B["gate_set"], 1)
            nc.gpsimd.memset(BG["w2"][0:33, :, :], 0.0).then_inc(B["gate_set"], 1)
            pool.wait_ge(B["gate_set"], 2)
            pool.dma_start(gw_raw, a["b_w_in"][0, :, 3072:3104].rearrange("(k p) n -> p k n", p=P)).then_inc(B["w_loaded"], 16)
            for n in range(2):
                pool.dma_start(BG["w2"][RANK * n:RANK * n + RANK, n, :], a["b_gate_w2"][0, n]).then_inc(B["gate_loaded"], 16)
            pool.dma_start(BG["w2"][32:33, :, :], a["b_gate_b"]).then_inc(B["gate_loaded"], 16)
            pool.dma_start(BB["cum"], a["k_cum"].rearrange("p (m s) -> p m s", m=2 * NL)).then_inc(B["gate_loaded"], 16)
            pool.dma_start(b_masks_f, a["k_masks"]).then_inc(B["masks_loaded"], 16)

        def pe_b_in(pe):
            pe.wait_ge(act_ready, 24)
            for k2 in range(2):
                for b in range(2):
                    pe_feature_slab(pe, "b_qk", k2, b)
            pe.wait_ge(acc_free, 2 * (FS["b_qk"] + 4))
            pe_token_layer(pe, "b_v")
            pe.wait_ge(sum_added, 4 * TH["b_v"] + 4)
            for k2 in range(2):
                for b in range(2):
                    pe_feature_slab(pe, "b_r", k2, b)
            pe.wait_ge(sum_added, 4 * TH["b_v"] + 8)
            pe.wait_ge(B["w_ready"], 1)
            for kt in range(KT):
                mm = mm3(bk[4][0:32, :], gw_hi[:, kt, :], gw_lo[:, kt, :], act_hi[:, kt, :], act_lo[:, kt, :],
                         kt == 0, kt == KT - 1)
            mm.then_inc(B["gl_mm"], 1)
            pe.wait_ge(B["gl"], 1)
            pe.wait_ge(B["gate_loaded"], 16 * 4)
            for n in range(2):
                for st in range(ST):
                    t = ST * n + st
                    if t >= 2:
                        pe.wait_ge(B["la"], t - 1)
                    nc.tensor.matmul(bk[6 + t % 2][:, :], BG["glT"][0:33, st * P:st * P + P], BG["w2"][0:33, n, :],
                                     start=True, stop=True).then_inc(B["la_mm"], 1)

        def act_b_in(act):
            for k2 in range(2):
                for b in range(2):
                    for j in range(2):
                        wait_tile(act, "b_qk", k2, b, j)
                        dst = (b_qT, b_kT)[k2][:, 2 * b + j, :]
                        nc.scalar.activation(dst, bk[2 * b + j][:, :], ACT.Copy, scale=float(P) ** -0.5 if k2 == 0 else 1.0
                                             ).then_inc(acc_free, 1)
                    split_hi(act, next_pair("b_qk", k2), b)
            for half in range(2):
                for b in range(2):
                    split_hi(act, next_pair("b_v", half), b)
                for st in range(ST):
                    wait_sum(act, "b_v", half, st)
                    nc.scalar.activation(b_v[:, st, half * 512:half * 512 + 512], bk[4 * half + st][:, :], ACT.Copy
                                         ).then_inc(sum_added, 1)
            for k2 in range(2):
                for b in range(2):
                    for j in range(2):
                        wait_tile(act, "b_r", k2, b, j)
                        nc.scalar.activation(b_rT[:, 4 * k2 + 2 * b + j, :], bk[2 * b + j][:, :], ACT.Silu).then_inc(acc_free, 1)
                    split_hi(act, next_pair("b_r", k2), b)
            log_exp_table()
            act.wait_ge(B["gl_mm"], 1)
            act.wait_ge(B["gate_set"], 2)
            nc.scalar.activation(BG["glT"][0:32, :], bk[4][0:32, :], ACT.Copy).then_inc(B["gl"], 1)
            for t in range(2 * ST):
                tb = BG["t"][:, t % 2, :]
                act.wait_ge(B["la_mm"], t + 1)
                if t >= 2:
                    act.wait_ge(B["la"], t - 1)
                nc.scalar.activation(tb, bk[6 + t % 2][:, :], ACT.Abs).then_inc(B["absd"], 1)
                act.wait_ge(B["absd"], t + 1)
                nc.scalar.activation(tb, tb, ACT.Exp, scale=-1.0).then_inc(B["expd"], 1)
                act.wait_ge(B["expd"], t + 1)
                nc.scalar.activation(tb, tb, ACT.Ln, bias=1.0).then_inc(B["ln"], 1)
            act.wait_ge(B["masks_ready"], 1)

        def act_b_gate_weights(act):
            act.wait_ge(B["w_loaded"], 16)
            nc.scalar.activation(gw_hi, gw_raw, ACT.Copy).then_inc(B["w_hi"], 1)

        def dve_b_in(dve):
            dve.wait_ge(B["w_hi"], 1)
            nc.vector.tensor_tensor(gw_lo, gw_raw, gw_hi, ALU.subtract).then_inc(B["w_ready"], 1)
            with dve.Fori(0, 6) as k2:
                for b in range(2):
                    split_lo(dve, next_pair("b_qk", k2), b)
            dve.wait_ge(B["masks_loaded"], 16)
            nc.vector.tensor_copy(BB["masks"].bitcast(U8), b_masks_f).then_inc(B["masks_ready"], 1)
            for t in range(2 * ST):
                dve.wait_ge(B["ln"], t + 1)
                nc.vector.scalar_tensor_tensor(out=b_la[:, t, :], in0=bk[6 + t % 2][:, :], scalar=0.0,
                                               in1=BG["t"][:, t % 2, :], op0=ALU.min, op1=ALU.subtract).then_inc(B["la"], 1)

        def halves(t, l):
            return t.rearrange("p (n t b) -> p n t b", t=2, b=1 << l)

        def pool_b_kh(pool, h):
            nc.gpsimd.tensor_copy(BB["kh"], b_kT[:, bass.ds(h, 1), :].squeeze(1)).then_inc(B["kh"], 1)

        def pool_b_las(pool, h, d):
            nc.gpsimd.tensor_copy(BB["las"], b_la[:, ST * d:ST * d + ST, bass.ds(h * P, P)]).then_inc(B["las"], 1)

        def pool_b_head(pool, h, more):
            for d in range(2):
                if d == 1:
                    pool.wait_ge(B["e_mm"], h * 18 + 10)
                    gap(pool)
                    pool_b_las(pool, h, 1)
                else:
                    pool.wait_ge(B["kh"], h + 1)
                for l in range(LEVELS):
                    pool.wait_ge(B["exp"], h * 18 + (3 + 9 * d + (4 if l < 4 else 8)))
                    e = halves(BB[f"E{d}"][:, l, :], l)[:, :, d, :]
                    nc.gpsimd.tensor_tensor(e, e, halves(BB["kh"], l)[:, :, d, :], ALU.mult).then_inc(B["zk"], 1)
                pool.wait_ge(B["exp"], h * 18 + (3 + 9 * d + 9))
                e = BB[f"E{d}"][:, LEVELS + 1, :]
                nc.gpsimd.tensor_tensor(e, e, BB["kh"], ALU.mult).then_inc(B["zk"], 1)
                if d == 0:
                    pool.wait_ge(B["o_done"], h + 1)
                    gap(pool)
                    nc.gpsimd.tensor_copy(BB["vs"], b_v[:, :, bass.ds(h * BDV, BDV)]).then_inc(B["vs"], 1)
            if more:
                pool.wait_ge(B["sc"], h * 16 + 9)
                pool.wait_ge(B["zk"], h * 16 + 16)
                pool.wait_ge(B["e_mm"], h * 18 + 19)
                gap(pool)
                pool_b_kh(pool, h + 1)
                pool_b_las(pool, h + 1, 0)

        def act_b_head(act, h):
            act.wait_ge(B["o_done"], h + 1)
            for d in range(2):
                E = BB[f"E{d}"]
                for i in range(9):
                    act.wait_ge(B["e_mm"], h * 18 + (9 * d + i + 2))
                    if i < 8:
                        c = i % 4
                        dst = E[:, 4 * (i // 4):4 * (i // 4) + 4, c * P:c * P + P]
                        src = chunks(bk[i % 3])
                    else:
                        dst, src = E[:, LEVELS + 1, :], bk[i % 3][:, :]
                    nc.scalar.activation(dst, src, ACT.Exp, scale=1.0 / 16.0).then_inc(B["exp"], 1)
                act.wait_ge(B["kd_turned"], h * 2 + (d + 1))
                nc.scalar.activation(BB[f"kdt{d}"], chunks(bk[3]), ACT.Copy).then_inc(B["kdt"], 1)
            act.wait_ge(B["o_done"], h + 2)
            for e in range(2):
                gap(act)
                nc.scalar.activation(head_tile(act_f, h * 2, e), bk[6 + e][:, :], ACT.Square).then_inc(B["o_sq"], 1)
            act.wait_ge(B["o_sum"], h + 1)
            nc.scalar.activation(BB["rs"], bk[5][:, :], ACT.Ln, bias=RMS_EPS, scale=1.0 / BDV).then_inc(B["o_ln"], 1)
            act.wait_ge(B["o_ln"], h + 1)
            nc.scalar.activation(BB["rs"], BB["rs"], ACT.Exp, scale=-0.5).then_inc(B["o_rs"], 1)

        def pe_b_head(pe, h):
            for d in range(2):
                E = BB[f"E{d}"]
                pe.wait_ge(B["las"], h * 2 + (d + 1))
                for i in range(9):
                    pe.wait_ge(B["exp"], h * 18 + (9 * d + i + 1))
                    if i < 8:
                        m0 = NL * d + 4 * (i // 4)
                        mm = nc.tensor.matmul(chunks(bk[i % 3]), BB["las"][:, i % 4, :], BB["cum"][:, m0:m0 + 4, :],
                                              start=True, stop=True)
                    else:
                        for c in range(ST):
                            mm = nc.tensor.matmul(bk[i % 3][:, c * P:c * P + P], BB["las"][:, c, :],
                                                  BB["cum"][:, NL * d + NL - 1, :], start=True, stop=True, skip_group_check=True)
                    mm.then_inc(B["e_mm"], 1)
                if d == 0:
                    pe.wait_ge(B["kh"], h + 1)
                for i in range(8):
                    pe.wait_ge(B["st"], h * 16 + (8 * d + i + 1))
                    if i > 0:
                        pe.wait_ge(B["zk"], h * 16 + (8 * d + i))
                        pe.wait_ge(B["zq"], h * 16 + (8 * d + i))
                    for c in range(ST):
                        cs = slice(c * P, c * P + P)
                        if i == 0:
                            l_, r_ = BB["kh"][:, cs], b_qT[:, bass.ds(h, 1), cs].squeeze(1)
                        else:
                            l_ = r_ = E[:, i - 1, cs]
                        mm = nc.tensor.matmul(bk[4 + i % 2][:, cs], l_, r_, start=True, stop=True, skip_group_check=True)
                    mm.then_inc(B["sc"], 1)
                pe.wait_ge(B["zk"], h * 16 + (8 * d + 8))
                if d == 0:
                    pe.wait_ge(B["o_out"], h * 2 + 2)
                else:
                    pe.wait_ge(B["kdt"], h * 2 + 1)
                for c in range(ST):
                    mm = nc.tensor.transpose(bk[3][:, c * P:c * P + P], E[:, LEVELS + 1, c * P:c * P + P], eye[:, :])
                mm.then_inc(B["kd_turned"], 1)
            pe.wait_ge(B["kdt"], h * 2 + 2)
            pe.wait_ge(B["vs"], h + 1)
            pe.wait_ge(B["st"], 2 + 16 * h + 16)
            pe.wait_ge(B["zq"], h * 16 + 16)
            for cc in range(ST):
                for d in range(2):
                    c = chunk_of(cc, d)
                    cs = slice(c * P, c * P + P)
                    if cc > 0:
                        pe.wait_ge(B["s"], h * 6 + (2 * (cc - 1) + d + 1))
                    for e in range(2):
                        es = slice(e * P, e * P + P)
                        if cc > 0:
                            nc.tensor.matmul(bk[6 + e][:, cs], BB[f"S{d}"][:, es], BB[f"E{d}"][:, LEVELS, cs], start=False,
                                             stop=False, skip_group_check=True)
                        mm = nc.tensor.matmul(bk[6 + e][:, cs], BB["vs"][:, c, es], BB[f"ST{d}"][:, c, :],
                                              start=cc == 0 and d == 0, stop=cc == 3, skip_group_check=True)
                    if cc < 3:
                        nc.tensor.matmul(bk[3 * (1 - d)][:, 0:BDV], BB[f"kdt{d}"][:, c, :], BB["vs"][:, c, :], start=True,
                                         stop=True, skip_group_check=True).then_inc(B["u"], 1)
            mm.then_inc(B["o_done"], 1)
            for e in range(2):
                pe.wait_ge(B["o_sq"], h * 2 + (e + 1))
                mm = nc.tensor.matmul(bk[5][:, :], ones[:, :], head_tile(act_f, h * 2, e), start=e == 0, stop=e == 1)
            mm.then_inc(B["o_sum"], 1)

        def dve_b_head(dve, h):
            for d in range(2):
                E = BB[f"E{d}"]
                for l in range(LEVELS):
                    dve.wait_ge(B["exp"], 3 + 18 * h + (9 * d + (4 if l < 4 else 8)))
                    e = halves(E[:, l, :], l)[:, :, 1 - d, :]
                    nc.vector.tensor_tensor(e, e, halves(head_tile(b_qT, h), l)[:, :, 1 - d, :], ALU.mult).then_inc(B["zq"], 1)
                nc.vector.tensor_copy(BB["gl"][:, 4 * d:4 * d + 4],
                                      E[:, LEVELS, (P - 1 if d == 0 else 0)::P]).then_inc(B["gl_col"], 1)
                dve.wait_ge(B["gl_col"], h * 2 + (d + 1))
                nc.vector.tensor_tensor(E[:, LEVELS, :], E[:, LEVELS, :], head_tile(b_qT, h), ALU.mult).then_inc(B["zq"], 1)
                for i in range(8):
                    dve.wait_ge(B["sc"], h * 16 + (8 * d + i + 1))
                    src = chunks(bk[4 + i % 2])
                    if i == 0:
                        nc.vector.tensor_tensor(BB[f"ST{d}"], src, bc_mat(eye[:, :]), ALU.mult).then_inc(B["st"], 1)
                    else:
                        dve.wait_ge(B["st"], 2 + 16 * h + (8 * d + i))
                        nc.vector.memset(pause[:, i:i + 1], 0.0)
                        nc.vector.copy_predicated(BB[f"ST{d}"], bc_mat(b_masks[:, d, i - 1, :]), src).then_inc(B["st"], 1)
            for cc in range(ST - 1):
                for d in range(2):
                    dve.wait_ge(B["u"], h * 6 + (2 * cc + d + 1))
                    s, u = BB[f"S{d}"], bk[3 * (1 - d)][:, 0:BDV]
                    if cc == 0:
                        nc.vector.tensor_copy(s, u).then_inc(B["s"], 1)
                    else:
                        c = chunk_of(cc, d)
                        dve.wait_ge(B["s"], h * 6 + (2 * (cc - 1) + d + 1))
                        nc.vector.scalar_tensor_tensor(out=s, in0=s, scalar=BB["gl"][:, 4 * d + c:4 * d + c + 1], in1=u,
                                                       op0=ALU.mult, op1=ALU.add).then_inc(B["s"], 1)
            dve.wait_ge(B["o_rs"], h + 1)
            for e in range(2):
                nc.vector.tensor_tensor(head_tile(act_f, h * 2, e), bk[6 + e][:, :], BB["rs"], ALU.mult).then_inc(B["of1"], 1)
            for e in range(2):
                dve.wait_ge(B["of1"], h * 2 + (e + 1))
                nc.vector.scalar_tensor_tensor(out=head_tile(act_f, h * 2, e), in0=head_tile(act_f, h * 2, e),
                                               scalar=col("b_norm_g", e), in1=head_tile(b_rT, h * 2, e), op0=ALU.mult,
                                               op1=ALU.mult).then_inc(B["o_out"], 1)

        N = S + CTX
        c_ga = arena[:, 0:2048].rearrange("p (n s) -> p n s", n=4)
        c_gp = arena[:, 2048:4096].rearrange("p (n s) -> p n s", n=4)
        c_pin = arena[:, 4096:6208].rearrange("p (n s) -> p n s", n=4)
        c_cq = arena[:, 6208:7232].rearrange("p (n s) -> p n s", n=2)
        c_ckv = arena[:, 7232:8000]
        c_kr = arena[0:64, 8000:8768]
        c_v = arena[:, 8768:11840].rearrange("p (c n) -> p c n", c=6)
        c_tmp = arena[:, 13888:14912].rearrange("p (i s) -> p i s", i=2)
        c_PT = arena[:, 11840:14912].rearrange("p (k s) -> p k s", k=6)
        c_invc = work[:, 0:2048].rearrange("p (g s) -> p g s", g=4)
        c_gate = work[:, 2048:3072]
        c_gbias = work[:, 3072:4096]
        c_xn = arena[:, 6208:10304].rearrange("p (c n) -> p c n", c=ST)
        c_ctx = work[:, 9216:11264].rearrange("p (c n) -> p c n", c=CT)
        CW = carve(work, [("uq", 2, 4 * QK_DIM), ("ukv", D), ("pool", 4, P), ("cos", N), ("sin", N), ("rot", P),
                          ], start=4096)
        c_csb = work[:, 8192:9216].rearrange("p (k n) -> p k n", k=KT)
        CL = carve(work, [("sqq", 2, S), ("sqk", N), ("rsq", S), ("rsk", N)], start=10272)
        CH = carve(work, [("pa", S + 16), ("pb", S + 16), ("qn", S), ("qr", S), ("kn", N), ("kr", N), ("p", 2, N),
                          ("vh", 6, P), ("sqn", S), ("sqr", S), ("m", 2, 4), ("acc", 2, 4), ("r", 4)], start=9216)
        CT_ = carve(arena, [("rsq", S), ("rsk", N), ("rt", N)], start=11840)
        CWH = carve(arena, [("uq", 2, QK_DIM), ("uk", P)], start=15680)
        c_fin = arena[:, 0:4096].rearrange("p (c n) -> p c n", c=ST)

        class Steps:
            def __init__(self, name, what, credit=0):
                self.sem, self.what, self.n, self.credit = sem(name), what, 0, credit

            def at(self, what, i=0, h=None):
                v = [k for k, w in enumerate(self.what) if w == what][i] + 1 + self.credit
                return v if h is None else h * len(self.what) + v

            def inc(self, instruction, what):
                assert self.what[self.n % len(self.what)] == what, (self.n, what)
                self.n += 1
                instruction.then_inc(self.sem, 1)

        def lst(*parts):
            return [n for names, k in parts for n in names.split() * k]

        V = Steps("c_vector", lst(("ga1 ga", 1), ("stats stats mean ms", 6), ("lo", 16), ("gate", 1), ("lat", 3)))
        K = Steps("c_scalar", lst(("csb", 1), ("ln rs xn", 6), ("tmp hi", 16), ("ckv kr", 1), ("sq", 3),
                                  ("ln2 rs2", 3), ("v", 6)))
        T = Steps("c_tensor", lst(("gate", 1), ("turned", 16), ("ctx ctx", 1), ("sum", 3), ("v", 6)))
        Q = Steps("c_pool", lst(("pads", 1), *[(" ".join(["add"] * (g + 1)) + " mul pooled", 1) for g in range(4)]))
        HV = Steps("h_vector", lst(("q q", 1), ("k k k", 1), ("rt", 1), ("cos", 1), ("q_roped", 1), ("rt rt", 1), ("cos", 1), ("k_roped", 1),
                                   ("max max nmax sum rsum p pt", 4), ("o", 1)), 1)
        HK = Steps("h_scalar", lst(("sqq sqq sqk sqk sqk", 1), ("ln ln ln", 1), ("rs rs rs", 1), ("e e pt", 4)))
        HT = Steps("h_tensor", lst(("sum_q sum_k sum_k", 1), ("rot rot rot", 1), ("score score", 2),
                                   ("turned turned score score", 2), ("turned turned", 2), ("o", 1)), 1)
        h_weights = sem("h_weights")
        h_v = sem("h_v")
        h_project = sem("h_project")
        c_const = sem("c_const")
        ctx_loaded = sem("ctx_loaded")
        inv_loaded = sem("inv_loaded")
        br_mm = sem("br_mm")
        br_f = sem("br_f")
        fin1 = sem("fin1")
        fin = sem("fin")
        stored = sem("stored")
        x_src = [(c_ctx, 0), (c_ctx, 1)] + [(X, t) for t in range(ST)]
        xn_dst = [(c_ctx, 0), (c_ctx, 1)] + [(c_xn, t) for t in range(ST)]

        def pool_c_load(pool):
            pool.dma_start(c_ctx, a["ctx_2"][0].rearrange("(c p) n -> p c n", p=P)).then_inc(ctx_loaded, 16)
            pool.wait_ge(T.sem, T.at("gate"))
            uq, ukv = a["w_uq_2"][0], a["w_ukv_2"][0]
            for dst, src in ((CW["uq"], uq.rearrange("(k p) n -> p k n", p=P)), (CW["ukv"], ukv),
                             (CW["pool"], a["w_pool_2"][0].rearrange("g c d -> c g d")), (CW["cos"][0:64, :], a["k_cos"]),
                             (CW["sin"][0:64, :], a["k_sin"]), (CW["rot"][0:64, :], a["k_rot"])):
                pool.dma_start(dst, src).then_inc(c_const, 16)
            pool.dma_start(c_invc, a["k_invcount"].rearrange("g s -> (g s)").partition_broadcast(P)).then_inc(inv_loaded, 16)
            pool.dma_start(c_gbias, a["b_mod_2"][0, 2 * D:3 * D].partition_broadcast(P)).then_inc(inv_loaded, 16)
            Q.inc(nc.gpsimd.memset(arena[:, 4096:6208], 0.0), "pads")

        def pe_c_gate(pe):
            pe.wait_ge(wmod_loaded, 48)
            pe.wait_ge(K.sem, K.at("csb"))
            pe.wait_ge(sum_added, 4 * TH["down1"] + 8)
            for half in range(2):
                for kt in range(KT):
                    mm = nc.tensor.matmul(bk[6 + half][:, :], c_csb[:, kt, :], wmod[:, kt, half * 512:half * 512 + 512],
                                          start=kt == 0, stop=kt == KT - 1)
            T.inc(mm, "gate")

        def act_c_csb(act):
            K.inc(nc.scalar.activation(c_csb, csil[:, 0:KT].unsqueeze(2).broadcast_to([P, KT, P]), ACT.Copy), "csb")

        def stat_slot(t):
            return (t + ST) % (ST + CT)

        def dve_c_stats(dve, tiles):
            for t in tiles:
                src, n = x_src[t]
                k = stat_slot(t)
                for hf in range(2):
                    V.inc(nc.vector.bn_stats(stats[:, k, hf, :], src[:, n, hf * 512:hf * 512 + 512]), "stats")
                dve.wait_ge(V.sem, V.at("stats", 2 * t + 1))
                V.inc(nc.vector.bn_aggr(mv[:, k, :], stats[:, k, :, :]), "mean")
                dve.wait_ge(V.sem, V.at("mean", t))
                V.inc(nc.vector.scalar_tensor_tensor(out=mv[:, k, 0:1], in0=mv[:, k, 0:1], scalar=mv[:, k, 0:1],
                                                     in1=mv[:, k, 1:2], op0=ALU.mult, op1=ALU.add), "ms")

        def act_c_xn(act, tiles):
            for t in tiles:
                (src, n), (dst, m), k = x_src[t], xn_dst[t], stat_slot(t)
                act.wait_ge(V.sem, V.at("ms", t))
                K.inc(nc.scalar.activation(rstd[:, k, 0:1], mv[:, k, 0:1], ACT.Ln, bias=RMS_EPS), "ln")
                act.wait_ge(K.sem, K.at("ln", t))
                K.inc(nc.scalar.activation(rstd[:, k, 1:2], rstd[:, k, 0:1], ACT.Exp, scale=-0.5), "rs")
                act.wait_ge(K.sem, K.at("rs", t))
                K.inc(nc.scalar.activation(dst[:, m, :], src[:, n, :], ACT.Copy, scale=rstd[:, k, 1:2]), "xn")

        def dve_c_ctx(dve):
            r = VEC["norm_g"][0]
            dve.wait_ge(mod_read, 2)
            V.inc(nc.vector.tensor_scalar(modg[:, :, :], modc[:, 8:16, :], 1.0, None, ALU.add), "ga1")
            dve.wait_ge(V.sem, V.at("ga1"))
            V.inc(nc.vector.tensor_tensor(modg[:, :, :], modg[:, :, :], cols[:, r:r + 8].unsqueeze(2).broadcast_to([P, KT, 2]),
                                          ALU.mult), "ga")
            dve.wait_ge(ctx_loaded, 16)
            dve_c_stats(dve, (0, 1))

        def dve_c_norm(dve):
            dve.wait_ge(x_ready, 16)
            dve_c_stats(dve, (2, 3, 4, 5))
            for i in range(16):
                tmp, src, hi, lo = c_turned(i)
                dve.wait_ge(K.sem, K.at("hi", i))
                V.inc(nc.vector.tensor_tensor(lo, tmp, hi, ALU.subtract), "lo")
            dve.wait_ge(T.sem, T.at("gate"))
            dve.wait_ge(inv_loaded, 32)
            for half in range(2):
                hs = slice(half * 512, half * 512 + 512)
                i = nc.vector.tensor_tensor(c_gate[:, hs], bk[6 + half][:, :], c_gbias[:, hs], ALU.add)
            V.inc(i, "gate")

        def c_turned(i):
            kt = i % 8
            if i < 8:
                return (c_tmp[:, i % 2, 0:CTX], bk[4 + kt % 2][:, 0:CTX], ctx_hi[:, kt, :], ctx_lo[:, kt, :])
            return c_tmp[:, i % 2, :], bk[kt % 4][:, :], act_hi[:, kt, :], act_lo[:, kt, :]

        def act_c_norm(act):
            act_c_xn(act, (2, 3, 4, 5))
            act.wait_ge(V.sem, V.at("ga"))
            for i in range(16):
                tmp, src, hi, _ = c_turned(i)
                kt, w = i % 8, 1 if i < 8 else 0
                act.wait_ge(T.sem, T.at("turned", i))
                if i >= 2:
                    act.wait_ge(V.sem, V.at("lo", i - 2))
                for dst, what in ((tmp, "tmp"), (hi, "hi")):
                    K.inc(nc.scalar.activation(dst, src, ACT.Identity, scale=modg[:, kt, w:w + 1], bias=modc[:, kt, w:w + 1]), what)

        def pe_c_turn(pe):
            for i in range(16):
                kt = i % 8
                if i == 0:
                    pe.wait_ge(K.sem, K.at("xn", 1))
                    pe.wait_ge(sum_added, 4 * TH["down1"] + 8)
                if i == 8:
                    pe.wait_ge(K.sem, K.at("xn", 5))
                if 2 <= i < 8:
                    pe.wait_ge(K.sem, K.at("hi", i - 2))
                if i >= 12:
                    pe.wait_ge(K.sem, K.at("hi", i - 4))
                for t in range(CT if i < 8 else ST):
                    src, n = xn_dst[t if i < 8 else t + 2]
                    mm = nc.tensor.transpose(c_turned(i)[1][:, t * P:t * P + P], src[:, n, kt * P:kt * P + P], eye[:, :])
                T.inc(mm, "turned")

        def sp_c_in(sp):
            w = a["w_in_2"][0].rearrange("(k p) n -> p k n", p=P)
            k0 = PH["c_in"][0] // 2
            load_slab(sp, k0, 0, w[:, :, 0:256])
            load_slab(sp, k0, 1, w[:, :, 256:448])
            with sp.Fori(1, 4) as k2:
                for b in range(2):
                    load_slab(sp, k2 + k0, b, slab_source("c_in", k2, b))

        def pe_c_in(pe):
            pe.wait_ge(V.sem, V.at("lo", 15))
            pe_feature_slab(pe, "c_in", 0, 0)
            pe.wait_ge(w_ready, 2 * (PH["c_in"][0] + 2))
            hi, lo = slab_view(whi[1], KT), slab_view(wlo[1], KT)
            for j, m in enumerate((P, 64)):
                for kt in range(KT):
                    c = slice(j * P, j * P + m)
                    mm = mm3(bk[4 + j][0:m, 0:CTX], hi[:, kt, c], lo[:, kt, c], ctx_hi[:, kt, :], ctx_lo[:, kt, :],
                             kt == 0, kt == KT - 1)
                T.inc(mm, "ctx")
            pe_feature_slab(pe, "c_in", 0, 1, 192)
            for k2 in range(1, 4):
                for b in range(2):
                    pe_feature_slab(pe, "c_in", k2, b)

        def act_c_in(act):
            for j in range(2):
                wait_tile(act, "c_in", 0, 0, j)
                i = nc.scalar.activation(c_cq[:, j, :], bk[j][:, :], ACT.Copy)
                i.then_inc(acc_free, 1)
            split_hi(act, next_pair("c_in", 0), 0)
            act.wait_ge(T.sem, T.at("ctx", 1))
            K.inc(nc.scalar.activation(c_ckv[:, 0:CTX], bk[4][:, 0:CTX], ACT.Copy), "ckv")
            K.inc(nc.scalar.activation(c_kr[:, 0:CTX], bk[5][0:64, 0:CTX], ACT.Copy), "kr")
            for j, (dst, m) in enumerate(((c_ckv, P), (c_kr, 64))):
                wait_tile(act, "c_in", 0, 1, j)
                nc.scalar.activation(dst[:, CTX:N], bk[2 + j][0:m, :], ACT.Copy).then_inc(acc_free, 1)
            split_hi(act, next_pair("c_in", 0), 1)
            act.wait_ge(Q.sem, Q.at("pads"))
            for k2 in range(1, 4):
                for b in range(2):
                    for j in range(2):
                        n = 2 * b + j
                        wait_tile(act, "c_in", k2, b, j)
                        dst = (c_ga[:, n, :], c_pin[:, n, 8:8 + S], c_gp[:, n, :])[k2 - 1]
                        nc.scalar.activation(dst, bk[n][:, :], ACT.Copy if k2 == 2 else ACT.Silu).then_inc(acc_free, 1)
                    split_hi(act, next_pair("c_in", k2), b)
            log_exp_table()
            act.wait_ge(acc_free, 2 * FS["c_in"] + 4)
            for dst, src in ((CL["sqq"][:, 0, :], c_cq[:, 0, :]), (CL["sqq"][:, 1, :], c_cq[:, 1, :]), (CL["sqk"], c_ckv)):
                K.inc(nc.scalar.activation(dst, src, ACT.Square), "sq")
            for i, (dst, bank, n, width) in enumerate(((CL["rsq"], 0, S, 256), (CL["rsk"][:, 0:S], 1, S, P),
                                                       (CL["rsk"][:, S:N], 2, CTX, P))):
                act.wait_ge(T.sem, T.at("sum", i))
                K.inc(nc.scalar.activation(dst, bk[bank][:, 0:n], ACT.Ln, bias=RMS_EPS, scale=1.0 / width), "ln2")
                act.wait_ge(K.sem, K.at("ln2", i))
                K.inc(nc.scalar.activation(dst, dst, ACT.Exp, scale=-0.5), "rs2")
            for t in range(6):
                act.wait_ge(T.sem, T.at("v", t))
                K.inc(nc.scalar.activation(c_v[:, t, :], bk[4 + t % 2][:, :], ACT.Copy), "v")

        def dve_c_in(dve):
            with dve.Fori(0, 4) as k2:
                for b in range(2):
                    split_lo(dve, next_pair("c_in", k2), b)
            dve.wait_ge(acc_free, 2 * FS["c_in"] + 4)
            for i, (x, rs, g) in enumerate(((c_cq[:, 0, :], CL["rsq"], col("q_lora_g", 0)), (c_cq[:, 1, :], CL["rsq"], col("q_lora_g", 1)),
                                            (c_ckv, CL["rsk"], col("kv_lora_g")))):
                dve.wait_ge(K.sem, K.at("rs2", 0 if i < 2 else 2))
                V.inc(nc.vector.scalar_tensor_tensor(out=x, in0=x, scalar=g, in1=rs, op0=ALU.mult, op1=ALU.mult), "lat")

        def pe_c_latent(pe):
            pe.wait_ge(K.sem, K.at("sq", 1))
            pe.wait_ge(acc_free, 2 * FS["c_in"] + 16)
            for i in range(2):
                mm = nc.tensor.matmul(bk[0][:, :], ones[:, :], CL["sqq"][:, i, :], start=i == 0, stop=i == 1)
            T.inc(mm, "sum")
            pe.wait_ge(K.sem, K.at("sq", 2))
            T.inc(nc.tensor.matmul(bk[1][:, :], ones[:, :], CL["sqk"][:, 0:S], start=True, stop=True), "sum")
            T.inc(nc.tensor.matmul(bk[2][:, 0:CTX], ones[:, :], CL["sqk"][:, S:N], start=True, stop=True), "sum")
            pe.wait_ge(V.sem, V.at("lat", 2))
            wv = CW["ukv"].rearrange("p (h t n) -> p h t n", h=4, t=2)[:, :, 1, :]
            pe.wait_ge(c_const, 16 * 6)
            for t in range(6):
                if t >= 2:
                    pe.wait_ge(K.sem, K.at("v", t - 2))
                T.inc(nc.tensor.matmul(bk[4 + t % 2][:, :].rearrange("p (h n) -> p h n", h=4), c_ckv[:, t * P:t * P + P], wv,
                                       start=True, stop=True), "v")

        def pool_c_pooling(pool):
            pool.wait_ge(acc_free, 2 * FS["c_in"] + 12)
            pool.wait_ge(inv_loaded, 32)
            pool.wait_ge(V.sem, V.at("lo", 15))
            n_add = 0
            for g in range(4):
                src, width = c_pin[:, g, :], S + 16
                for j in range(g + 1):
                    dst = CH["pa"] if j % 2 == 0 else CH["pb"]
                    width -= 1 << j
                    if n_add:
                        pool.wait_ge(Q.sem, Q.at("add", n_add - 1) if j else Q.at("pooled", g - 1))
                    Q.inc(nc.gpsimd.tensor_tensor(dst[:, 0:width], src[:, 0:width], src[:, (1 << j):(1 << j) + width], ALU.add), "add")
                    n_add += 1
                    src = dst
                w = POOL_W[g]
                other = CH["pb"] if g % 2 == 0 else CH["pa"]
                pool.wait_ge(Q.sem, Q.at("add", n_add - 1))
                Q.inc(nc.gpsimd.tensor_tensor(other[:, 0:S], src[:, 8 - w // 2:8 - w // 2 + S], c_invc[:, g, :], ALU.mult), "mul")
                pool.wait_ge(Q.sem, Q.at("mul", g))
                x = c_pin[:, g, 8:8 + S]
                Q.inc(nc.gpsimd.tensor_tensor(x, other[:, 0:S], x, ALU.subtract), "pooled")

        SCALE = float(QK_DIM) ** -0.5
        def pool_c_weights(pool, h):
            nc.gpsimd.tensor_copy(CWH["uq"], CW["uq"][:, :, bass.ds(h * QK_DIM, QK_DIM)]).then_inc(h_weights, 1)
            nc.gpsimd.tensor_copy(CWH["uk"], CW["ukv"][:, bass.ds(h * 2 * P, P)]).then_inc(h_weights, 1)

        def pool_c_head(pool, h, more):
            pool.wait_ge(HT.sem, h * len(HT.what) + 1)
            gap(pool)
            nc.gpsimd.tensor_copy(CH["vh"], c_v[:, :, bass.ds(h * P, P)]).then_inc(h_v, 1)
            if more:
                pool.wait_ge(h_project, h * 4 + 4)
                gap(pool)
                pool_c_weights(pool, h + 1)

        def pe_c_project(pe, h):
            pe.wait_ge(h_weights, h * 2 + 2)
            for j, m in enumerate((P, 64)):
                for kt in range(2):
                    mm = nc.tensor.matmul(bk[j][0:m, :], CWH["uq"][:, kt, j * P:j * P + m], c_cq[:, kt, :], start=kt == 0, stop=kt == 1)
                mm.then_inc(h_project, 1)
            nc.tensor.matmul(bk[2][:, :], CWH["uk"], c_ckv[:, 0:S], start=True, stop=True).then_inc(h_project, 1)
            nc.tensor.matmul(bk[3][:, 0:CTX], CWH["uk"], c_ckv[:, S:N], start=True, stop=True).then_inc(h_project, 1)

        def pe_c_head(pe, h, more):
            pe.wait_ge(HK.sem, HK.at("sqq", 1, h))
            nc.tensor.matmul(bk[4][:, :], ones[:, :], CH["sqn"], start=True, stop=False)
            HT.inc(nc.tensor.matmul(bk[4][:, :], ones[0:64, :], CH["sqr"][0:64, :], start=False, stop=True), "sum_q")
            pe.wait_ge(HK.sem, HK.at("sqk", 2, h))
            for bank, ts in ((5, slice(0, S)), (6, slice(S, N))):
                n = ts.stop - ts.start
                nc.tensor.matmul(bk[bank][:, 0:n], ones[:, :], CH["p"][:, 0, ts], start=True, stop=False)
                HT.inc(nc.tensor.matmul(bk[bank][:, 0:n], ones[0:64, :], CH["p"][0:64, 1, ts], start=False, stop=True), "sum_k")
            pe.wait_ge(HV.sem, HV.at("q", 1, h))
            HT.inc(nc.tensor.matmul(bk[1][:, :], CW["rot"][0:64, :], CH["qr"][0:64, :], start=True, stop=True), "rot")
            pe.wait_ge(HV.sem, HV.at("k", 2, h))
            HT.inc(nc.tensor.matmul(bk[2][:, :], CW["rot"][0:64, :], CH["kr"][0:64, 0:S], start=True, stop=True), "rot")
            HT.inc(nc.tensor.matmul(bk[3][:, 0:CTX], CW["rot"][0:64, :], CH["kr"][0:64, S:N], start=True, stop=True), "rot")
            pe.wait_ge(HV.sem, HV.at("k_roped", 0, h))

            def scores(qt):
                if qt >= 2:
                    pe.wait_ge(HK.sem, HK.at("e", 2 * (qt - 2) + 1, h))
                qs = slice(qt * P, qt * P + P)
                for half, (ts, n) in enumerate(((slice(0, S), S), (slice(S, N), CTX))):
                    dst = bk[2 * (qt % 2) + half][:, 0:n]
                    nc.tensor.matmul(dst, CH["qn"][:, qs], CH["kn"][:, ts], start=True, stop=False)
                    HT.inc(nc.tensor.matmul(dst, CH["qr"][0:64, qs], CH["kr"][0:64, ts], start=False, stop=True), "score")

            def turn(qt):
                pe.wait_ge(HV.sem, HV.at("p", qt, h))
                if qt > 0:
                    pe.wait_ge(HK.sem, HK.at("pt", qt - 1, h))
                    pe.wait_ge(HV.sem, HV.at("pt", qt - 1, h))
                for k in range(6):
                    mm = nc.tensor.transpose(bk[4 + k // 4][:, (k % 4) * P:(k % 4) * P + P], CH["p"][:, qt % 2, k * P:k * P + P], eye[:, :])
                    if k in (3, 5):
                        HT.inc(mm, "turned")

            scores(0)
            for qt in range(ST):
                if qt + 1 < ST:
                    scores(qt + 1)
                turn(qt)
            if more:
                pe_c_project(pe, h + 1)
            pe.wait_ge(h_v, h + 1)
            pe.wait_ge(HV.sem, h * len(HV.what) + 1)
            pe.wait_ge(HK.sem, HK.at("pt", 3, h))
            pe.wait_ge(HV.sem, HV.at("pt", 3, h))
            for k in range(6):
                mm = nc.tensor.matmul(bk[7][:, :], CH["vh"][:, k, :], c_PT[:, k, :], start=k == 0, stop=k == 5)
            HT.inc(mm, "o")

        def act_c_head(act, h):
            act.wait_ge(h_project, h * 4 + 1)
            HK.inc(nc.scalar.activation(CH["sqn"], bk[0][:, :], ACT.Square), "sqq")
            act.wait_ge(h_project, h * 4 + 2)
            HK.inc(nc.scalar.activation(CH["sqr"][0:64, :], bk[1][0:64, :], ACT.Square), "sqq")
            act.wait_ge(h_project, h * 4 + 3)
            HK.inc(nc.scalar.activation(CH["p"][:, 0, 0:S], bk[2][:, :], ACT.Square), "sqk")
            act.wait_ge(h_project, h * 4 + 4)
            HK.inc(nc.scalar.activation(CH["p"][:, 0, S:N], bk[3][:, 0:CTX], ACT.Square), "sqk")
            HK.inc(nc.scalar.activation(CH["p"][0:64, 1, :], c_kr, ACT.Square), "sqk")
            jobs = ((CT_["rsq"], 4, S), (CT_["rsk"][:, 0:S], 5, S), (CT_["rsk"][:, S:N], 6, CTX))
            for i, (dst, bank, n) in enumerate(jobs):
                act.wait_ge(HT.sem, HT.at("sum_q", 0, h) if i == 0 else HT.at("sum_k", i - 1, h))
                HK.inc(nc.scalar.activation(dst, bk[bank][:, 0:n], ACT.Ln, bias=RMS_EPS, scale=1.0 / QK_DIM), "ln")
            for i, (dst, bank, n) in enumerate(jobs):
                act.wait_ge(HK.sem, HK.at("ln", i, h))
                HK.inc(nc.scalar.activation(dst, dst, ACT.Exp, scale=-0.5), "rs")

            for qt in range(ST):
                act.wait_ge(HV.sem, HV.at("nmax", qt, h))
                if qt >= 2:
                    act.wait_ge(HT.sem, HT.at("turned", 2 * (qt - 2) + 1, h))
                for half, (ts, n) in enumerate(((slice(0, S), S), (slice(S, N), CTX))):
                    HK.inc(nc.scalar.activation(CH["p"][:, qt % 2, ts], bk[2 * (qt % 2) + half][:, 0:n], ACT.Exp, scale=SCALE,
                                                bias=CH["m"][:, 0, qt:qt + 1], accum_out=CH["acc"][:, half, qt:qt + 1]), "e")
                act.wait_ge(HT.sem, HT.at("turned", 2 * qt, h))
                HK.inc(nc.scalar.activation(c_PT[:, 0:4, qt * P:qt * P + P], chunks(bk[4]), ACT.Copy), "pt")

        def dve_c_head(dve, h):
            stt = lambda out, x, g, rs: nc.vector.scalar_tensor_tensor(out=out, in0=x, scalar=g, in1=rs, op0=ALU.mult, op1=ALU.mult)
            qg, kg = [col("q_norm_g", 0), col("q_norm_g", 1)[0:64, :]], [col("k_norm_g", 0), col("k_norm_g", 1)[0:64, :]]
            dve.wait_ge(HK.sem, HK.at("rs", 0, h))
            HV.inc(stt(CH["qn"], bk[0][:, :], qg[0], CT_["rsq"]), "q")
            HV.inc(stt(CH["qr"][0:64, :], bk[1][0:64, :], qg[1], CT_["rsq"][0:64, :]), "q")
            dve.wait_ge(HK.sem, HK.at("rs", 2, h))
            HV.inc(stt(CH["kn"][:, 0:S], bk[2][:, :], kg[0], CT_["rsk"][:, 0:S]), "k")
            HV.inc(stt(CH["kn"][:, S:N], bk[3][:, 0:CTX], kg[0], CT_["rsk"][:, S:N]), "k")
            HV.inc(stt(CH["kr"][0:64, :], c_kr, kg[1], CT_["rsk"][0:64, :]), "k")
            rt = CT_["rt"][0:64, :]
            for i, (x, off, parts) in enumerate(((CH["qr"][0:64, :], CTX, ((1, 0, S),)),
                                                 (CH["kr"][0:64, :], 0, ((2, 0, S), (3, S, N))))):
                cos, sin = CW["cos"][0:64, off:N], CW["sin"][0:64, off:N]
                width = N - off
                if i == 1:
                    dve.wait_ge(HV.sem, HV.at("q_roped", 0, h))
                for j, (bank, t0, t1) in enumerate(parts):
                    dve.wait_ge(HT.sem, HT.at("rot", i + j, h))
                    HV.inc(nc.vector.tensor_tensor(rt[:, t0:t1], bk[bank][0:64, 0:t1 - t0], sin[:, t0:t1], ALU.mult), "rt")
                HV.inc(nc.vector.tensor_tensor(x, x, cos, ALU.mult), "cos")
                dve.wait_ge(HV.sem, HV.at("cos", i, h))
                HV.inc(nc.vector.tensor_tensor(x, x, rt[:, 0:width], ALU.add), ("q_roped", "k_roped")[i])
            for qt in range(ST):
                for half, n in enumerate((S, CTX)):
                    dve.wait_ge(HT.sem, HT.at("score", 2 * qt + half, h))
                    HV.inc(nc.vector.reduce_max(CH["m"][:, half, qt:qt + 1], bk[2 * (qt % 2) + half][:, 0:n], AX_X), "max")
                dve.wait_ge(HV.sem, HV.at("max", 2 * qt + 1, h))
                HV.inc(nc.vector.tensor_scalar(CH["m"][:, 0, qt:qt + 1], CH["m"][:, 0, qt:qt + 1], CH["m"][:, 1, qt:qt + 1],
                                               -SCALE, ALU.max, ALU.mult), "nmax")
                dve.wait_ge(HK.sem, HK.at("e", 2 * qt + 1, h))
                HV.inc(nc.vector.tensor_tensor(CH["r"][:, qt:qt + 1], CH["acc"][:, 0, qt:qt + 1], CH["acc"][:, 1, qt:qt + 1],
                                               ALU.add), "sum")
                dve.wait_ge(HV.sem, HV.at("sum", qt, h))
                HV.inc(nc.vector.reciprocal(CH["r"][:, qt:qt + 1], CH["r"][:, qt:qt + 1]), "rsum")
                dve.wait_ge(HV.sem, HV.at("rsum", qt, h))
                HV.inc(nc.vector.tensor_scalar(CH["p"][:, qt % 2, :], CH["p"][:, qt % 2, :], CH["r"][:, qt:qt + 1], None,
                                               ALU.mult), "p")
                dve.wait_ge(HT.sem, HT.at("turned", 2 * qt + 1, h))
                HV.inc(nc.vector.tensor_copy(c_PT[:, 4:6, qt * P:qt * P + P],
                                             bk[5][:, 0:CTX].rearrange("p (k s) -> p k s", k=2)), "pt")
            dve.wait_ge(HT.sem, HT.at("o", 0, h))
            at_token = lambda v: v.rearrange("p (i b) -> p b i", b=ST)
            HV.inc(nc.vector.tensor_tensor(at_token(head_tile(act_f, h)), bk[7][:, :].rearrange("p (b i) -> p b i", b=ST),
                                           at_token(head_tile(c_ga, h)), ALU.mult), "o")

        def pe_c_pool(pe):
            pe.wait_ge(Q.sem, Q.at("pooled", 3))
            pe.wait_ge(HV.sem, 4 * len(HV.what) + 1)
            for g in range(4):
                nc.tensor.matmul(bk[g][:, :], CW["pool"][:, g, :], c_pin[:, g, 8:8 + S], start=True, stop=True).then_inc(br_mm, 1)

        def dve_c_pool(dve):
            for g in range(4):
                dve.wait_ge(br_mm, g + 1)
                nc.vector.scalar_tensor_tensor(out=act_f[:, 4 + g, :], in0=bk[g][:, :], scalar=col("pool_scale", g), in1=c_gp[:, g, :],
                                               op0=ALU.mult, op1=ALU.mult).then_inc(br_f, 1)

        def dve_c_out(dve):
            for b in range(2):
                split_lo(dve, next_pair("c_out", 0), b)
            n = 0
            for half in range(2):
                for st in range(ST):
                    hs = slice(half * 512, half * 512 + 512)
                    wait_sum(dve, "c_out", half, st)
                    nc.vector.tensor_tensor(c_fin[:, st, hs], bk[4 * half + st][:, :], c_gate[:, hs], ALU.mult).then_inc(fin1, 1)
                    n += 1
                    dve.wait_ge(fin1, n)
                    nc.vector.tensor_tensor(X[:, st, hs], X[:, st, hs], c_fin[:, st, hs], ALU.add).then_inc(fin, 1)

        def act_c_out(act):
            for b in range(2):
                split_hi(act, next_pair("c_out", 0), b)

        def sp_store(sp):
            for st in range(ST):
                sp.wait_ge(fin, 4 + st + 1)
                sp.dma_start(out[0, st * P:st * P + P, :], X[:, st, :]).then_inc(stored, 16)
            sp.wait_ge(stored, 16 * ST)

        block = ctx.enter_context(nc.Block())

        @block.sync
        def _(sp):
            sp_start(sp)
            sp_feature(sp, "a_in", 1)
            sp_token(sp, "a_out")
            sp_feature(sp, "up0")
            sp_token(sp, "down0")
            sp_feature(sp, "b_qk")
            sp_token(sp, "b_v")
            sp_feature(sp, "b_r")
            sp_token(sp, "b_out")
            sp_feature(sp, "up1")
            sp_token(sp, "down1")
            sp_c_in(sp)
            sp_token(sp, "c_out")
            sp_store(sp)

        @block.gpsimd
        def _(pool):
            pool_start(pool)
            pool_a_first(pool)
            with pool.Fori(0, AH) as h:
                pool_a_head(pool, h)
            pool.wait_ge(G["o_out"], AH + 1)
            pool.wait_ge(G["gl"], 4 * (AH + 1))
            load_lnrow(pool, 1, a["ln1_g"][0], a["ln1_b"][0])
            load_wmod(pool, 0)
            pool.wait_ge(x_ready, 4)
            load_lnrow(pool, 2, a["ln2_g"][0], a["ln2_b"][0])
            pool_b_load(pool)
            pool.wait_ge(B["la"], 2 * ST)
            pool_b_kh(pool, 0)
            pool_b_las(pool, 0, 0)
            with pool.Fori(0, BH - 1) as h:
                pool_b_head(pool, h, True)
            pool_b_head(pool, BH - 1, False)
            pool.wait_ge(B["o_out"], 2 * BH + 2)
            load_lnrow(pool, 3, a["ln1_g"][1], a["ln1_b"][1])
            load_wmod(pool, 1)
            pool.wait_ge(x_ready, 12)
            load_lnrow(pool, 4, a["ln2_g"][1], a["ln2_b"][1])
            pool.wait_ge(mod_mm, 2)
            load_wmod(pool, 2)
            pool_c_load(pool)
            pool_c_pooling(pool)
            pool.wait_ge(c_const, 16 * 6)
            pool_c_weights(pool, 0)
            pool.wait_ge(K.sem, K.at("v", 5))
            with pool.Fori(0, 3) as h:
                pool_c_head(pool, h, True)
            pool_c_head(pool, 3, False)

        @block.scalar
        def _(act):
            act_start(act)
            act_begin(act)
            act_a_gates(act)
            act_a_in(act)
            log_exp_table()
            act_a_decays(act)
            act_a_k_tok(act, 0, 0)
            with act.Fori(0, AH) as h:
                act_a_head(act, h)
            act.wait_ge(G["gl"], 4 * (AH + 1))
            act_mixed(act, G["o_out"], AH + 1, "a_out")
            act_token_layer(act, "a_out", 1)
            act_up(act, 0)
            act_token_layer(act, "down0", 2)
            act_b_gate_weights(act)
            act_b_in(act)
            with act.Fori(0, BH) as h:
                act_b_head(act, h)
            act_mixed(act, B["o_out"], 2 * BH + 2, "b_out")
            act_token_layer(act, "b_out", 3)
            act_c_csb(act)
            act_c_xn(act, (0, 1))
            act_up(act, 1)
            act_token_layer(act, "down1", 4)
            act_c_norm(act)
            act_c_in(act)
            with act.Fori(0, 4) as h:
                act_c_head(act, h)
            act_mixed(act, br_f, 4, "c_out")
            act_c_out(act)

        @block.vector
        def _(dve):
            dve_start(dve)
            dve_a_gates(dve)
            dve_a_in(dve)
            dve_a_decays(dve)
            dve_a_vb(dve, 0, 0)
            with dve.Fori(0, AH) as h:
                dve_a_head(dve, h)
            dve_mixed(dve, "a_out")
            dve_token_layer(dve, "a_out", 1)
            dve_mod(dve, 0)
            dve_up(dve, 0)
            dve_token_layer(dve, "down0", 2)
            dve_b_in(dve)
            with dve.Fori(0, BH) as h:
                dve_b_head(dve, h)
            dve_mixed(dve, "b_out")
            dve_token_layer(dve, "b_out", 3)
            dve_mod(dve, 1)
            dve_c_ctx(dve)
            dve_up(dve, 1)
            dve_token_layer(dve, "down1", 4)
            dve_c_norm(dve)
            dve_c_in(dve)
            with dve.Fori(0, 4) as h:
                dve_c_head(dve, h)
            dve_c_pool(dve)
            dve_mixed(dve, "c_out")
            dve_c_out(dve)

        @block.tensor
        def _(pe):
            pe_start(pe)
            pe_a_in(pe)
            with pe.Fori(0, AH) as h:
                pe_a_head(pe, h)
            pe.wait_ge(G["o_out"], AH + 1)
            pe_token_layer(pe, "a_out")
            pe_mod(pe, 0, "a_out")
            pe_turn(pe, 1, 4 * (TH["a_out"] + 1))
            pe_up(pe, 0, 1)
            pe_down(pe, 0)
            pe_turn(pe, 2, 4 * (TH["down0"] + 1))
            pe_b_in(pe)
            with pe.Fori(0, BH) as h:
                pe_b_head(pe, h)
            pe.wait_ge(B["o_out"], 2 * BH + 2)
            pe_token_layer(pe, "b_out")
            pe_mod(pe, 1, "b_out")
            pe_turn(pe, 3, 4 * (TH["b_out"] + 1))
            pe_up(pe, 1, 3)
            pe_down(pe, 1)
            pe_c_gate(pe)
            pe_c_turn(pe)
            pe_c_in(pe)
            pe_c_latent(pe)
            pe_c_project(pe, 0)
            with pe.Fori(0, 3) as h:
                pe_c_head(pe, h, True)
            pe_c_head(pe, 3, False)
            pe_c_pool(pe)
            pe_token_layer(pe, "c_out")


_INS = ["x", "a_w_in", "a_conv", "a_alog", "a_dt_bias", "a_norm_g", "a_w_out", "b_w_in", "b_gate_w2", "b_gate_b",
        "b_norm_g", "b_w_out", "ln1_g", "ln1_b", "mlp_w1", "mlp_w2", "ln2_g", "ln2_b", "c_2", "ctx_2", "c_ctx_2",
        "w_mod_2", "b_mod_2", "norm_g_2", "w_in_2", "q_lora_g_2", "w_uq_2", "kv_lora_g_2", "w_ukv_2", "q_norm_g_2",
        "k_norm_g_2", "w_pool_2", "pool_scale_2", "w_out_2"]


def kernel(**inputs):
    import concourse.bacc as bacc
    from concourse.bass_utils import run_bass_kernel_spmd

    nc = bacc.Bacc("TRN2", target_bir_lowering=False, num_devices=1)
    arrays, aps = {}, {}
    given = {n: inputs[n] for n in _INS}
    given.update(shape_constants())
    for name, v in given.items():
        v = np.ascontiguousarray(v)
        arrays[f"in_{name}"] = v
        aps[name] = nc.dram_tensor(f"in_{name}", v.shape, mybir.dt.from_np(v.dtype), kind="ExternalInput").ap()
    out = nc.dram_tensor("out", (1, S, D), F32, kind="ExternalOutput").ap()
    build(nc, aps, out)
    r = run_bass_kernel_spmd(nc, [arrays], core_ids=[0])
    return r.results[0]["out"]
```
